# Optimizing a Trainium2 kernel written in Bass

```python
import jax, jax.numpy as jnp
from jax import lax
import numpy as np

D_MODEL = 2048
BATCH = 1
SEQ = 256
DEPTH = 1
DEC_BATCH = 8
DEC_SEQ = 1
PAST_LEN = 2048
PAGE_SIZE = 128

N_MEM = 256
CHUNK = 128
GMLP_GROUPS = 6
GMLP_GROUP_DIM = 128
GMLP_WIDTH = GMLP_GROUPS * GMLP_GROUP_DIM
POOL_WINDOWS = (2, 4, 8, 16)
POOL_GROUPS = len(POOL_WINDOWS)
POOL_GROUP_DIM = 192
POOL_WIDTH = POOL_GROUPS * POOL_GROUP_DIM
POOL_STATE = max(POOL_WINDOWS) - 1
XA_HEADS = 4
XA_HEAD_DIM = 128
XA_WIDTH = XA_HEADS * XA_HEAD_DIM
N_BRANCHES = 3
IN_WIDTH = 2 * GMLP_WIDTH + POOL_WIDTH + XA_WIDTH + N_BRANCHES * D_MODEL
SPLITS = (GMLP_WIDTH, 2 * GMLP_WIDTH, 2 * GMLP_WIDTH + POOL_WIDTH,
          2 * GMLP_WIDTH + POOL_WIDTH + XA_WIDTH)
N_EXPERT_GROUPS = 4
EXPERTS_PER_GROUP = 8
N_EXPERTS = N_EXPERT_GROUPS * EXPERTS_PER_GROUP
TOP_K = 2
D_EXPERT = 512
EPS = 1e-6

kernel_name = "hybrid_gmlp_pool_memxattn_hmoe_step"

def rmsnorm(x, g):
    xf = x.astype(jnp.float32)
    y = xf * lax.rsqrt(jnp.mean(xf * xf, axis=-1, keepdims=True) + EPS)
    return (y * g.astype(jnp.float32)).astype(x.dtype)

def layernorm(x, g, b):
    xf = x.astype(jnp.float32)
    mu = jnp.mean(xf, axis=-1, keepdims=True)
    xc = xf - mu
    var = jnp.mean(xc * xc, axis=-1, keepdims=True)
    return (xc * lax.rsqrt(var + EPS) * g.astype(jnp.float32) + b.astype(jnp.float32)).astype(x.dtype)

def chunk_spatial_gate(u, v, w_s, b_s):
    bsz, L, _ = v.shape
    n_chunks = -(-L // CHUNK)
    pad = n_chunks * CHUNK - L
    vp = jnp.pad(v, ((0, 0), (0, pad), (0, 0))).reshape(bsz, n_chunks, CHUNK, GMLP_GROUPS, GMLP_GROUP_DIM)
    mask = jnp.tril(jnp.ones((CHUNK, CHUNK), dtype=bool))
    w = jnp.where(mask, w_s, 0).astype(v.dtype)
    mixed = jnp.einsum('gij,bcjgh->bcigh', w, vp) + b_s.T.astype(v.dtype)[None, None, :, :, None]
    mixed = mixed.reshape(bsz, n_chunks * CHUNK, GMLP_WIDTH)[:, :L]
    return u * mixed

def multi_scale_pool(p_ext, n_prefix, w_pool, pool_scale):
    T = p_ext.shape[1]
    pf = p_ext.astype(jnp.float32)
    cs = jnp.concatenate([jnp.zeros_like(pf[:, :1]), jnp.cumsum(pf, axis=1)], axis=1)
    t = jnp.arange(T)
    outs = []
    for g, w in enumerate(POOL_WINDOWS):
        lo_c, hi_c = g * POOL_GROUP_DIM, (g + 1) * POOL_GROUP_DIM
        hi = cs[:, 1:, lo_c:hi_c]
        lo = jnp.pad(cs[:, :T + 1 - w, lo_c:hi_c], ((0, 0), (w - 1, 0), (0, 0)))
        cnt = jnp.minimum(t + 1, w).astype(jnp.float32)[None, :, None]
        diff = ((hi - lo) / cnt - pf[:, :, lo_c:hi_c])[:, n_prefix:].astype(p_ext.dtype)
        outs.append(jnp.einsum('blc,cd->bld', diff, w_pool[g]))
    return jnp.concatenate(outs, axis=-1) * pool_scale

def memory_kv(mem, g_mem, w_mkv):
    bsz, m, _ = mem.shape
    kv = rmsnorm(mem, g_mem) @ w_mkv
    k, v = jnp.split(kv, 2, axis=-1)
    return (k.reshape(bsz, m, XA_HEADS, XA_HEAD_DIM), v.reshape(bsz, m, XA_HEADS, XA_HEAD_DIM))

def memory_attention(q, k, v):
    bsz, L = q.shape[0], q.shape[1]
    s = jnp.einsum('blhd,bmhd->bhlm', q * (XA_HEAD_DIM ** -0.5), k.astype(q.dtype)).astype(jnp.float32)
    p = jax.nn.softmax(s, axis=-1).astype(q.dtype)
    o = jnp.einsum('bhlm,bmhd->blhd', p, v.astype(q.dtype))
    return o.reshape(bsz, L, XA_WIDTH)

def mixer_block(x, mem_k, mem_v, pool_prefix, g_mix, w_in, ln_v_g, ln_v_b, w_s, b_s,
                w_pool, pool_scale, w_br_a, w_br_b, w_br_c, w_o):
    bsz, L, _ = x.shape
    xn = rmsnorm(x, g_mix)
    z = xn @ w_in
    u_pre, v_pre, p_in, q, gate_pre = jnp.split(z, SPLITS, axis=-1)
    u = jax.nn.gelu(u_pre, approximate=False)
    v = layernorm(jax.nn.gelu(v_pre, approximate=False), ln_v_g, ln_v_b)
    br_a = chunk_spatial_gate(u, v, w_s, b_s)
    if pool_prefix is None:
        n_prefix, p_ext = 0, p_in
    else:
        n_prefix = pool_prefix.shape[1]
        p_ext = jnp.concatenate([pool_prefix.astype(p_in.dtype), p_in], axis=1)
    br_b = multi_scale_pool(p_ext, n_prefix, w_pool, pool_scale)
    br_c = memory_attention(q.reshape(bsz, L, XA_HEADS, XA_HEAD_DIM), mem_k, mem_v)
    gates = jax.nn.sigmoid(gate_pre.astype(jnp.float32)).astype(x.dtype).reshape(bsz, L, N_BRANCHES, D_MODEL)
    merged = (gates[:, :, 0] * (br_a @ w_br_a) + gates[:, :, 1] * (br_b @ w_br_b)
              + gates[:, :, 2] * (br_c @ w_br_c))
    return x + merged @ w_o, v, p_ext[:, -POOL_STATE:]

def hierarchical_moe(x, g_ffn, w_rg, b_rg, w_re, b_re, w_gate, w_up, w_down):
    bsz, L, _ = x.shape
    xn = rmsnorm(x, g_ffn).reshape(bsz * L, D_MODEL)
    g_logits = (xn @ w_rg).astype(jnp.float32) + b_rg.astype(jnp.float32)
    g_probs = jax.nn.softmax(g_logits, axis=-1)
    grp = jnp.argmax(g_logits, axis=-1)
    p_grp = jnp.take_along_axis(g_probs, grp[:, None], axis=-1)
    e_logits = jnp.einsum('nd,gde->nge', xn, w_re).astype(jnp.float32) + b_re.astype(jnp.float32)
    e_sel = jnp.take_along_axis(e_logits, grp[:, None, None], axis=1)[:, 0]
    top_v, top_i = lax.top_k(e_sel, TOP_K)
    top_w = jax.nn.softmax(top_v, axis=-1) * p_grp
    flat_idx = grp[:, None] * EXPERTS_PER_GROUP + top_i
    combine = jnp.sum(jax.nn.one_hot(flat_idx, N_EXPERTS, dtype=jnp.float32) * top_w[..., None], axis=1)
    combine = combine.reshape(-1, N_EXPERT_GROUPS, EXPERTS_PER_GROUP).astype(x.dtype)
    out = jnp.zeros_like(xn)
    for g in range(N_EXPERT_GROUPS):
        h = jax.nn.silu(jnp.einsum('nd,edf->nef', xn, w_gate[g])) * jnp.einsum('nd,edf->nef', xn, w_up[g])
        out = out + jnp.einsum('nef,efd->nd', h * combine[:, g, :, None], w_down[g])
    return x + out.reshape(bsz, L, D_MODEL)

def setup_inputs(seed: int = 0) -> dict:
    key = jax.random.key(seed)
    ks = iter(jax.random.split(key, 48))
    f32 = jnp.float32

    def nrm(shape, scale):
        return jax.random.normal(next(ks), shape, f32) * scale

    def gain(shape):
        return 1.0 + 0.05 * jax.random.normal(next(ks), shape, f32)

    G, E = N_EXPERT_GROUPS, EXPERTS_PER_GROUP
    return {
        "x_prompt": nrm((BATCH, SEQ, D_MODEL), 1.0),
        "x_sample": nrm((DEC_BATCH, DEC_SEQ, D_MODEL), 1.0),
        "mem_prompt": nrm((BATCH, N_MEM, D_MODEL), 1.0),
        "cache_mem_k": nrm((DEPTH, DEC_BATCH, N_MEM, XA_HEADS, XA_HEAD_DIM), 1.0),
        "cache_mem_v": nrm((DEPTH, DEC_BATCH, N_MEM, XA_HEADS, XA_HEAD_DIM), 1.0),
        "state_pool": nrm((DEPTH, DEC_BATCH, POOL_STATE, POOL_WIDTH), 1.0),
        "g_mix": gain((DEPTH, D_MODEL)),
        "w_in": nrm((DEPTH, D_MODEL, IN_WIDTH), D_MODEL ** -0.5),
        "ln_v_g": gain((DEPTH, GMLP_WIDTH)),
        "ln_v_b": nrm((DEPTH, GMLP_WIDTH), 0.02),
        "w_s": nrm((DEPTH, GMLP_GROUPS, CHUNK, CHUNK), CHUNK ** -0.5),
        "b_s": gain((DEPTH, GMLP_GROUPS, CHUNK)),
        "w_pool": nrm((DEPTH, POOL_GROUPS, POOL_GROUP_DIM, POOL_GROUP_DIM), POOL_GROUP_DIM ** -0.5),
        "pool_scale": gain((DEPTH, POOL_WIDTH)),
        "g_mem": gain((DEPTH, D_MODEL)),
        "w_mkv": nrm((DEPTH, D_MODEL, 2 * XA_WIDTH), D_MODEL ** -0.5),
        "w_br_a": nrm((DEPTH, GMLP_WIDTH, D_MODEL), GMLP_WIDTH ** -0.5),
        "w_br_b": nrm((DEPTH, POOL_WIDTH, D_MODEL), POOL_WIDTH ** -0.5),
        "w_br_c": nrm((DEPTH, XA_WIDTH, D_MODEL), XA_WIDTH ** -0.5),
        "w_o": nrm((DEPTH, D_MODEL, D_MODEL), D_MODEL ** -0.5),
        "g_ffn": gain((DEPTH, D_MODEL)),
        "w_rg": nrm((DEPTH, D_MODEL, G), D_MODEL ** -0.5),
        "b_rg": nrm((DEPTH, G), 0.01),
        "w_re": nrm((DEPTH, G, D_MODEL, E), D_MODEL ** -0.5),
        "b_re": nrm((DEPTH, G, E), 0.01),
        "w_gate": nrm((DEPTH, G, E, D_MODEL, D_EXPERT), D_MODEL ** -0.5),
        "w_up": nrm((DEPTH, G, E, D_MODEL, D_EXPERT), D_MODEL ** -0.5),
        "w_down": nrm((DEPTH, G, E, D_EXPERT, D_MODEL), D_EXPERT ** -0.5),
        "g_final": gain((D_MODEL,)),
    }

def reference(x_prompt, x_sample, mem_prompt, cache_mem_k, cache_mem_v, state_pool,
              g_mix, w_in, ln_v_g, ln_v_b, w_s, b_s, w_pool, pool_scale, g_mem, w_mkv,
              w_br_a, w_br_b, w_br_c, w_o, g_ffn, w_rg, b_rg, w_re, b_re,
              w_gate, w_up, w_down, g_final):
    h_p, h_s = x_prompt, x_sample
    mk_p, mv_p, ps_p, ps_s, gv_s = [], [], [], [], []
    for l in range(DEPTH):
        mix_w = (g_mix[l], w_in[l], ln_v_g[l], ln_v_b[l], w_s[l], b_s[l], w_pool[l], pool_scale[l],
                 w_br_a[l], w_br_b[l], w_br_c[l], w_o[l])
        ffn_w = (g_ffn[l], w_rg[l], b_rg[l], w_re[l], b_re[l], w_gate[l], w_up[l], w_down[l])
        k_p, v_p = memory_kv(mem_prompt, g_mem[l], w_mkv[l])
        h_p, _, pool_p = mixer_block(h_p, k_p, v_p, None, *mix_w)
        h_p = hierarchical_moe(h_p, *ffn_w)
        h_s, v_s, pool_s = mixer_block(h_s, cache_mem_k[l], cache_mem_v[l], state_pool[l], *mix_w)
        h_s = hierarchical_moe(h_s, *ffn_w)
        mk_p.append(k_p)
        mv_p.append(v_p)
        ps_p.append(pool_p)
        ps_s.append(pool_s)
        gv_s.append(v_s)
    y_prompt = rmsnorm(h_p, g_final)
    y_sample = rmsnorm(h_s, g_final)
    return (y_prompt, y_sample, jnp.stack(mk_p), jnp.stack(mv_p), jnp.stack(ps_p),
            jnp.stack(ps_s), jnp.stack(gv_s))


_drawn_inputs = setup_inputs


def setup_inputs(seed=0):
    import zlib

    import numpy as np

    out = dict(_drawn_inputs(seed))
    spreads = {}
    factors = {'ln_v_b': 2.935, 'b_re': 8.39}
    for name, (base, spread) in spreads.items():
        noise = np.random.default_rng([zlib.crc32(name.encode()), seed]).standard_normal(out[name].shape)
        drawn = base * np.exp(spread * noise) if base else spread * noise
        out[name] = __import__('jax').numpy.asarray(drawn.astype(out[name].dtype))
    for name, factor in factors.items():
        out[name] = (out[name] * factor).astype(out[name].dtype)
    return out
```

```python
import concourse.bass as bass
from concourse import mybir
from contextlib import ExitStack

F32 = mybir.dt.float32
I32 = mybir.dt.int32
ALU = mybir.AluOpType
ACT = mybir.ActivationFunctionType
AX = mybir.AxisListType

P = 128
D = 2048
KT = D // P
TP, TS = 256, 8
T = TP + TS
TILES = ((0, P), (P, P), (TP, TS))
NM = 256
NH, DH = 4, 128
GG = 6
BW = GG * P
PG = 192
WINDOWS = (2, 4, 8, 16)
NST = 15
PAD = 16
NG, NE = 4, 8
NX = NG * NE
DE = 512
EPS = 1e-6
SCALE = float(DH) ** -0.5
CAP = 32
EPR = 4
ROUNDS = NX // EPR
CHUNK = 4096
CC = CHUNK // KT
FAR = 10000.0

N_MKV, N_Z, N_GRP = 4, 11, 8
GATE0 = N_MKV + N_Z
OUT0 = GATE0 + 4 * N_GRP
N_DENSE = OUT0 + 8
Z_COLS = (768, 1024, 1280, 2304, 2560, 1536, 1792, 2048, 0, 256, 512)
GATE_COL = 2816
Z_V, Z_Q, Z_P, Z_U, Z_G = 8, 14, 18, 24, 30
Z_O = Z_G + 6 * N_GRP
Z_END = Z_O + 16
ESLOTS = 6
EORDER = (4, 5, 3, 0, 1, 2)
CPR = 24
CREDIT = ESLOTS

_n = 0


def _span(count):
    global _n
    _n += count
    return _n - count


A_MEM = _span(8)
A_X = _span(9)
A_KT = _span(4)
A_WS = _span(2)
A_VN = _span(6)
A_ST = _span(2)
A_QN = _span(1)
A_SC01 = _span(2)
A_HEAD = []
A_SC = [A_SC01, A_SC01 + 1]
for _h in range(NH):
    A_HEAD.append(_span(2))
    if _h + 2 < NH:
        A_SC.append(_span(1))
A_QB = _span(TS)
A_SS = _span(1)
A_PN = _span(2)
A_SP = _span(1)
A_SV = _span(1)
A_MX = _span(5)
A_PL = _span(6)
A_O = _span(16)
A_RT = _span(9)
A_LG = _span(1)
A_POS = _span(1)
A_E = _n
JPR = 18


def branch_kernel(nc, io, outs):
    (x_prompt, x_sample, mem_prompt, cache_k, cache_v, state_pool, g_mix, w_in, ln_v_g, ln_v_b,
     w_s, b_s, w_pool, pool_scale, g_mem, w_mkv, w_br_a, w_br_b, w_br_c, w_o, g_ffn, w_rg, b_rg,
     w_re, b_re, w_gate, w_up, w_down, g_final) = io
    (y_prompt, y_sample, new_k, new_v, new_st_p, new_st_s, new_gv) = outs

    ctx = ExitStack()
    with ctx:
        def sb(name, n, dt=F32):
            return ctx.enter_context(nc.sbuf_tensor(name, [P, n], dt))

        def sem(name):
            return ctx.enter_context(nc.semaphore(name))

        ring = sb("ring", 4 * CHUNK)
        x_all = sb("x_all", 3 * D)
        trunk = sb("trunk", 3 * KT * T)
        side = sb("side", 17456)
        ident = sb("ident", P)
        small = sb("small", 240)
        npass_i = sb("npass_i", 1, I32)
        bank = [ctx.enter_context(nc.psum_tensor(f"bank{i}", [P, 512], F32)) for i in range(8)]

        def view(t, at, *dims):
            n = 1
            for d in dims:
                n *= d
            v = t[:, at:at + n]
            if len(dims) == 1:
                return v
            names = "abc"[:len(dims)]
            pat = f"p ({' '.join(names)}) -> p {' '.join(names)}"
            return v.rearrange(pat, **dict(zip(names, dims)))

        x = view(x_all, 0, 3, D)
        xnT = view(trunk, 0, KT, T)
        brT = view(trunk, KT * T, KT, T)
        mgT = view(trunk, 2 * KT * T, KT, T)
        memT = view(trunk, KT * T, KT, NM)
        mem = view(trunk, 2 * KT * T, 2, D)
        stA = view(trunk, 2 * KT * T, 6, 272)
        stB = view(trunk, 2 * KT * T + 1632, 6, 272)
        stN = view(trunk, 2 * KT * T, 768)
        sT = view(trunk, 2 * KT * T + 3264, 2, 32)
        Ps = view(trunk, 2 * KT * T + 3328, 256)
        PsT = view(trunk, 2 * KT * T + 3584, 2, 32)
        qn = view(trunk, 2 * KT * T + 3648, 512)
        at = 0
        xs = view(side, 0, 2, D)
        vN = view(side, 0, 3, BW)
        vT = view(side, 3 * BW, GG, T)
        diff = view(side, 3 * BW, GG, T)
        sg = side[:, 0:2 * 3 * T].rearrange(
            "p (b i t) -> p b i t", b=2, i=3)
        gp = view(side, 2 * 3 * T, 4, T)
        oT = view(side, 2 * 3 * T + 4 * T, 2, T)
        at = 4096
        kvK = view(side, at, 2, 512)
        kvV = view(side, at + 1024, 2, 512)
        Pp = [[view(side, at + b * 512 + t * NM, NM) for t in range(2)] for b in range(2)]
        at += 2048
        kT = view(side, at, NH, NM)
        at += NH * NM
        qT = view(side, at, NH, T)
        at += NH * T
        pT = view(side, at, GG, PAD + T)
        at += GG * (PAD + T)
        wp = view(side, at, GG, PG)
        at += GG * PG
        wsT = view(side, at, GG, P)
        at += GG * P
        bs = view(side, at, GG, P)
        at += GG * P
        lng, lnb = view(side, at, BW), view(side, at + BW, BW)
        cache_flat = [view(side, at + 1024 * b, 1024) for b in range(2)]
        cache = [view(side, at + 1024 * b, 2, 512) for b in range(2)]
        at += 2048
        prod = view(side, at, 2, 512)
        prod_flat = view(side, at, 1024)
        wsN = view(side, at, GG, P)
        mixt = view(side, at, 4, P)
        at += 1024
        PpT_flat = [view(side, at + b * 512, 512) for b in range(2)]
        PpT = [[view(side, at + b * 512 + m * NM, NM) for m in range(2)] for b in range(2)]
        pn = view(side, at, BW)
        at += 1024
        ext = side[:, at:at + 768].rearrange("p (k b t) -> p k b t", k=GG, b=TS)
        at += 768
        assert at <= 17456, at
        e_slot = {0: view(ring, 0, CHUNK), 1: view(ring, CHUNK, CHUNK), 2: view(ring, 2 * CHUNK, CHUNK),
                  3: view(ring, 3 * CHUNK, CHUNK), 4: view(side, 4096, CHUNK), 5: view(side, 8192, CHUNK)}
        y = view(side, 0, 4, 512)
        hs = view(side, 2048, 512)
        h = view(side, 2560, 4, P)
        hT = view(side, 3072, 4, P)
        PwT = view(side, 3584, T)
        at = 12288
        gfin = view(side, at, D)
        at += D
        P01 = side[:, at:at + 384].rearrange("p (t e c) -> p t e c", t=3, e=EPR)
        P01f = view(side, at, 3, P)
        at += 384
        Pw = side[:, at:at + 384].rearrange("p (t e c) -> p t e c", t=3, e=EPR)
        Pwf = view(side, at, 3, P)
        at += 384
        wre = side[:, at:at + 512].rearrange("p (g j e) -> p g j e", g=NG, j=KT)
        wrg = view(side, at + 512, KT, NG)
        tri = view(side, at, P)
        ones = view(side, at + P, P)
        at += 576
        wr = view(side, at, KT, 36)
        at += 576
        lg = view(side, at, 3, 36)
        at += 108
        lgb = view(side, at, 36)
        at += 36
        combx = view(side, at, 3, NX + EPR)
        comb = combx[:, :, 0:NX].rearrange("p t (g e) -> p t g e", g=NG)
        at += 108
        sel = side[:, at:at + 96].rearrange("p (t g e) -> p t g e", t=3, g=NG)
        self_ = view(side, at, 3, NX)
        at += 96
        pos = view(side, at, 3, NX + EPR)
        at += 108
        t32 = side[:, at:at + 96].rearrange("p (t g e) -> p t g e", t=3, g=NG)
        at += 96
        r4 = [view(side, at + 12 * i, 3, NG) for i in range(3)]
        at += 36
        r8 = [view(side, at + 24 * i, 3, NE) for i in range(5)]
        at += 120
        r1 = [view(side, at + 3 * i, 3) for i in range(12)]
        at += 36
        cidx = view(side, at, CAP)
        at += CAP
        rev = view(side, at, NE)
        at += NE
        thr = view(side, at, 9)
        at += 9
        thr2 = view(side, at, 9)
        at += 9
        npf = view(side, at, 2)
        at += 2
        assert at <= 17456, at
        xn2 = trunk[:, 0:3 * D].rearrange("p (t j c) -> p t j c", t=3, j=KT)
        xn2T = view(trunk, 3 * D, KT, T)
        xgT = view(trunk, 3 * D, KT, P)

        gmixc, gmemc, gffnc = view(small, 0, KT), view(small, 16, KT), view(small, 32, KT)
        pscale = view(small, 48, GG)
        w00 = view(small, 54, GG)
        ssm, ssx, ssh = view(small, 60, 2), view(small, 62, 3), view(small, 65, 3)
        rm, rx, rh = view(small, 68, 2), view(small, 70, 3), view(small, 73, 3)
        mx = view(small, 76, 2)
        negm = view(small, 78, 2)
        rs = view(small, 80, 2)
        lmu, lvar = view(small, 82, 3), view(small, 85, 3)
        dg = view(small, 88, GG, TS)
        rc = view(small, 136, 4, 16)
        wsum = view(small, 200, TS)
        tmp16 = view(small, 208, 16)
        smx, snegm, srs = view(small, 224, 1), view(small, 225, 1), view(small, 226, 1)

        full = [sem(f"slot{i}_full") for i in range(6)]
        mem_in, x_in = [sem("mem0_in"), sem("mem1_in")], sem("x_in")
        gcol_in, const_in, ln_in, pool_in = sem("gcol_in"), sem("const_in"), sem("ln_in"), sem("pool_w_in")
        state_in, router_in, gfin_in = sem("state_in"), sem("router_in"), sem("gfin_in")
        cache_in = [sem("cache0_in"), sem("cache1_in")]
        kv_out, gv_out, st_out, y_out = sem("kv_out"), sem("gv_out"), sem("st_out"), sem("y_out")
        z_ready, z_done = sem("z_ready"), sem("z_done")
        aux_ready, aux_done = sem("aux_ready"), sem("aux_done")
        br_ready, merged = sem("br_ready"), sem("merged")
        id_ok, pool_chain, rc_ok = sem("id_ok"), sem("pool_chain"), sem("rc_ok")
        act_chain, dve_chain = sem("act_chain"), sem("dve_chain")
        mem_ss, mem_sqrt, x_ss, x_sqrt = sem("mem_ss"), sem("mem_sqrt"), sem("x_ss"), sem("x_sqrt")
        mem_var, x_var, ln_var, ln_sqrt = sem("mem_var"), sem("x_var"), sem("ln_var"), sem("ln_sqrt")
        xs_ready, ss_zero = sem("xs_ready"), sem("ss_zero")
        ln_done, negm_ready, exp_done = sem("ln_done"), sem("negm_ready"), sem("exp_done")
        ck_used, cv_used = sem("ck_used"), sem("cv_used")
        diff_ready, pad_ok = sem("diff_ready"), sem("pad_ok")
        s_ready, dg_ready = sem("s_ready"), sem("dg_ready")
        merge_step = sem("merge_step")
        h_done, h_ss, h_var, h_sqrt, xn2_ready = sem("h_done"), sem("h_ss"), sem("h_var"), sem("h_sqrt"), sem("xn2_ready")
        wr_copied, lg_exp_in, lg_exp = sem("wr_copied"), sem("lg_exp_in"), sem("lg_exp")
        tri_ok, sel_ready, np_ready = sem("tri_ok"), sem("sel_ready"), sem("np_ready")
        e_used, p_ready, p_step, silu_done, h_ready, y_ready = (
            sem("e_used"), sem("p_ready"), sem("p_step"), sem("silu_done"), sem("h_ready"), sem("y_ready"))
        f_ss, f_var, f_sqrt, y_final = sem("f_ss"), sem("f_var"), sem("f_sqrt"), sem("y_final")

        def dense_full(n):
            total = 0
            for k in range(n % 4, n + 1, 4):
                total += 48 if GATE0 <= k < OUT0 and (k - GATE0) % 4 == 3 else 16
            return total

        before = {s: dense_full(max(n for n in range(N_DENSE) if n % 4 == s)) for s in range(4)}
        before[4] = before[5] = 0

        win_v = w_in[0].rearrange("(p j) c -> p j c", j=KT)
        wmkv_v = w_mkv[0].rearrange("(p j) c -> p j c", j=KT)
        wo_v = w_o[0].rearrange("(j p) c -> p j c", p=P)
        bra_v = w_br_a[0].rearrange("(j p) c -> p j c", p=P)
        brb_v = w_br_b[0].rearrange("(j p) c -> p j c", p=P)
        brc_v = w_br_c[0].rearrange("(j p) c -> p j c", p=P)
        wg_v = w_gate[0].rearrange("g e (p j) f -> p (g e) (j f)", j=KT)
        wu_v = w_up[0].rearrange("g e (p j) f -> p (g e) (j f)", j=KT)
        wd_v = w_down[0].rearrange("g e (p j) n -> p (g e) (j n)", j=4)

        def slot(n):
            return view(ring, (n % 4) * CHUNK, KT, CC)

        def z_used(n):
            if n < GATE0:
                return 2 * (n + 1)
            if n < OUT0:
                return Z_G + 6 * ((n - GATE0) // 4) + 2 * ((n - GATE0) % 4 + 1)
            return Z_O + 2 * (n - OUT0 + 1)

        def gate_load(sp, g, i):
            n = GATE0 + i
            src = win_v[:, :, bass.ds(g * CC + (GATE_COL + i * D), CC)]
            sp.dma_start(slot(n), src).then_inc(full[n % 4], 16)

        def branch_load(sp, cols):
            n = GATE0 + 3
            sp.dma_start(slot(n)[:, 0:6, :], bra_v[:, :, cols]).then_inc(full[n % 4], 16)
            sp.dma_start(slot(n)[:, 6:12, :], brb_v[:, :, cols]).then_inc(full[n % 4], 16)
            sp.dma_start(slot(n)[:, 12:16, :], brc_v[:, :, cols]).then_inc(full[n % 4], 16)

        block = ctx.enter_context(nc.Block())

        @block.sync
        def _(sp):
            for t in range(2):
                sp.dma_start(mem[:, t, :], mem_prompt[0, t * P:(t + 1) * P, :]).then_inc(mem_in[t], 16)
            for n in range(GATE0):
                if n >= 4:
                    sp.wait_ge(z_ready, z_used(n - 4))
                src = wmkv_v[:, :, n * CC:(n + 1) * CC] if n < N_MKV else \
                    win_v[:, :, Z_COLS[n - N_MKV]:Z_COLS[n - N_MKV] + CC]
                sp.dma_start(slot(n), src).then_inc(full[n % 4], 16)
            for i in range(4):
                n = GATE0 + i
                sp.wait_ge(z_ready, z_used(n - 4))
                if i < 3:
                    gate_load(sp, 0, i)
                else:
                    branch_load(sp, slice(0, CC))
            with sp.Fori(0, N_GRP - 1) as g:
                for i in range(3):
                    sp.wait_ge(z_ready, g * 6 + (Z_G + 2 * (i + 1)))
                    gate_load(sp, g + 1, i)
                sp.wait_ge(br_ready, g * 2 + 2)
                branch_load(sp, bass.ds(g * CC + CC, CC))
            for c in range(8):
                n = OUT0 + c
                if c < 3 or c > 3:
                    sp.wait_ge(z_ready, z_used(n - 4))
                else:
                    sp.wait_ge(br_ready, 2 * N_GRP)
                sp.dma_start(slot(n), wo_v[:, :, c * CC:(c + 1) * CC]).then_inc(full[n % 4], 16)
            sp.wait_ge(z_ready, Z_END)
            sp.wait_ge(np_ready, 1)
            npass = sp.value_load(npass_i[0:1, 0:1], min_val=1, max_val=9)
            with sp.Fori(0, npass) as k:
                with sp.Fori(0, ROUNDS) as r:
                    it = k * ROUNDS + r
                    for c in range(CPR):
                        s = EORDER[c % ESLOTS]
                        sp.wait_ge(e_used, it * CPR + (c + 1))
                        e0 = bass.ds(r * EPR, EPR)
                        if c < 16:
                            w = wg_v if c < 8 else wu_v
                            src = w[:, e0, (c % 8) * 1024:(c % 8 + 1) * 1024]
                        else:
                            half, j = (c - 16) // 4, (c - 16) % 4
                            src = wd_v[:, e0, j * D + half * 1024:j * D + (half + 1) * 1024]
                        dst = e_slot[s].rearrange("p (e n) -> p e n", e=EPR)
                        sp.dma_start(dst, src).then_inc(full[s], 16)
            for t, (t0, n) in enumerate(TILES):
                sp.wait_ge(y_final, t + 1)
                dst = y_sample[:, 0, :] if t == 2 else y_prompt[0, t0:t0 + n, :]
                sp.dma_start(dst, x[0:n, t, :]).then_inc(y_out, 16)
            sp.wait_ge(y_out, 48)

        @block.gpsimd
        def _(pool):
            nc.gpsimd.memset(ident[:, :], 0.0).then_inc(pool_chain, 1)
            pool.wait_ge(pool_chain, 1)
            nc.gpsimd.affine_select(out=ident[:, :], in_=ident[:, :], compare_op=ALU.not_equal, fill=1.0, base=0,
                                    pattern=[[-1, P]], channel_multiplier=1).then_inc(id_ok, 1)
            row = lambda a, n: a.rearrange("(o n) -> o n", o=1).to_broadcast([n, a.shape[0]])
            pool.dma_start(wsN, w_s[0].rearrange("g i j -> i g j")).then_inc(const_in, 16)
            pool.dma_start(bs, b_s[0].rearrange("(o g) i -> o g i", o=1).to_broadcast([P, GG, P])).then_inc(const_in, 16)
            with nc.allow_non_contiguous_dma(reason="a few hundred words of per-channel constants"):
                pool.dma_start(pscale, pool_scale[0].rearrange("(k p) -> p k", p=P)).then_inc(const_in, 16)
                pool.dma_start(w00[0:TS, :], w_s[0, :, 0, 0:1].rearrange("(o g) a -> o (g a)", o=1)
                               .to_broadcast([TS, GG])).then_inc(const_in, 16)
            pool.dma_start(lng, row(ln_v_g[0], P)).then_inc(ln_in, 16)
            pool.dma_start(lnb, row(ln_v_b[0], P)).then_inc(ln_in, 16)
            for g in range(4):
                b0 = 3 * (g // 2)
                if g % 2 == 0:
                    pool.dma_start(wp[:, b0, :], w_pool[0, g, 0:P, :]).then_inc(pool_in, 16)
                    pool.dma_start(wp[0:64, b0 + 1, :], w_pool[0, g, P:PG, :]).then_inc(pool_in, 16)
                else:
                    pool.dma_start(wp[64:P, b0 + 1, :], w_pool[0, g, 0:64, :]).then_inc(pool_in, 16)
                    pool.dma_start(wp[:, b0 + 2, :], w_pool[0, g, 64:PG, :]).then_inc(pool_in, 16)
            nc.gpsimd.iota(rc, pattern=[[0, 4], [1, 16]], base=1, channel_multiplier=0,
                           allow_small_or_imprecise_dtypes=True).then_inc(rc_ok, 1)
            pool.wait_ge(const_in, 64)
            nc.gpsimd.affine_select(out=wsN, in_=wsN, compare_op=ALU.is_ge, fill=0.0, base=0,
                                    pattern=[[0, GG], [-1, P]], channel_multiplier=1).then_inc(pool_chain, 1)
            pool.dma_start(new_st_s[0, :, 0:NST - 1, :], state_pool[0, :, 1:NST, :]).then_inc(st_out, 16)
            pool.wait_ge(aux_ready, A_MEM + 8)
            pool.dma_start(stN[0:TS * NST, :], state_pool[0].rearrange("b t c -> (b t) c")).then_inc(state_in, 16)
            pool.wait_ge(z_done, Z_V)
            for t in range(2):
                pool.dma_start(new_k[0, 0, t * P:(t + 1) * P].rearrange("m h d -> m (h d)"), kvK[:, t, :]).then_inc(kv_out, 16)
                pool.dma_start(new_v[0, 0, t * P:(t + 1) * P].rearrange("m h d -> m (h d)"), kvV[:, t, :]).then_inc(kv_out, 16)
            pool.wait_ge(ln_done, 1)
            pool.dma_start(new_gv[0, :, 0, :], vN[0:TS, 2, :]).then_inc(gv_out, 16)
            for i in range(2 * TS):
                if 2 <= i < TS + 2:
                    pool.wait_ge(ck_used, i - 1)
                elif i >= TS + 2:
                    pool.wait_ge(cv_used, i - TS - 1)
                src = (cache_k if i < TS else cache_v)[0, i % TS].rearrange("(p m) h d -> p m (h d)", m=2)
                pool.dma_start(cache_flat[i % 2], src).then_inc(cache_in[i % 2], 16)
            pool.wait_ge(aux_done, A_PN + 2)
            pool.dma_start(new_st_p[0, 0], pn[0:NST, :]).then_inc(st_out, 16)
            pool.dma_start(new_st_s[0, :, NST - 1, :], pn[NST:NST + TS, :]).then_inc(st_out, 16)
            pool.wait_ge(st_out, 48)
            pool.wait_ge(kv_out, 64)
            pool.wait_ge(gv_out, 16)
            pool.wait_ge(aux_done, A_PL + 6)
            pool.dma_start(gfin, row(g_final, P)).then_inc(gfin_in, 16)
            pool.dma_start(lgb[:, 0:NG], row(b_rg[0], P)).then_inc(router_in, 16)
            pool.dma_start(lgb[:, NG:36], row(b_re[0].rearrange("g e -> (g e)"), P)).then_inc(router_in, 16)
            pool.dma_start(wrg, w_rg[0].rearrange("(p j) g -> p j g", j=KT)).then_inc(router_in, 16)
            pool.dma_start(wre, w_re[0].rearrange("g (p j) e -> p g j e", j=KT)).then_inc(router_in, 16)
            nc.gpsimd.iota(cidx, pattern=[[1, CAP]], base=0, channel_multiplier=0,
                           allow_small_or_imprecise_dtypes=True).then_inc(pool_chain, 1)
            nc.gpsimd.iota(rev, pattern=[[-1, NE]], base=NE, channel_multiplier=0,
                           allow_small_or_imprecise_dtypes=True).then_inc(tri_ok, 1)
            nc.gpsimd.iota(thr, pattern=[[CAP, 9]], base=0, channel_multiplier=0,
                           allow_small_or_imprecise_dtypes=True).then_inc(tri_ok, 1)
            pool.wait_ge(wr_copied, 1)
            nc.gpsimd.memset(ones, 1.0).then_inc(pool_chain, 1)
            pool.wait_ge(pool_chain, 4)
            nc.gpsimd.affine_select(out=tri, in_=ones, compare_op=ALU.is_gt, fill=0.0, base=0,
                                    pattern=[[1, P]], channel_multiplier=-1).then_inc(tri_ok, 1)

        @block.scalar
        def _(act):
            with nc.allow_non_contiguous_dma(reason="per-channel gains, 64 bytes a partition"):
                act.dma_start(gmemc, g_mem[0].rearrange("(p j) -> p j", j=KT)).then_inc(gcol_in, 16)
                act.dma_start(gmixc, g_mix[0].rearrange("(p j) -> p j", j=KT)).then_inc(gcol_in, 16)
                act.dma_start(gffnc, g_ffn[0].rearrange("(p j) -> p j", j=KT)).then_inc(gcol_in, 16)
            act.dma_start(x[:, 0, :], x_prompt[0, 0:P, :]).then_inc(x_in, 16)
            act.dma_start(x[:, 1, :], x_prompt[0, P:TP, :]).then_inc(x_in, 16)
            act.dma_start(x[0:TS, 2, :], x_sample[:, 0, :]).then_inc(x_in, 16)
            chain = [0]

            def link(ins):
                chain[0] += 1
                ins.then_inc(act_chain, 1)
                act.wait_ge(act_chain, chain[0])

            act.wait_ge(ss_zero, 1)
            for t in range(2):
                act.wait_ge(mem_in[t], 16)
                link(nc.scalar.activation(trunk[:, 0:D], mem[:, t, :], ACT.Square, accum_out=ssm[:, t:t + 1]))
            act.wait_ge(x_in, 48)
            act.wait_ge(mem_var, 1)
            nc.scalar.activation(rm, ssm, ACT.Sqrt).then_inc(mem_sqrt, 1)
            for t, (_, n) in enumerate(TILES):
                link(nc.scalar.activation(trunk[0:n, 0:D], x[0:n, t, :], ACT.Square, accum_out=ssx[0:n, t:t + 1]))
            act.wait_ge(x_var, 1)
            nc.scalar.activation(rx, ssx, ACT.Sqrt).then_inc(x_sqrt, 1)

            def take_z(n):
                act.wait_ge(z_ready, n + 1)
                return bank[n % 2]

            for n in range(Z_V):
                ps, c, t = take_z(n), n // 2, n % 2
                dst = (kvK if c < 2 else kvV)[:, t, (c % 2) * CC:(c % 2 + 1) * CC]
                nc.scalar.activation(dst, ps[:, 0:CC], ACT.Copy).then_inc(z_done, 1)
            for n in range(Z_V, Z_Q):
                nc.scalar.activation(vT[:, n - Z_V, :], take_z(n)[:, 0:T], ACT.Gelu).then_inc(z_done, 1)
            for n in range(Z_Q, Z_P):
                nc.scalar.activation(qT[:, n - Z_Q, :], take_z(n)[:, 0:T], ACT.Copy).then_inc(z_done, 1)
            act.wait_ge(ln_var, 1)
            nc.scalar.activation(lvar, lvar, ACT.Sqrt).then_inc(ln_sqrt, 1)
            for n in range(Z_P, Z_U):
                nc.scalar.activation(pT[:, n - Z_P, PAD:PAD + T], take_z(n)[:, 0:T], ACT.Copy).then_inc(z_done, 1)

            def exp_head(hd):
                act.wait_ge(negm_ready, hd + 1)
                if hd == 0:
                    act.wait_ge(kv_out, 64)
                ps = bank[2 + A_SC[hd] % 6]
                for t in range(2):
                    ins = nc.scalar.activation(Pp[hd % 2][t],
                                               ps[:, t * NM:(t + 1) * NM], ACT.Exp, bias=negm[:, t:t + 1],
                                               scale=SCALE, accum_out=rs[:, t:t + 1])
                    if t == 0:
                        link(ins)
                ins.then_inc(exp_done, 1)

            exp_head(0)
            exp_head(1)
            exp_head(2)
            exp_head(3)
            for n in range(Z_U, Z_G):
                nc.scalar.activation(brT[:, n - Z_U, :], take_z(n)[:, 0:T], ACT.Gelu).then_inc(z_done, 1)
            act.wait_ge(negm_ready, NH + 1)
            nc.scalar.activation(Ps[0:32, :], bank[2 + A_SS % 6][0:32, 0:256], ACT.Exp, bias=snegm[0:32],
                                 scale=SCALE, accum_out=srs[0:32]).then_inc(exp_done, 1)
            with act.Fori(0, N_GRP) as g:
                for i in range(3):
                    for b in range(2):
                        n = 2 * i + b
                        act.wait_ge(z_ready, g * 6 + (Z_G + n + 1))
                        if i == 0:
                            act.wait_ge(merged, g * 2 + (b + 1))
                        nc.scalar.activation(sg[:, b, i, :], bank[n % 2][:, 0:T], ACT.Sigmoid).then_inc(z_done, 1)
            for n in range(Z_O, Z_END):
                ps = take_z(n)
                b = n - Z_O
                if b >= 2:
                    act.wait_ge(aux_ready, A_O + b - 1)
                else:
                    act.wait_ge(merged, 2 + 2 * N_GRP)
                nc.scalar.activation(oT[:, b % 2, :], ps[:, 0:T], ACT.Copy).then_inc(z_done, 1)
            act.wait_ge(h_done, 1)
            for t, (_, n) in enumerate(TILES):
                link(nc.scalar.activation(trunk[0:n, 0:D], x[0:n, t, :], ACT.Square, accum_out=ssh[0:n, t:t + 1]))
            act.wait_ge(h_var, 1)
            nc.scalar.activation(rh, ssh, ACT.Sqrt).then_inc(h_sqrt, 1)
            act.wait_ge(lg_exp_in, 1)
            nc.scalar.activation(r4[0], r4[0], ACT.Exp).then_inc(lg_exp, 1)
            act.wait_ge(lg_exp_in, 2)
            nc.scalar.activation(r1[5], r1[5], ACT.Exp).then_inc(lg_exp, 1)
            act.wait_ge(np_ready, 1)
            npass = act.value_load(npass_i[0:1, 0:1], min_val=1, max_val=9)
            with act.Fori(0, npass) as k:
                with act.Fori(0, ROUNDS) as r:
                    it = k * ROUNDS + r
                    act.wait_ge(e_used, it * CPR + (CREDIT + 8))
                    nc.scalar.activation(hs, bank[0][:, :], ACT.Silu).then_inc(silu_done, 1)
                    for n in range(4):
                        if n % 2 == 0:
                            act.wait_ge(e_used, it * CPR + (CREDIT + 20 + 2 * n))
                        nc.scalar.activation(y[:, n, :], bank[2 + n][:, :], ACT.Copy).then_inc(y_ready, 1)
            act.wait_ge(aux_done, npass * (JPR * ROUNDS) + A_E)
            for t, (_, n) in enumerate(TILES):
                act.wait_ge(act_chain, chain[0])
                nc.scalar.activation(trunk[0:n, t * D:(t + 1) * D], x[0:n, t, :], ACT.Square,
                                     accum_out=ssx[0:n, t:t + 1]).then_inc(f_ss, 1)
            act.wait_ge(f_var, 1)
            nc.scalar.activation(rx, ssx, ACT.Sqrt).then_inc(f_sqrt, 1)

        @block.vector
        def _(dve):
            chain = [0]

            def link(ins):
                chain[0] += 1
                ins.then_inc(dve_chain, 1)
                dve.wait_ge(dve_chain, chain[0])

            def take(job):
                dve.wait_ge(aux_ready, job + 1)
                return bank[2 + job % 6]

            V = nc.vector
            nc.vector.memset(small[:, 60:68], 1.0).then_inc(ss_zero, 1)
            V.memset(pT[:, :, 0:PAD], 0.0).then_inc(pad_ok, 1)
            V.memset(rx, 1.0).then_inc(merged, 2)
            V.memset(rm, 1.0).then_inc(e_used, CREDIT)

            def mean_eps(ss, n, done):
                V.tensor_scalar(ss, ss, 1.0 / n, EPS, ALU.mult, ALU.add).then_inc(done, 1)

            dve.wait_ge(act_chain, 2)
            mean_eps(ssm, D, mem_var)
            dve.wait_ge(mem_sqrt, 1)
            link(V.reciprocal(rm, rm))
            for t in range(2):
                V.tensor_scalar(xs[:, t, :], mem[:, t, :], rm[:, t:t + 1], None, ALU.mult).then_inc(xs_ready, 1)

            def take_t4(job, dst, gain, q, t0):
                ps = take(job)
                V.tensor_tensor(dst[:, 4 * q:4 * q + 4, t0:t0 + P], ps[:, :].rearrange("p (j t) -> p j t", j=4),
                                gain[:, 4 * q:4 * q + 4].unsqueeze(2).to_broadcast([P, 4, P]), ALU.mult).then_inc(aux_done, 1)

            dve.wait_ge(gcol_in, 48)
            for q in range(4):
                take_t4(A_MEM + q, memT, gmemc, q, 0)
            dve.wait_ge(act_chain, 5)
            mean_eps(ssx, D, x_var)
            dve.wait_ge(x_sqrt, 1)
            link(V.reciprocal(rx, rx))
            V.tensor_scalar(xs[:, 0, :], x[:, 0, :], rx[:, 0:1], None, ALU.mult).then_inc(xs_ready, 1)
            for q in range(4):
                take_t4(A_MEM + 4 + q, memT, gmemc, q, P)
            V.tensor_scalar(xs[:, 1, :], x[:, 1, :], rx[:, 1:2], None, ALU.mult).then_inc(xs_ready, 1)
            for q in range(4):
                take_t4(A_X + q, xnT, gmixc, q, 0)
            V.tensor_scalar(xs[0:TS, 0, :], x[0:TS, 2, :], rx[0:TS, 2:3], None, ALU.mult).then_inc(xs_ready, 1)
            for q in range(4):
                take_t4(A_X + 4 + q, xnT, gmixc, q, P)
            ps = take(A_X + 8)
            V.tensor_tensor(xnT[:, :, TP:T], ps[:, 0:P].rearrange("p (j t) -> p j t", j=KT),
                            gmixc.unsqueeze(2).to_broadcast([P, KT, TS]), ALU.mult).then_inc(aux_done, 1)
            for hd in range(NH):
                ps = take(A_KT + hd)
                V.tensor_copy(kT[:, hd, :], ps[:, 0:NM]).then_inc(aux_done, 1)
            dve.wait_ge(const_in, 64)
            dve.wait_ge(id_ok, 1)
            V.tensor_tensor(dg[0:TS], ident[0:TS, 0:TS].unsqueeze(1).to_broadcast([TS, GG, TS]),
                            w00[0:TS, :].unsqueeze(2).to_broadcast([TS, GG, TS]), ALU.mult).then_inc(dg_ready, 1)
            for i in range(2):
                ps, n = take(A_WS + i), 4 - 2 * i
                V.tensor_copy(wsT[:, 4 * i:4 * i + n, :].rearrange("p g i -> p (g i)"), ps[:, 0:n * P]).then_inc(aux_done, 1)
            for t, (_, n) in enumerate(TILES):
                for i in range(2):
                    ps, w = take(A_VN + 2 * t + i), 512 - 256 * i
                    V.tensor_copy(vN[0:n, t, 512 * i:512 * i + w], ps[0:n, 0:w]).then_inc(aux_done, 1)
            link(V.memset(small[:, 82:88], 1.0))
            dve.wait_ge(aux_done, A_VN + 6)
            dve.wait_ge(ln_in, 32)
            dve.wait_ge(aux_ready, A_WS + 2)
            for t, (_, n) in enumerate(TILES):
                v = vN[0:n, t, :]
                link(V.tensor_reduce(lmu[0:n, t:t + 1], v, AX.X, ALU.add))
                link(V.tensor_scalar(lmu[0:n, t:t + 1], lmu[0:n, t:t + 1], -1.0 / BW, None, ALU.mult))
                link(V.tensor_scalar(v, v, lmu[0:n, t:t + 1], None, ALU.add))
                ins = V.tensor_tensor_reduce(out=prod_flat[0:n, 0:BW], in0=v, in1=v, scale=1.0, scalar=0.0,
                                             op0=ALU.mult, op1=ALU.add, accum_out=lvar[0:n, t:t + 1])
                link(ins)
            V.tensor_scalar(lvar, lvar, 1.0 / BW, EPS, ALU.mult, ALU.add).then_inc(ln_var, 1)
            dve.wait_ge(ln_sqrt, 1)
            link(V.reciprocal(lvar, lvar))
            for t, (_, n) in enumerate(TILES):
                v = vN[0:n, t, :]
                link(V.scalar_tensor_tensor(out=v, in0=v, scalar=lvar[0:n, t:t + 1], in1=lng[0:n, :],
                                            op0=ALU.mult, op1=ALU.mult))
                ins = V.tensor_tensor(v, v, lnb[0:n, :], ALU.add)
                if t < 2:
                    link(ins)
            ins.then_inc(ln_done, 1)
            for i in range(2):
                ps, n = take(A_ST + i), 4 - 2 * i
                V.tensor_copy(ext[:, 4 * i:4 * i + n, :, 0:NST],
                              ps[:, 0:n * 120].rearrange("p (k b t) -> p k b t", k=n, b=TS)).then_inc(aux_done, 1)
            dve.wait_ge(z_done, Z_U)
            link(V.tensor_copy(ext[:, :, :, NST], pT[:, :, PAD + TP:PAD + T]))
            ps = take(A_QN)
            V.tensor_copy(qn[0:TS, :], ps[0:TS, 0:512]).then_inc(aux_done, 1)

            def head_max(hd):
                ps = take(A_SC[hd])
                link(V.tensor_reduce(mx, ps[:, :].rearrange("p (t m) -> p t m", t=2), AX.X, ALU.max))
                V.tensor_scalar(negm, mx, -SCALE, None, ALU.mult).then_inc(negm_ready, 1)

            def head_norm(hd):
                dve.wait_ge(exp_done, hd + 1)
                link(V.reciprocal(rs, rs))
                link(V.tensor_scalar(Pp[hd % 2][0], Pp[hd % 2][0], rs[:, 0:1], None, ALU.mult))
                V.tensor_scalar(Pp[hd % 2][1], Pp[hd % 2][1], rs[:, 1:2], None, ALU.mult).then_inc(aux_done, 1)

            def head_out(hd):
                ps = take(A_HEAD[hd])
                V.tensor_copy(PpT_flat[hd % 2], ps[:, :]).then_inc(aux_done, 1)
                ps = take(A_HEAD[hd] + 1)
                V.tensor_copy(brT[:, 12 + hd, 0:TP], ps[:, 0:TP]).then_inc(aux_done, 1)

            head_max(0)
            head_norm(0)
            head_max(1)
            head_norm(1)
            for hd in range(NH):
                head_out(hd)
                if hd + 2 < NH:
                    head_max(hd + 2)
                    head_norm(hd + 2)
            for b in range(TS):
                dve.wait_ge(cache_in[b % 2], 16 * (b // 2 + 1))
                ps = take(A_QB + b)
                if b:
                    dve.wait_ge(ck_used, b)
                V.tensor_tensor(prod, cache[b % 2], ps[:, :].unsqueeze(1).to_broadcast([P, 2, 512]),
                                ALU.mult).then_inc(aux_done, 1)
                dve.wait_ge(aux_done, A_QB + b + 1)
                V.tensor_reduce(sT[:, :, 4 * b:4 * b + 4], prod.rearrange("p m (h d) -> p m h d", h=NH),
                                AX.X, ALU.add).then_inc(ck_used, 1)
            dve.wait_ge(pad_ok, 1)
            link(V.tensor_tensor(stA[:, :, 1:272], pT[:, :, 1:272], pT[:, :, 0:271], ALU.add))
            dve.wait_ge(rc_ok, 1)
            for g, w in enumerate(WINDOWS):
                link(V.tensor_scalar(rc[:, g, :], rc[:, g, :], float(w), None, ALU.min))
            link(V.reciprocal(rc, rc))
            src, other = stA, stB
            for g, w in enumerate(WINDOWS):
                if g:
                    b0 = (1, 3, 4)[g - 1]
                    lo = w - 1
                    link(V.tensor_tensor(other[:, b0:, lo:272], src[:, b0:, lo:272], src[:, b0:, lo - w // 2:272 - w // 2],
                                         ALU.add))
                    src, other = other, src
                b0 = 3 * (g // 2)
                pieces = ((b0, 0, P), (b0 + 1, 0, 64)) if g % 2 == 0 else ((b0 + 1, 64, P), (b0 + 2, 0, P))
                for k, p0, p1 in pieces:
                    V.scalar_tensor_tensor(out=diff[p0:p1, k, PAD:TP], in0=src[p0:p1, k, 2 * PAD:PAD + TP], scalar=1.0 / w,
                                           in1=pT[p0:p1, k, 2 * PAD:PAD + TP], op0=ALU.mult, op1=ALU.subtract)
                    link(V.tensor_tensor(tmp16[p0:p1, :], src[p0:p1, k, PAD:2 * PAD], rc[p0:p1, g, :], ALU.mult))
                    link(V.tensor_tensor(diff[p0:p1, k, 0:PAD], tmp16[p0:p1, :], pT[p0:p1, k, PAD:2 * PAD], ALU.subtract))
                    link(V.tensor_reduce(wsum[p0:p1, :], ext[p0:p1, k, :, PAD - w:PAD], AX.X, ALU.add))
                    link(V.scalar_tensor_tensor(out=diff[p0:p1, k, TP:T], in0=wsum[p0:p1, :], scalar=1.0 / w,
                                                in1=pT[p0:p1, k, PAD + TP:PAD + T], op0=ALU.mult, op1=ALU.subtract))
            dve.nop().then_inc(diff_ready, 1)
            ps = take(A_SS)
            link(V.tensor_reduce(smx[0:32], ps[0:32, 0:256], AX.X, ALU.max))
            V.tensor_scalar(snegm[0:32], smx[0:32], -SCALE, None, ALU.mult).then_inc(negm_ready, 1)
            dve.wait_ge(exp_done, NH + 1)
            link(V.reciprocal(srs[0:32], srs[0:32]))
            V.tensor_scalar(Ps[0:32, :], Ps[0:32, :], srs[0:32], None, ALU.mult).then_inc(aux_done, 1)
            for i in range(2):
                ps, w = take(A_PN + i), 512 - 256 * i
                V.tensor_copy(pn[0:NST + TS, 512 * i:512 * i + w], ps[0:NST + TS, 0:w]).then_inc(aux_done, 1)
            ps = take(A_SP)
            V.tensor_copy(PsT.rearrange("p m c -> p (m c)"), ps[:, 0:64]).then_inc(aux_done, 1)
            ps = take(A_SV)
            V.tensor_copy(brT[:, 12:16, TP:T], ps[:, 0:32].rearrange("p (h b) -> p h b", h=NH)).then_inc(aux_done, 1)
            dve.wait_ge(z_done, Z_G)
            dve.wait_ge(const_in, 64)
            for t in range(2):
                for i in range(2):
                    ps, g0, n = take(A_MX + 2 * t + i), 4 * i, 4 - 2 * i
                    link(V.tensor_tensor(mixt[:, 0:n, :], ps[:, 0:n * P].rearrange("p (g i) -> p g i", g=n),
                                         bs[:, g0:g0 + n, :], ALU.add))
                    u = brT[:, g0:g0 + n, t * P:(t + 1) * P]
                    V.tensor_tensor(u, u, mixt[:, 0:n, :], ALU.mult).then_inc(aux_done, 1)
                    dve.wait_ge(aux_done, A_MX + 2 * t + i + 1)
            ps = take(A_MX + 4)
            m8 = prod_flat[:, 0:GG * TS].rearrange("p (g t) -> p g t", g=GG)
            link(V.tensor_tensor(m8, ps[:, 0:GG * TS].rearrange("p (g t) -> p g t", g=GG),
                                 bs[:, :, 0:1].to_broadcast([P, GG, TS]), ALU.add))
            V.tensor_tensor(brT[:, 0:GG, TP:T], brT[:, 0:GG, TP:T], m8, ALU.mult).then_inc(aux_done, 1)
            for k in range(GG):
                ps = take(A_PL + k)
                V.tensor_scalar(brT[:, GG + k, :], ps[:, 0:T], pscale[:, k:k + 1], None, ALU.mult).then_inc(aux_done, 1)

            with dve.Fori(0, N_GRP) as g:
                for b in range(2):
                    dve.wait_ge(z_done, g * 6 + (Z_G + 5 + b))
                    dve.wait_ge(br_ready, g * 2 + (b + 1))
                    if b == 1:
                        dve.wait_ge(merged, g * 2 + 3)
                    else:
                        dve.wait_ge(merged, g * 2 + 2)
                    for i in range(3):
                        V.tensor_tensor(gp[:, i, :], sg[:, b, i, :], bank[2 + 3 * b + i][:, 0:T], ALU.mult).then_inc(merge_step, 1)
                    dve.wait_ge(merge_step, g * 8 + (4 * b + 3))
                    V.tensor_tensor(gp[:, 3, :], gp[:, 0, :], gp[:, 1, :], ALU.add).then_inc(merge_step, 1)
                    dve.wait_ge(merge_step, g * 8 + (4 * b + 4))
                    V.tensor_tensor(trunk[:, bass.ds(g * (2 * T) + (2 * KT * T + b * T), T)], gp[:, 3, :], gp[:, 2, :],
                                    ALU.add).then_inc(merged, 1)

            for b in range(16):
                ps = take(A_O + b)
                cols = slice(b * P, (b + 1) * P)
                link(V.tensor_tensor(x[0:TS, 2, cols], x[0:TS, 2, cols], ps[0:TS, 2 * P:3 * P], ALU.add))
                V.tensor_tensor(x[:, 0:2, cols], x[:, 0:2, cols], ps[:, 0:2 * P].rearrange("p (t c) -> p t c", t=2),
                                ALU.add).then_inc(aux_done, 1)
            dve.wait_ge(router_in, 64)
            V.memset(lg, 0.0).then_inc(h_done, 1)
            dve.wait_ge(aux_done, A_O + 16)
            link(V.tensor_copy(wr[:, :, 0:NG], wrg))
            V.tensor_copy(wr[:, :, NG:36].rearrange("p j (g e) -> p g j e", g=NG), wre).then_inc(wr_copied, 1)
            dve.wait_ge(act_chain, 2 + 3 + NH + 3)
            V.tensor_scalar(ssh, ssh, 1.0 / D, EPS, ALU.mult, ALU.add).then_inc(h_var, 1)
            dve.wait_ge(h_sqrt, 1)
            link(V.reciprocal(rh, rh))
            for t, (_, n) in enumerate(TILES):
                V.tensor_scalar(xn2[0:n, t].rearrange("p j c -> p c j"), x[0:n, t, :].rearrange("p (c j) -> p c j", j=KT),
                                rh[0:n, t:t + 1], None, ALU.mult).then_inc(xn2_ready, 1)
                if t < 2:
                    for q in range(4):
                        take_t4(A_RT + 4 * t + q, xn2T, gffnc, q, t * P)
            ps = take(A_RT + 8)
            V.tensor_tensor(xn2T[:, :, TP:T], ps[:, 0:P].rearrange("p (j t) -> p j t", j=KT),
                            gffnc.unsqueeze(2).to_broadcast([P, KT, TS]), ALU.mult).then_inc(aux_done, 1)

            ps = take(A_LG)
            bias2 = lgb.unsqueeze(1).to_broadcast([P, 2, 36])
            V.tensor_tensor(lg[:, 0:2, :], ps[:, 0:72].rearrange("p (t c) -> p t c", t=2), bias2, ALU.add)
            link(V.tensor_tensor(lg[0:TS, 2, :], ps[0:TS, 72:108], lgb[0:TS, :], ALU.add))
            dve.wait_ge(tri_ok, 3)
            V.memset(comb, 0.0)
            V.memset(sel, 0.0).then_inc(aux_done, 1)

            def over(a, n):
                return a.unsqueeze(2).to_broadcast([P, 3, n])

            def first_max(vals, n, m, eq, key, km, hot):
                link(V.tensor_reduce(m, vals, AX.X, ALU.max))
                link(V.tensor_tensor(eq, vals, over(m, n), ALU.is_equal))
                link(V.tensor_tensor(key, eq, rev[:, 0:n].unsqueeze(1).to_broadcast([P, 3, n]), ALU.mult))
                link(V.tensor_reduce(km, key, AX.X, ALU.max))
                link(V.tensor_tensor(hot, key, over(km, n), ALU.is_equal))

            gl = lg[:, :, 0:NG]
            gmax, km, gsum, m1, m2, dm, den, w1, w2 = r1[0], r1[1], r1[2], r1[3], r1[4], r1[5], r1[6], r1[7], r1[8]
            ohg = r4[1]
            first_max(gl, NG, gmax, r4[0], r4[2], km, ohg)
            V.tensor_tensor(r4[0], gl, over(gmax, NG), ALU.subtract).then_inc(lg_exp_in, 1)
            link(V.tensor_tensor(t32, lg[:, :, NG:36].rearrange("p t (g e) -> p t g e", g=NG),
                                 ohg.unsqueeze(3).to_broadcast([P, 3, NG, NE]), ALU.mult))
            esel, oh1, oh2, eqk, e2 = r8
            link(V.tensor_reduce(esel, t32.rearrange("p t g e -> p t e g"), AX.X, ALU.add))
            first_max(esel, NE, m1, oh2, eqk, km, oh1)
            link(V.scalar_tensor_tensor(out=e2, in0=oh1, scalar=-1e30, in1=esel, op0=ALU.mult, op1=ALU.add))
            first_max(e2, NE, m2, eqk, esel, km, oh2)
            V.tensor_tensor(dm, m2, m1, ALU.subtract).then_inc(lg_exp_in, 1)
            dve.wait_ge(lg_exp, 2)
            link(V.tensor_reduce(gsum, r4[0], AX.X, ALU.add))
            link(V.tensor_scalar(den, dm, 1.0, None, ALU.add))
            link(V.tensor_tensor(den, den, gsum, ALU.mult))
            link(V.reciprocal(w1, den))
            link(V.tensor_tensor(w2, w1, dm, ALU.mult))
            link(V.tensor_tensor(eqk, oh2, over(w2, NE), ALU.mult))
            link(V.tensor_tensor(esel, oh1, over(w1, NE), ALU.mult))
            link(V.tensor_tensor(esel, esel, eqk, ALU.add))
            link(V.tensor_tensor(e2, oh1, oh2, ALU.add))
            for p1, t0, t1 in ((P, 0, 2), (TS, 2, 3)):
                n = t1 - t0
                hot = ohg[0:p1, t0:t1].unsqueeze(3).to_broadcast([p1, n, NG, NE])
                V.tensor_tensor(sel[0:p1, t0:t1], hot, e2[0:p1, t0:t1].unsqueeze(2).to_broadcast([p1, n, NG, NE]),
                                ALU.mult).then_inc(sel_ready, 1)
                V.tensor_tensor(comb[0:p1, t0:t1], hot, esel[0:p1, t0:t1].unsqueeze(2).to_broadcast([p1, n, NG, NE]),
                                ALU.mult).then_inc(sel_ready, 1)
            dve.wait_ge(sel_ready, 4)
            ps = take(A_POS)
            link(V.scalar_tensor_tensor(out=pos[:, :, 0:NX], in0=self_, scalar=-FAR, in1=ps[:, 0:96].rearrange("p (t x) -> p t x", t=3),
                                        op0=ALU.mult, op1=ALU.add))
            link(V.tensor_scalar(pos[:, :, 0:NX], pos[:, :, 0:NX], FAR, None, ALU.add))
            link(V.tensor_scalar(pos[:, :, NX:NX + EPR], pos[:, :, 0:EPR], -float(CAP), None, ALU.add))
            link(V.tensor_copy(combx[:, :, NX:NX + EPR], combx[:, :, 0:EPR]))

            def slot_maps(e0, step):
                V.tensor_tensor(P01, pos[:, :, e0].unsqueeze(3).to_broadcast([P, 3, EPR, CAP]),
                                cidx.unsqueeze(1).unsqueeze(1).to_broadcast([P, 3, EPR, CAP]), ALU.is_equal).then_inc(p_step, 1)
                dve.wait_ge(p_step, step)
                V.tensor_tensor(Pw, P01, combx[:, :, e0].unsqueeze(3).to_broadcast([P, 3, EPR, CAP]), ALU.mult).then_inc(p_ready, 1)

            slot_maps(slice(0, EPR), 1)
            link(V.tensor_reduce(npf[:, 0:1], ps[:, 96:128], AX.X, ALU.max))
            link(V.tensor_scalar(thr2, thr, npf[:, 0:1], None, ALU.is_lt))
            V.tensor_reduce(npf[:, 1:2], thr2, AX.X, ALU.add).then_inc(aux_done, 1)
            dve.wait_ge(aux_done, A_POS + 1)
            V.tensor_copy(npass_i[:, :], npf[:, 1:2]).then_inc(np_ready, 1)
            dve.wait_ge(np_ready, 1)
            npass = dve.value_load(npass_i[0:1, 0:1], min_val=1, max_val=9)
            with dve.Fori(0, npass) as k:
                with dve.Fori(0, ROUNDS) as r:
                    it = k * ROUNDS + r
                    for q in range(4):
                        dve.wait_ge(aux_ready, it * JPR + (A_E + q + 1))
                        V.tensor_tensor(xgT[:, 4 * q:4 * q + 4, :], bank[6 + q % 2][:, :].rearrange("p (j t) -> p j t", j=4),
                                        gffnc[:, 4 * q:4 * q + 4].unsqueeze(2).to_broadcast([P, 4, P]),
                                        ALU.mult).then_inc(aux_done, 1)
                    dve.wait_ge(aux_ready, it * JPR + (A_E + 5))
                    V.tensor_copy(PwT, bank[6][:, 0:T]).then_inc(aux_done, 1)
                    slot_maps(bass.ds(r * EPR + EPR, EPR), it + k + 2)
                    dve.wait_ge(silu_done, it + 1)
                    dve.wait_ge(e_used, it * CPR + (CREDIT + 16))
                    V.tensor_tensor(h.rearrange("s j p -> s p j"), hs.rearrange("s (p j) -> s p j", j=4),
                                    bank[1][:, :].rearrange("s (p j) -> s p j", j=4), ALU.mult).then_inc(h_ready, 1)
                    dve.wait_ge(aux_ready, it * JPR + (A_E + 6))
                    V.tensor_copy(hT.rearrange("p j s -> p (j s)"), bank[7][:, :]).then_inc(aux_done, 1)
                    for n in range(4):
                        for t, (_, cnt) in enumerate(TILES):
                            q = 6 + 3 * n + t
                            dve.wait_ge(aux_ready, it * JPR + (A_E + q + 1))
                            xv = x[0:cnt, t, n * 512:(n + 1) * 512]
                            V.tensor_tensor(xv, xv, bank[6 + q % 2][0:cnt, :], ALU.add).then_inc(aux_done, 1)
                V.tensor_scalar(cidx, cidx, float(CAP), None, ALU.add).then_inc(p_step, 1)
                dve.wait_ge(p_step, k * (ROUNDS + 1) + (ROUNDS + 2))
            dve.wait_ge(f_ss, 3)
            V.tensor_scalar(ssx, ssx, 1.0 / D, EPS, ALU.mult, ALU.add).then_inc(f_var, 1)
            dve.wait_ge(f_sqrt, 1)
            link(V.reciprocal(rx, rx))
            dve.wait_ge(gfin_in, 16)
            for t, (_, n) in enumerate(TILES):
                V.scalar_tensor_tensor(out=x[0:n, t, :], in0=x[0:n, t, :], scalar=rx[0:n, t:t + 1], in1=gfin[0:n, :],
                                       op0=ALU.mult, op1=ALU.mult).then_inc(y_final, 1)

        @block.tensor
        def _(pe):
            mm, tr = nc.tensor.matmul, nc.tensor.transpose

            def aux(job):
                if job >= 6:
                    pe.wait_ge(aux_done, job - 5)
                return bank[2 + job % 6]

            def z(n):
                if n >= 2:
                    pe.wait_ge(z_done, n - 1)
                return bank[n % 2]

            def rows_to_columns(base, src, n, wait):
                wait()
                if n == P:
                    for q in range(4):
                        ps = aux(base + q)
                        for j in range(4):
                            ins = tr(ps[:, j * P:(j + 1) * P], src(4 * q + j), ident[:, :])
                        ins.then_inc(aux_ready, 1)
                else:
                    ps = aux(base)
                    for j in range(KT):
                        ins = tr(ps[:, j * n:(j + 1) * n], src(j), ident[0:n, 0:n])
                    ins.then_inc(aux_ready, 1)

            def strided(b, n):
                v = xs[0:n, b, :].rearrange("p (c j) -> p j c", j=KT)
                return lambda j: v[:, j, :]

            pe.wait_ge(id_ok, 1)
            rows_to_columns(A_MEM, strided(0, P), P, lambda: pe.wait_ge(xs_ready, 1))
            rows_to_columns(A_MEM + 4, strided(1, P), P, lambda: pe.wait_ge(xs_ready, 2))
            rows_to_columns(A_X, strided(0, P), P, lambda: pe.wait_ge(xs_ready, 3))
            rows_to_columns(A_X + 4, strided(1, P), P, lambda: pe.wait_ge(xs_ready, 4))
            rows_to_columns(A_X + 8, strided(0, TS), TS, lambda: pe.wait_ge(xs_ready, 5))
            pe.wait_ge(aux_done, A_MEM + 8)
            for c in range(N_MKV):
                pe.wait_ge(full[c % 4], dense_full(c))
                w = slot(c)
                for t in range(2):
                    ps = z(2 * c + t)
                    for j in range(KT):
                        ins = mm(ps[:, 0:CC], memT[:, j, t * P:(t + 1) * P], w[:, j, :], start=j == 0, stop=j == KT - 1)
                    ins.then_inc(z_ready, 1)

            def project(c):
                n = N_MKV + c
                pe.wait_ge(full[n % 4], dense_full(n))
                w = slot(n)
                for b in range(2):
                    ps = z(2 * n + b)
                    for j in range(KT):
                        ins = mm(ps[:, 0:T], w[:, j, b * P:(b + 1) * P], xnT[:, j, :], start=j == 0, stop=j == KT - 1)
                    ins.then_inc(z_ready, 1)

            pe.wait_ge(aux_done, A_X + 9)
            for c in range(3):
                project(c)
            for hd in range(NH):
                ps = aux(A_KT + hd)
                for t in range(2):
                    ins = tr(ps[:, t * P:(t + 1) * P], kvK[:, t, hd * P:(hd + 1) * P], ident[:, :])
                ins.then_inc(aux_ready, 1)
            project(3)
            project(4)
            pe.wait_ge(pool_chain, 2)
            for i in range(2):
                ps, n = aux(A_WS + i), 4 - 2 * i
                for g in range(n):
                    ins = tr(ps[:, g * P:(g + 1) * P], wsN[:, 4 * i + g, :], ident[:, :])
                ins.then_inc(aux_ready, 1)
            pe.wait_ge(z_done, Z_Q)
            for t, (t0, cnt) in enumerate(TILES):
                for i in range(2):
                    ps, n = aux(A_VN + 2 * t + i), 4 - 2 * i
                    for g in range(n):
                        ins = tr(ps[0:cnt, g * P:(g + 1) * P], vT[:, 4 * i + g, t0:t0 + cnt], ident[:, :])
                    ins.then_inc(aux_ready, 1)
            for c in range(5, 8):
                project(c)
            pe.wait_ge(state_in, 16)
            for i in range(2):
                ps, n = aux(A_ST + i), 4 - 2 * i
                for g in range(n):
                    ins = tr(ps[:, g * 120:(g + 1) * 120], stN[0:120, (4 * i + g) * P:(4 * i + g + 1) * P],
                             ident[0:120, 0:120])
                ins.then_inc(aux_ready, 1)
            ps = aux(A_QN)
            for hd in range(NH):
                ins = tr(ps[0:TS, hd * P:(hd + 1) * P], qT[:, hd, TP:T], ident[:, :])
            ins.then_inc(aux_ready, 1)

            def scores(hd):
                ps = aux(A_SC[hd])
                for t in range(2):
                    ins = mm(ps[:, t * NM:(t + 1) * NM], qT[:, hd, t * P:(t + 1) * P], kT[:, hd, :], start=True, stop=True)
                ins.then_inc(aux_ready, 1)

            pe.wait_ge(aux_done, A_KT + 4)
            scores(0)
            scores(1)
            project(8)
            for hd in range(NH):
                ps = aux(A_HEAD[hd])
                pe.wait_ge(aux_done, A_SC[hd] + 1)
                for m in range(2):
                    for t in range(2):
                        ins = tr(ps[:, m * NM + t * P:m * NM + (t + 1) * P], Pp[hd % 2][t][:, m * P:(m + 1) * P],
                                 ident[:, :])
                ins.then_inc(aux_ready, 1)
                ps = aux(A_HEAD[hd] + 1)
                pe.wait_ge(aux_done, A_HEAD[hd] + 1)
                for m in range(2):
                    ins = mm(ps[:, 0:TP], kvV[:, m, hd * P:(hd + 1) * P], PpT[hd % 2][m], start=m == 0, stop=m == 1)
                ins.then_inc(aux_ready, 1)
                if hd + 2 < NH:
                    scores(hd + 2)
            pe.wait_ge(aux_done, A_QN + 1)
            for b in range(TS):
                ps = aux(A_QB + b)
                mm(ps[:, :], ident[0:TS, b:b + 1].to_broadcast([TS, P]), qn[0:TS, :], start=True, stop=True).then_inc(aux_ready, 1)
            project(9)
            pe.wait_ge(ck_used, TS)
            ps = aux(A_SS)
            for m in range(2):
                ins = tr(ps[0:32, m * P:(m + 1) * P], sT[:, m, :], ident[:, :])
            ins.then_inc(aux_ready, 1)
            for i in range(2):
                ps, n = aux(A_PN + i), 4 - 2 * i
                for g in range(n):
                    ins = tr(ps[0:NST + TS, g * P:(g + 1) * P], pT[:, 4 * i + g, PAD + TP - NST:PAD + T], ident[:, :])
                ins.then_inc(aux_ready, 1)
            project(10)
            ps = aux(A_SP)
            pe.wait_ge(aux_done, A_SS + 1)
            for m in range(2):
                ins = tr(ps[:, m * 32:(m + 1) * 32], Ps[0:32, m * P:(m + 1) * P], ident[0:32, 0:32])
            ins.then_inc(aux_ready, 1)
            ps = aux(A_SV)
            pe.wait_ge(aux_done, A_SP + 1)
            for b in range(TS):
                pe.wait_ge(cache_in[b % 2], 64 + 16 * (b // 2 + 1))
                for hd in range(NH):
                    for m in range(2):
                        ins = mm(ps[:, hd * TS + b:hd * TS + b + 1], cache[b % 2][:, m, hd * P:(hd + 1) * P],
                                 PsT[:, m, 4 * b + hd:4 * b + hd + 1], start=m == 0, stop=m == 1)
                ins.then_inc(cv_used if b < TS - 1 else aux_ready, 1)
            pe.wait_ge(ln_done, 1)
            pe.wait_ge(aux_done, A_WS + 2)
            for t in range(2):
                for i in range(2):
                    ps, n = aux(A_MX + 2 * t + i), 4 - 2 * i
                    for g in range(n):
                        ins = mm(ps[:, g * P:(g + 1) * P], vN[:, t, (4 * i + g) * P:(4 * i + g + 1) * P], wsT[:, 4 * i + g, :],
                                 start=True, stop=True)
                    ins.then_inc(aux_ready, 1)
            ps = aux(A_MX + 4)
            pe.wait_ge(dg_ready, 1)
            for g in range(GG):
                ins = mm(ps[:, g * TS:(g + 1) * TS], vN[0:TS, 2, g * P:(g + 1) * P], dg[0:TS, g, :], start=True, stop=True)
            ins.then_inc(aux_ready, 1)
            pe.wait_ge(diff_ready, 1)
            pe.wait_ge(pool_in, 128)
            for k in range(GG):
                ps = aux(A_PL + k)
                b0 = 3 * (k // 3)
                lo = ((b0, 0, P), (b0 + 1, 0, 64))
                hi = ((b0 + 1, 64, P), (b0 + 2, 0, P))
                parts = (((0, P, lo, 0),), ((0, 64, lo, P), (64, P, hi, 0)), ((0, P, hi, 64),))[k % 3]
                for o0, o1, ins_of, c0 in parts:
                    for i, (kb, p0, p1) in enumerate(ins_of):
                        ins = mm(ps[o0:o1, 0:T], wp[p0:p1, kb, c0:c0 + o1 - o0], diff[p0:p1, kb, :], start=i == 0, stop=i == 1)
                ins.then_inc(aux_ready, 1)

            pe.wait_ge(aux_done, A_PL + 6)
            with pe.Fori(0, N_GRP) as g:
                for i in range(3):
                    n = GATE0 + i
                    pe.wait_ge(full[n % 4], g * 16 + dense_full(n))
                    w = slot(n)
                    for b in range(2):
                        pe.wait_ge(z_done, g * 6 + (Z_G + 2 * i + b - 1))
                        ps = bank[b]
                        for j in range(KT):
                            ins = mm(ps[:, 0:T], w[:, j, b * P:(b + 1) * P], xnT[:, j, :], start=j == 0, stop=j == KT - 1)
                        ins.then_inc(z_ready, 1)
                n = GATE0 + 3
                pe.wait_ge(full[n % 4], g * 48 + dense_full(n))
                w = slot(n)
                for b in range(2):
                    pe.wait_ge(merged, g * 2 + (b + 1))
                    for i, (k0, k1) in enumerate(((0, 6), (6, 12), (12, 16))):
                        ps = bank[2 + 3 * b + i]
                        for j in range(k0, k1):
                            ins = mm(ps[:, 0:T], w[:, j, b * P:(b + 1) * P], brT[:, j, :], start=j == k0, stop=j == k1 - 1)
                    ins.then_inc(br_ready, 1)

            pe.wait_ge(merged, 2 + 2 * N_GRP)

            def out_rows(b):
                ps = aux(A_O + b)
                pe.wait_ge(z_done, Z_O + b + 1)
                for t, (t0, cnt) in enumerate(TILES):
                    ins = tr(ps[0:cnt, t * P:(t + 1) * P], oT[:, b % 2, t0:t0 + cnt], ident[:, :])
                ins.then_inc(aux_ready, 1)

            for c in range(8):
                n = OUT0 + c
                pe.wait_ge(full[n % 4], dense_full(n))
                w = slot(n)
                for b in range(2):
                    k = 2 * c + b
                    ps = z(Z_O + k)
                    for j in range(KT):
                        ins = mm(ps[:, 0:T], w[:, j, b * P:(b + 1) * P], mgT[:, j, :], start=j == 0, stop=j == KT - 1)
                    ins.then_inc(z_ready, 1)
                    if k:
                        out_rows(k - 1)
            out_rows(15)

            for t, (_, n) in enumerate(TILES):
                rows_to_columns(A_RT + 4 * t, lambda j, t=t, n=n: xn2[0:n, t, j, :], n,
                                lambda t=t: pe.wait_ge(xn2_ready, t + 1))
            pe.wait_ge(aux_done, A_RT + 9)
            pe.wait_ge(wr_copied, 1)
            ps = aux(A_LG)
            for t, (t0, cnt) in enumerate(TILES):
                for j in range(KT):
                    ins = mm(ps[0:cnt, t * 36:(t + 1) * 36], xn2T[:, j, t0:t0 + cnt], wr[:, j, :], start=j == 0, stop=j == KT - 1)
            ins.then_inc(aux_ready, 1)
            pe.wait_ge(sel_ready, 4)
            pe.wait_ge(tri_ok, 3)
            ps = aux(A_POS)
            for t in range(4):
                last = min(t, 2)
                for u in range(last + 1):
                    lhs = tri if u == t else ones
                    ins = mm(ps[:, t * NX:(t + 1) * NX], lhs, self_[:, u, :], start=u == 0, stop=u == last)
            ins.then_inc(aux_ready, 1)

            pe.wait_ge(np_ready, 1)
            npass = pe.value_load(npass_i[0:1, 0:1], min_val=1, max_val=9)
            with pe.Fori(0, npass) as k:
                with pe.Fori(0, ROUNDS) as r:
                    it = k * ROUNDS + r

                    def eaux(q):
                        pe.wait_ge(aux_done, it * JPR + (A_E + q - 1))
                        return bank[6 + q % 2]

                    pe.wait_ge(p_ready, it + 1)
                    for q in range(4):
                        ps = eaux(q)
                        for jj in range(4):
                            for t, (_, cnt) in enumerate(TILES):
                                ins = mm(ps[:, jj * P:(jj + 1) * P], xn2[0:cnt, t, 4 * q + jj, :], P01f[0:cnt, t, :],
                                         start=t == 0, stop=t == 2)
                        ins.then_inc(aux_ready, 1)
                    ps = eaux(4)
                    for t, (t0, cnt) in enumerate(TILES):
                        ins = tr(ps[:, t0:t0 + cnt], Pwf[0:cnt, t, :], ident[0:cnt, 0:cnt])
                    ins.then_inc(aux_ready, 1)
                    pe.wait_ge(aux_done, it * JPR + (A_E + 4))
                    for c in range(CPR):
                        s = EORDER[c % ESLOTS]
                        if c == 16:
                            ps = eaux(5)
                            pe.wait_ge(h_ready, it + 1)
                            for j in range(4):
                                ins = tr(ps[:, j * P:(j + 1) * P], h[:, j, :], ident[:, :])
                            ins.then_inc(aux_ready, 1)
                            pe.wait_ge(aux_done, it * JPR + (A_E + 6))
                        pe.wait_ge(full[s], it * (16 * CPR // ESLOTS) + (before[s] + 16 * (c // ESLOTS + 1)))
                        w = e_slot[s].rearrange("p (e j n) -> p e j n", e=EPR, j=2)
                        for jj in range(2):
                            for e in range(EPR):
                                sl = slice(e * CAP, (e + 1) * CAP)
                                if c < 16:
                                    j = 2 * (c % 8) + jj
                                    ins = mm(bank[c // 8][sl, :], xgT[:, j, sl], w[:, e, jj, :], start=j == 0, stop=j == KT - 1)
                                else:
                                    half, j = (c - 16) // 4, (c - 16) % 4
                                    ins = mm(bank[2 + 2 * half + jj][sl, :], hT[:, j, sl], w[:, e, jj, :],
                                             start=j == 0, stop=j == 3)
                        ins.then_inc(e_used, 1)
                    for n in range(4):
                        for t, (t0, cnt) in enumerate(TILES):
                            ps = eaux(6 + 3 * n + t)
                            if t == 0:
                                pe.wait_ge(y_ready, it * 4 + (n + 1))
                            mm(ps[0:cnt, :], PwT[:, t0:t0 + cnt], y[:, n, :], start=True, stop=True).then_inc(aux_ready, 1)



_INS = ["x_prompt", "x_sample", "mem_prompt", "cache_mem_k", "cache_mem_v", "state_pool", "g_mix", "w_in", "ln_v_g",
        "ln_v_b", "w_s", "b_s", "w_pool", "pool_scale", "g_mem", "w_mkv", "w_br_a", "w_br_b", "w_br_c", "w_o", "g_ffn",
        "w_rg", "b_rg", "w_re", "b_re", "w_gate", "w_up", "w_down", "g_final"]
_OUTS = [(1, 256, 2048), (8, 1, 2048), (1, 1, 256, 4, 128), (1, 1, 256, 4, 128), (1, 1, 15, 768), (1, 8, 15, 768),
         (1, 8, 1, 768)]


def kernel(**inputs):
    import numpy as _np
    import concourse.bacc as _bacc
    from concourse.bass_utils import run_bass_kernel_spmd as _run

    nc = _bacc.Bacc("TRN2", target_bir_lowering=False, num_devices=1)
    arrays, ins, outs = {}, [], []
    for name in _INS:
        a = _np.ascontiguousarray(inputs[name])
        arrays[f"in_{name}"] = a
        ins.append(nc.dram_tensor(f"in_{name}", a.shape, mybir.dt.from_np(a.dtype), kind="ExternalInput").ap())
    for i, shape in enumerate(_OUTS):
        outs.append(nc.dram_tensor(f"out_{i}", shape, F32, kind="ExternalOutput").ap())
    branch_kernel(nc, ins, outs)
    r = _run(nc, [arrays], core_ids=[0])
    return tuple(r.results[0][f"out_{i}"] for i in range(len(_OUTS)))
```

```python
import concourse.bass as bass
from concourse import mybir
from contextlib import ExitStack

F32 = mybir.dt.float32
F32R = mybir.dt.float32r
I32 = mybir.dt.int32
ALU = mybir.AluOpType
ACT = mybir.ActivationFunctionType
AX = mybir.AxisListType

P = 128
D = 2048
KT = D // P
TP, TS = 256, 8
T = TP + TS
TILES = ((0, P), (P, P), (TP, TS))
NM = 256
NH, DH = 4, 128
GG = 6
BW = GG * P
PG = 192
WINDOWS = (2, 4, 8, 16)
NST = 15
PAD = 16
NG, NE = 4, 8
NX = NG * NE
DE = 512
EPS = 1e-6
SCALE = float(DH) ** -0.5
CAP = 32
EPR = 4
ROUNDS = NX // EPR
CHUNK = 4096
CC = CHUNK // KT
FAR = 10000.0

N_MKV, N_Z, N_GRP = 4, 11, 8
N_EARLY = N_MKV + N_Z
C_OUT = 4 * N_GRP
PIECES = 2
Z_COLS = (768, 1024, 1280, 2304, 2560, 1536, 1792, 2048, 0, 256, 512)
GATE_COL = 2816
Z_V, Z_Q, Z_P, Z_U, Z_G = 8, 14, 18, 24, 30
Z_O = Z_G + 6 * N_GRP
Z_END = Z_O + 16
ESLOTS = 6
EORDER = (4, 5, 0, 1, 3, 2)
CPR = 24
CREDIT = ESLOTS

_n = 0


def _span(count):
    global _n
    _n += count
    return _n - count


A_MEM = _span(8)
A_X = _span(9)
A_KT = _span(4)
A_WS = _span(2)
A_VN = _span(6)
A_QN = _span(1)
A_QB = _span(TS)
A_SC = [_span(1), _span(1)]
A_ST = _span(2)
A_SS = _span(1)
A_SP = _span(1)
A_HEAD = []
for _h in range(NH):
    A_HEAD.append(_span(2))
    if _h + 2 < NH:
        A_SC.append(_span(1))
A_PN = _span(2)
A_MX = _span(5)
A_PL = _span(6)
A_O, A_R = [], []
for _b in range(KT):
    A_O.append(_span(1))
    if _b:
        A_R.append(_span(1))
A_R.append(_span(1))
A_LT = _span(1)
A_POS = _span(1)
A_E = _n
AUX = 5
JPR = 18


def branch_kernel(nc, io, outs):
    (x_prompt, x_sample, mem_prompt, cache_k, cache_v, state_pool, g_mix, w_in, ln_v_g, ln_v_b,
     w_s, b_s, w_pool, pool_scale, g_mem, w_mkv, w_br_a, w_br_b, w_br_c, w_o, g_ffn, w_rg, b_rg,
     w_re, b_re, w_gate, w_up, w_down, g_final) = io
    (y_prompt, y_sample, new_k, new_v, new_st_p, new_st_s, new_gv) = outs

    ctx = ExitStack()
    with ctx:
        def sb(name, n, dt=F32):
            return ctx.enter_context(nc.sbuf_tensor(name, [P, n], dt))

        def sem(name):
            return ctx.enter_context(nc.semaphore(name))

        arena = -(-nc.sbuf_base // 32) * 32
        ring = sb("ring", 4 * CHUNK)
        x_all = sb("x_all", 3 * D)
        trunk = sb("trunk", 3 * KT * T)
        side = sb("side", 17456)
        ident = sb("ident", P)
        small = sb("small", 256)
        npass_i = sb("npass_i", 1, I32)
        bank = [ctx.enter_context(nc.psum_tensor(f"bank{i}", [P, 512], F32)) for i in range(8)]

        def view(t, at, *dims):
            n = 1
            for d in dims:
                n *= d
            v = t[:, at:at + n]
            if len(dims) == 1:
                return v
            names = "abc"[:len(dims)]
            pat = f"p ({' '.join(names)}) -> p {' '.join(names)}"
            return v.rearrange(pat, **dict(zip(names, dims)))

        x = view(x_all, 0, 3, D)
        xnT = view(trunk, 0, KT, T)
        brT = view(trunk, KT * T, KT, T)
        memT = view(trunk, KT * T, KT, NM)
        mem = view(trunk, 2 * KT * T, 2, D)
        stA = view(trunk, 2 * KT * T, 6, 272)
        stB = view(trunk, 2 * KT * T + 1632, 6, 272)
        stN = view(trunk, 2 * KT * T, 768)
        sT = view(trunk, 2 * KT * T + 3264, 2, 32)
        Ps = view(trunk, 2 * KT * T + 3328, 256)
        PsT = view(trunk, 2 * KT * T + 3584, 2, 32)
        qn = view(trunk, 2 * KT * T + 3648, 512)
        at = 0
        xs = view(side, 0, 2, D)
        vN = view(side, 0, 3, BW)
        vT = view(side, 3 * BW, GG, T)
        diff = view(side, 3 * BW, GG, T)
        sg = side[:, 0:2 * 3 * T].rearrange(
            "p (b i t) -> p b i t", b=2, i=3)
        gp = view(side, 2 * 3 * T, 4, T)
        oT = view(side, 2 * 3 * T + 4 * T, 2, T)
        hgT = view(side, 2 * 3 * T + 6 * T, 2, T)
        lgT = view(side, 2 * 3 * T + 8 * T, T)
        at = 4096
        kvK = view(side, at, 2, 512)
        kvV = view(side, at + 1024, 2, 512)
        Pp = [[view(side, at + b * 512 + t * NM, NM) for t in range(2)] for b in range(2)]
        at += 2048
        kT = view(side, at, NH, NM)
        at += NH * NM
        qT = view(side, at, NH, T)
        at += NH * T
        pT = view(side, at, GG, PAD + T)
        at += GG * (PAD + T)
        wp = view(side, at, GG, PG)
        at += GG * PG
        wsT = view(side, at, GG, P)
        at += GG * P
        bs = view(side, at, GG, P)
        at += GG * P
        lng, lnb = view(side, at, BW), view(side, at + BW, BW)
        cache_flat = [view(side, at + 1024 * b, 1024) for b in range(2)]
        cache = [view(side, at + 1024 * b, 2, 512) for b in range(2)]
        at += 2048
        prod = view(side, at, 2, 512)
        prod_flat = view(side, at, 1024)
        wsN = view(side, at, GG, P)
        mixt = view(side, at, 4, P)
        at += 1024
        PpT_flat = [view(side, at + b * 512, 512) for b in range(2)]
        PpT = [[view(side, at + b * 512 + m * NM, NM) for m in range(2)] for b in range(2)]
        pn = view(side, at, BW)
        at += 1024
        ext = side[:, at:at + 768].rearrange("p (k b t) -> p k b t", k=GG, b=TS)
        at += 768
        assert at <= 17456, at

        def split_part(name, at, n):
            return nc.alloc_sbuf_tensor_at(name, [P, n], F32R, offset=arena + 4 * at)

        TRUNK0 = 4 * CHUNK + 3 * D
        SIDE0 = TRUNK0 + 3 * KT * T
        w_hi = [split_part(f"w_hi{b}", (3 - b) * CHUNK, KT * P).rearrange("p (j c) -> p j c", j=KT) for b in range(2)]
        w_lo = [split_part(f"w_lo{b}", (3 - b) * CHUNK + KT * P, KT * P).rearrange("p (j c) -> p j c", j=KT)
                for b in range(2)]
        mg_hi_f = split_part("mg_hi", TRUNK0, KT * T)
        mg_lo_f = split_part("mg_lo", TRUNK0 + KT * T, KT * T)
        three = [mg_hi_f, mg_lo_f, split_part("xn_hi", TRUNK0 + 2 * KT * T, KT * T),
                 split_part("br_hi", SIDE0 + 4096, KT * T), split_part("br_lo", SIDE0 + 4096 + KT * T, KT * T),
                 split_part("xn_lo", SIDE0 + 4096 + 2 * KT * T, KT * T)]
        mg_hi, mg_lo, xn_hi, br_hi, br_lo, xn_lo = [v.rearrange("p (j t) -> p j t", j=KT) for v in three]
        e_slot = {0: view(ring, 0, CHUNK), 1: view(ring, CHUNK, CHUNK), 2: view(ring, 2 * CHUNK, CHUNK),
                  3: view(ring, 3 * CHUNK, CHUNK), 4: view(side, 4096, CHUNK), 5: view(side, 8192, CHUNK)}
        y = view(side, 0, 4, 512)
        hs = view(side, 2048, 512)
        h = view(side, 2560, 4, P)
        hT = view(side, 3072, 4, P)
        PwT = view(side, 3584, T)
        at = 12288
        gfin = view(side, at, D)
        at += D
        P01 = side[:, at:at + 384].rearrange("p (t e c) -> p t e c", t=3, e=EPR)
        P01f = view(side, at, 3, P)
        at += 384
        Pw = side[:, at:at + 384].rearrange("p (t e c) -> p t e c", t=3, e=EPR)
        Pwf = view(side, at, 3, P)
        at += 384
        tri = view(side, at, P)
        ones = view(side, at + P, P)
        at += 2 * P
        lg = view(side, at, 3, 36)
        at += 108
        combx = view(side, at, 3, NX + EPR)
        comb = combx[:, :, 0:NX].rearrange("p t (g e) -> p t g e", g=NG)
        at += 108
        sel = side[:, at:at + 96].rearrange("p (t g e) -> p t g e", t=3, g=NG)
        self_ = view(side, at, 3, NX)
        at += 96
        pos = view(side, at, 3, NX + EPR)
        at += 108
        t32 = side[:, at:at + 96].rearrange("p (t g e) -> p t g e", t=3, g=NG)
        at += 96
        r4 = [view(side, at + 12 * i, 3, NG) for i in range(3)]
        at += 36
        r8 = [view(side, at + 24 * i, 3, NE) for i in range(5)]
        at += 120
        r1 = [view(side, at + 3 * i, 3) for i in range(12)]
        at += 36
        cidx = view(side, at, CAP)
        at += CAP
        rev = view(side, at, NE)
        at += NE
        thr = view(side, at, 9)
        at += 9
        thr2 = view(side, at, 9)
        at += 9
        npf = view(side, at, 2)
        at += 2
        assert at <= 4096 + 3 * KT * T
        at = 4096 + 3 * KT * T
        wr = view(side, at, KT, 36)
        at += 576
        lgb = view(side, at, 36)
        at += 36
        assert at <= 17456, at
        xn2 = trunk[:, 0:3 * D].rearrange("p (t j c) -> p t j c", t=3, j=KT)
        xgT = view(trunk, 3 * D, KT, P)
        ys = view(trunk, 0, D)
        sq_out = view(trunk, 3 * D + KT * P, 512)

        gmixc, gmemc, gffnc = view(small, 0, KT), view(small, 16, KT), view(small, 32, KT)
        pscale = view(small, 48, GG)
        w00 = view(small, 54, GG)
        gffnr = view(small, 228, KT)
        ssm, ssx, ssh = view(small, 60, 2), view(small, 62, 3), view(small, 65, 3)
        ssh4 = view(small, 244, 3, 4)
        rm, rx, rh = view(small, 68, 2), view(small, 70, 3), view(small, 73, 3)
        mx = view(small, 76, 2)
        negm = view(small, 78, 2)
        rs = view(small, 80, 2)
        lmu, lvar = view(small, 82, 3), view(small, 85, 3)
        dg = view(small, 88, GG, TS)
        rc = view(small, 136, 4, 16)
        wsum = view(small, 200, TS)
        tmp16 = view(small, 208, 16)
        smx, snegm, srs = view(small, 224, 1), view(small, 225, 1), view(small, 226, 1)

        full = [sem(f"slot{i}_full") for i in range(6)]
        mem_in, x_in = [sem("mem0_in"), sem("mem1_in")], sem("x_in")
        gcol_in, const_in, ln_in, pool_in = sem("gcol_in"), sem("const_in"), sem("ln_in"), sem("pool_w_in")
        state_in, router_in, gfin_in = sem("state_in"), sem("router_in"), sem("gfin_in")
        cache_in = [sem("cache0_in"), sem("cache1_in")]
        kv_out, gv_out, st_out, y_out = sem("kv_out"), sem("gv_out"), sem("st_out"), sem("y_out")
        z_ready, z_done = sem("z_ready"), sem("z_done")
        aux_ready, aux_done = sem("aux_ready"), sem("aux_done")
        br_ready, merged = sem("br_ready"), sem("merged")
        id_ok, pool_chain, rc_ok = sem("id_ok"), sem("pool_chain"), sem("rc_ok")
        act_chain, dve_chain = sem("act_chain"), sem("dve_chain")
        mem_ss, mem_sqrt, x_ss, x_sqrt = sem("mem_ss"), sem("mem_sqrt"), sem("x_ss"), sem("x_sqrt")
        mem_var, x_var, ln_var, ln_sqrt = sem("mem_var"), sem("x_var"), sem("ln_var"), sem("ln_sqrt")
        xs_ready, ss_zero = sem("xs_ready"), sem("ss_zero")
        ln_done, negm_ready, exp_done = sem("ln_done"), sem("negm_ready"), sem("exp_done")
        ck_used, cv_used = sem("ck_used"), sem("cv_used")
        diff_ready, pad_ok = sem("diff_ready"), sem("pad_ok")
        s_ready, dg_ready = sem("s_ready"), sem("dg_ready")
        merge_step = sem("merge_step")
        h_done, h_var, h_sqrt, xn2_ready = sem("h_done"), sem("h_var"), sem("h_sqrt"), sem("xn2_ready")
        sv_ready, sv_done, lg_ready = sem("sv_ready"), sem("sv_done"), sem("lg_ready")
        hi_done, lo_done, xh_done, xn_split, br_split = (
            sem("hi_done"), sem("lo_done"), sem("xh_done"), sem("xn_split"), sem("br_split"))
        sp_step, gffnr_in, xn_copied = sem("sp_step"), sem("gffnr_in"), sem("xn_copied")
        lg_exp_in, lg_exp = sem("lg_exp_in"), sem("lg_exp")
        tri_ok, sel_ready, np_ready = sem("tri_ok"), sem("sel_ready"), sem("np_ready")
        e_used, p_ready, p_step, silu_done, h_ready, y_ready = (
            sem("e_used"), sem("p_ready"), sem("p_step"), sem("silu_done"), sem("h_ready"), sem("y_ready"))
        sq_done, f_var, f_sqrt, f_rms = sem("sq_done"), sem("f_var"), sem("f_sqrt"), sem("f_rms")
        y_final, ys_scaled, ys_final = sem("y_final"), sem("ys_scaled"), sem("ys_final")

        def early_full(n):
            return 16 * (n // 4 + 1)

        def raw_full(c, g=0):
            base = early_full(N_EARLY - 3 + c % 2)
            if c < 4:
                return g * (64 if c % 2 else 32) + (base + (16, 16, 32, 64)[c])
            k = c - C_OUT
            return base + N_GRP * (64 if c % 2 else 32) + 16 * (k // 2 + 1)

        before = {0: raw_full(C_OUT + 6), 1: raw_full(C_OUT + 7), 2: early_full(N_EARLY - 1), 3: early_full(N_EARLY - 4),
                  4: 0, 5: 0}

        win_v = w_in[0].rearrange("(p j) c -> p j c", j=KT)
        wmkv_v = w_mkv[0].rearrange("(p j) c -> p j c", j=KT)
        wo_v = w_o[0].rearrange("(j p) c -> p j c", p=P)
        bra_v = w_br_a[0].rearrange("(j p) c -> p j c", p=P)
        brb_v = w_br_b[0].rearrange("(j p) c -> p j c", p=P)
        brc_v = w_br_c[0].rearrange("(j p) c -> p j c", p=P)
        wg_v = w_gate[0].rearrange("g e (p j) f -> p (g e) (j f)", j=KT)
        wu_v = w_up[0].rearrange("g e (p j) f -> p (g e) (j f)", j=KT)
        wd_v = w_down[0].rearrange("g e (p j) n -> p (g e) (j n)", j=4)

        def slot(n):
            return view(ring, (n % 4) * CHUNK, KT, CC)

        def slot_half(c, b):
            return slot(c % 2)[:, :, b * P:(b + 1) * P]

        def gate_load(sp, g, i):
            src = win_v[:, :, bass.ds(g * CC + (GATE_COL + i * D), CC)]
            sp.dma_start(slot(i % 2), src).then_inc(full[i % 2], 16)

        def branch_load(sp, cols):
            sp.dma_start(slot(1)[:, 0:6, :], bra_v[:, :, cols]).then_inc(full[1], 16)
            sp.dma_start(slot(1)[:, 6:12, :], brb_v[:, :, cols]).then_inc(full[1], 16)
            sp.dma_start(slot(1)[:, 12:16, :], brc_v[:, :, cols]).then_inc(full[1], 16)

        block = ctx.enter_context(nc.Block())

        @block.sync
        def _(sp):
            for t in range(2):
                sp.dma_start(mem[:, t, :], mem_prompt[0, t * P:(t + 1) * P, :]).then_inc(mem_in[t], 16)
            sp.dma_start(slot(0), wmkv_v[:, :, 0:CC]).then_inc(full[0], 16)
            sp.dma_start(x[:, 0, :], x_prompt[0, 0:P, :]).then_inc(x_in, 16)
            sp.dma_start(x[:, 1, :], x_prompt[0, P:TP, :]).then_inc(x_in, 16)
            sp.dma_start(x[0:TS, 2, :], x_sample[:, 0, :]).then_inc(x_in, 16)
            for n in range(1, N_EARLY):
                if n >= 4:
                    sp.wait_ge(z_ready, 2 * (n - 3))
                src = wmkv_v[:, :, n * CC:(n + 1) * CC] if n < N_MKV else \
                    win_v[:, :, Z_COLS[n - N_MKV]:Z_COLS[n - N_MKV] + CC]
                sp.dma_start(slot(n), src).then_inc(full[n % 4], 16)
            for i in range(2):
                sp.wait_ge(z_ready, 2 * (N_EARLY - 3 + i + 1))
                gate_load(sp, 0, i)
            with sp.Fori(0, N_GRP - 1) as g:
                for c in range(2, 6):
                    sp.wait_ge(lo_done, g * (8 * PIECES) + 2 * PIECES * (c - 1))
                    if c == 3:
                        sp.sem_inc(sp_step, 1)
                        branch_load(sp, bass.ds(g * CC, CC))
                    else:
                        gate_load(sp, g + c // 4, c % 4)
            for c in range(C_OUT - 2, C_OUT + 8):
                sp.wait_ge(lo_done, 2 * PIECES * (c - 1))
                if c < C_OUT - 1:
                    gate_load(sp, N_GRP - 1, 2)
                elif c < C_OUT:
                    branch_load(sp, slice(D - CC, D))
                else:
                    k = c - C_OUT
                    sp.dma_start(slot(c % 2), wo_v[:, :, k * CC:(k + 1) * CC]).then_inc(full[c % 2], 16)

            def expert_load(c, e0):
                if c < 16:
                    src = (wg_v if c < 8 else wu_v)[:, e0, (c % 8) * 1024:(c % 8 + 1) * 1024]
                else:
                    half, j = (c - 16) // 4, (c - 16) % 4
                    src = wd_v[:, e0, j * D + half * 1024:j * D + (half + 1) * 1024]
                s = EORDER[c % ESLOTS]
                sp.dma_start(e_slot[s].rearrange("p (e n) -> p e n", e=EPR), src).then_inc(full[s], 16)

            for c, (signal, count) in enumerate(((br_ready, 2 * N_GRP), (br_ready, 2 * N_GRP),
                                                 (lo_done, 2 * PIECES * (C_OUT + 7)), (lo_done, 2 * PIECES * (C_OUT + 8)),
                                                 (z_ready, Z_END - 1), (z_ready, Z_END))):
                sp.wait_ge(signal, count)
                expert_load(c, slice(0, EPR))
            sp.wait_ge(np_ready, 1)
            npass = sp.value_load(npass_i[0:1, 0:1], min_val=1, max_val=9)
            with sp.Fori(0, npass) as k:
                with sp.Fori(2, ROUNDS + 1) as r:
                    for c in range(ESLOTS, CPR + ESLOTS):
                        sp.wait_ge(e_used, k * (ROUNDS * CPR) + r * CPR + (c + 1 - 2 * CPR))
                        if c in (8, 16):
                            sp.sem_inc(sp_step, 1)
                        expert_load(c % CPR, bass.ds(r * EPR + EPR * (c // CPR - 2), EPR))
                for c in range(ESLOTS, CPR):
                    sp.wait_ge(e_used, k * (ROUNDS * CPR) + ((ROUNDS - 1) * CPR + c + 1))
                    expert_load(c, slice(NX - EPR, NX))
                with sp.If(k < npass - 1):
                    for c in range(ESLOTS):
                        sp.wait_ge(e_used, k * (ROUNDS * CPR) + (ROUNDS * CPR + c + 1))
                        expert_load(c, slice(0, EPR))
                sp.nop()
            for i in range(4):
                t, cols = i // 2, slice(i % 2 * 1024, (i % 2 + 1) * 1024)
                sp.wait_ge(y_final, i + 1)
                sp.dma_start(y_prompt[0, t * P:(t + 1) * P, cols], x[:, t, cols]).then_inc(y_out, 16)
            sp.wait_ge(ys_final, 1)
            sp.dma_start(y_sample[:, 0, :], ys[0:TS, :]).then_inc(y_out, 16)
            sp.wait_ge(y_out, 80)

        @block.gpsimd
        def _(pool):
            nc.gpsimd.memset(ident[:, :], 0.0).then_inc(pool_chain, 1)
            pool.wait_ge(pool_chain, 1)
            nc.gpsimd.affine_select(out=ident[:, :], in_=ident[:, :], compare_op=ALU.not_equal, fill=1.0, base=0,
                                    pattern=[[-1, P]], channel_multiplier=1).then_inc(id_ok, 1)
            for t in range(2):
                pool.wait_ge(mem_in[t], 16)
            row = lambda a, n: a.rearrange("(o n) -> o n", o=1).to_broadcast([n, a.shape[0]])
            pool.dma_start(wsN, w_s[0].rearrange("g i j -> i g j")).then_inc(const_in, 16)
            pool.dma_start(bs, b_s[0].rearrange("(o g) i -> o g i", o=1).to_broadcast([P, GG, P])).then_inc(const_in, 16)
            with nc.allow_non_contiguous_dma(reason="a few hundred words of per-channel constants"):
                pool.dma_start(pscale, pool_scale[0].rearrange("(k p) -> p k", p=P)).then_inc(const_in, 16)
                pool.dma_start(w00[0:TS, :], w_s[0, :, 0, 0:1].rearrange("(o g) a -> o (g a)", o=1)
                               .to_broadcast([TS, GG])).then_inc(const_in, 16)
            pool.dma_start(lng, row(ln_v_g[0], P)).then_inc(ln_in, 16)
            pool.dma_start(lnb, row(ln_v_b[0], P)).then_inc(ln_in, 16)
            for g in range(4):
                b0 = 3 * (g // 2)
                if g % 2 == 0:
                    pool.dma_start(wp[:, b0, :], w_pool[0, g, 0:P, :]).then_inc(pool_in, 16)
                    pool.dma_start(wp[0:64, b0 + 1, :], w_pool[0, g, P:PG, :]).then_inc(pool_in, 16)
                else:
                    pool.dma_start(wp[64:P, b0 + 1, :], w_pool[0, g, 0:64, :]).then_inc(pool_in, 16)
                    pool.dma_start(wp[:, b0 + 2, :], w_pool[0, g, 64:PG, :]).then_inc(pool_in, 16)
            nc.gpsimd.iota(rc, pattern=[[0, 4], [1, 16]], base=1, channel_multiplier=0,
                           allow_small_or_imprecise_dtypes=True).then_inc(rc_ok, 1)
            pool.wait_ge(const_in, 64)
            nc.gpsimd.affine_select(out=wsN, in_=wsN, compare_op=ALU.is_ge, fill=0.0, base=0,
                                    pattern=[[0, GG], [-1, P]], channel_multiplier=1).then_inc(pool_chain, 1)
            pool.dma_start(new_st_s[0, :, 0:NST - 1, :], state_pool[0, :, 1:NST, :]).then_inc(st_out, 16)
            with nc.allow_non_contiguous_dma(reason="2048 gains"):
                pool.dma_start(gffnr, g_ffn[0].rearrange("(j p) -> p j", p=P)).then_inc(gffnr_in, 16)
            pool.wait_ge(aux_ready, A_MEM + 8)
            pool.dma_start(stN[0:TS * NST, :], state_pool[0].rearrange("b t c -> (b t) c")).then_inc(state_in, 16)
            pool.wait_ge(z_done, Z_V)
            for t in range(2):
                pool.dma_start(new_k[0, 0, t * P:(t + 1) * P].rearrange("m h d -> m (h d)"), kvK[:, t, :]).then_inc(kv_out, 16)
                pool.dma_start(new_v[0, 0, t * P:(t + 1) * P].rearrange("m h d -> m (h d)"), kvV[:, t, :]).then_inc(kv_out, 16)
            pool.wait_ge(ln_done, 1)
            pool.dma_start(new_gv[0, :, 0, :], vN[0:TS, 2, :]).then_inc(gv_out, 16)
            for i in range(2 * TS):
                if 2 <= i < TS + 2:
                    pool.wait_ge(ck_used, i - 1)
                elif i >= TS + 2:
                    pool.wait_ge(cv_used, i - TS - 1)
                src = (cache_k if i < TS else cache_v)[0, i % TS].rearrange("(p m) h d -> p m (h d)", m=2)
                pool.dma_start(cache_flat[i % 2], src).then_inc(cache_in[i % 2], 16)
            pool.wait_ge(aux_done, A_PN + 2)
            pool.dma_start(new_st_p[0, 0], pn[0:NST, :]).then_inc(st_out, 16)
            pool.dma_start(new_st_s[0, :, NST - 1, :], pn[NST:NST + TS, :]).then_inc(st_out, 16)
            pool.wait_ge(st_out, 48)
            pool.wait_ge(kv_out, 64)
            pool.wait_ge(gv_out, 16)
            pool.wait_ge(aux_done, A_PL + 6)
            pool.wait_ge(sv_ready, 1)
            with nc.allow_non_contiguous_dma(reason="router weights, d = (j p)"):
                pool.dma_start(wr[:, :, 0:NG], w_rg[0].rearrange("(j p) g -> p j g", p=P)).then_inc(router_in, 16)
                for g in range(NG):
                    pool.dma_start(wr[:, :, NG + g * NE:NG + (g + 1) * NE],
                                   w_re[0, g].rearrange("(j p) e -> p j e", p=P)).then_inc(router_in, 16)
            pool.dma_start(lgb[:, 0:NG], row(b_rg[0], P)).then_inc(router_in, 16)
            pool.dma_start(lgb[:, NG:36], row(b_re[0].rearrange("g e -> (g e)"), P)).then_inc(router_in, 16)
            pool.wait_ge(sv_done, 1)
            nc.gpsimd.tensor_copy(br_hi, brT).then_inc(br_split, 1)
            pool.wait_ge(br_split, 1)
            nc.gpsimd.tensor_tensor(br_lo, brT, br_hi, ALU.subtract).then_inc(br_split, 1)
            pool.wait_ge(br_ready, 2 * N_GRP)
            nc.gpsimd.memset(comb, 0.0).then_inc(tri_ok, 1)
            nc.gpsimd.memset(sel, 0.0).then_inc(tri_ok, 1)
            nc.gpsimd.memset(lg, 0.0).then_inc(tri_ok, 1)
            pool.dma_start(gfin, row(g_final, P)).then_inc(gfin_in, 16)
            nc.gpsimd.iota(cidx, pattern=[[1, CAP]], base=0, channel_multiplier=0,
                           allow_small_or_imprecise_dtypes=True).then_inc(tri_ok, 1)
            nc.gpsimd.iota(rev, pattern=[[-1, NE]], base=NE, channel_multiplier=0,
                           allow_small_or_imprecise_dtypes=True).then_inc(tri_ok, 1)
            nc.gpsimd.iota(thr, pattern=[[CAP, 9]], base=0, channel_multiplier=0,
                           allow_small_or_imprecise_dtypes=True).then_inc(tri_ok, 1)
            nc.gpsimd.memset(ones, 1.0).then_inc(pool_chain, 1)
            pool.wait_ge(pool_chain, 3)
            nc.gpsimd.affine_select(out=tri, in_=ones, compare_op=ALU.is_gt, fill=0.0, base=0,
                                    pattern=[[1, P]], channel_multiplier=-1).then_inc(tri_ok, 1)
            pool.wait_ge(ys_scaled, 1)
            pool.wait_ge(gfin_in, 16)
            nc.gpsimd.tensor_tensor(ys[0:TS, :], ys[0:TS, :], gfin[0:TS, :], ALU.mult).then_inc(ys_final, 1)

        @block.scalar
        def _(act):
            with nc.allow_non_contiguous_dma(reason="per-channel gains, 64 bytes a partition"):
                act.dma_start(gmemc, g_mem[0].rearrange("(p j) -> p j", j=KT)).then_inc(gcol_in, 16)
                act.dma_start(gmixc, g_mix[0].rearrange("(p j) -> p j", j=KT)).then_inc(gcol_in, 16)
                act.dma_start(gffnc, g_ffn[0].rearrange("(p j) -> p j", j=KT)).then_inc(gcol_in, 16)
            chain = [0]

            def link(ins):
                chain[0] += 1
                ins.then_inc(act_chain, 1)
                act.wait_ge(act_chain, chain[0])

            act.wait_ge(ss_zero, 2)
            for t in range(2):
                act.wait_ge(mem_in[t], 16)
                link(nc.scalar.activation(trunk[:, 0:D], mem[:, t, :], ACT.Square, accum_out=ssm[:, t:t + 1]))
                act.wait_ge(mem_var, t + 1)
                nc.scalar.activation(rm[:, t:t + 1], ssm[:, t:t + 1], ACT.Sqrt).then_inc(mem_sqrt, 1)
            act.wait_ge(x_in, 48)
            for t, (_, n) in enumerate(TILES):
                link(nc.scalar.activation(trunk[0:n, 0:D], x[0:n, t, :], ACT.Square, accum_out=ssx[0:n, t:t + 1]))
            act.wait_ge(x_var, 1)
            nc.scalar.activation(rx, ssx, ACT.Sqrt).then_inc(x_sqrt, 1)

            def take_z(n):
                act.wait_ge(z_ready, n + 1)
                return bank[n % 2]

            for n in range(Z_V):
                ps, c, t = take_z(n), n // 2, n % 2
                dst = (kvK if c < 2 else kvV)[:, t, (c % 2) * CC:(c % 2 + 1) * CC]
                nc.scalar.activation(dst, ps[:, 0:CC], ACT.Copy).then_inc(z_done, 1)
            for n in range(Z_V, Z_Q):
                nc.scalar.activation(vT[:, n - Z_V, :], take_z(n)[:, 0:T], ACT.Gelu).then_inc(z_done, 1)
            for n in range(Z_Q, Z_P):
                nc.scalar.activation(qT[:, n - Z_Q, :], take_z(n)[:, 0:T], ACT.Copy).then_inc(z_done, 1)
            act.wait_ge(ln_var, 1)
            nc.scalar.activation(lvar, lvar, ACT.Sqrt).then_inc(ln_sqrt, 1)
            for n in range(Z_P, Z_U):
                nc.scalar.activation(pT[:, n - Z_P, PAD:PAD + T], take_z(n)[:, 0:T], ACT.Copy).then_inc(z_done, 1)

            def quarter_squares(q):
                act.wait_ge(h_done, q + 1)
                for t, (_, n) in enumerate(TILES):
                    link(nc.scalar.activation(view(trunk, 2 * KT * T, 512)[0:n], x[0:n, t, 512 * q:512 * (q + 1)], ACT.Square,
                                              accum_out=ssh4[0:n, t, q:q + 1]))

            def exp_head(hd):
                act.wait_ge(negm_ready, hd + 1 + (hd > 1))
                if hd == 0:
                    act.wait_ge(kv_out, 64)
                ps = bank[2 + A_SC[hd] % AUX]
                for t in range(2):
                    ins = nc.scalar.activation(Pp[hd % 2][t],
                                               ps[:, t * NM:(t + 1) * NM], ACT.Exp, bias=negm[:, t:t + 1],
                                               scale=SCALE, accum_out=rs[:, t:t + 1])
                    if t == 0:
                        link(ins)
                ins.then_inc(exp_done, 1)

            def split_hi(b, full_at, free=None):
                act.wait_ge(full[full_at[0]], full_at[1])
                if free:
                    act.wait_ge(*free)
                for p in range(PIECES):
                    js = slice(p * KT // PIECES, (p + 1) * KT // PIECES)
                    nc.scalar.activation(w_hi[b][:, js, :], slot_half(full_at[0], b)[:, js, :], ACT.Copy).then_inc(hi_done, 1)

            def take_u(n):
                nc.scalar.activation(brT[:, n - Z_U, :], take_z(n)[:, 0:T], ACT.Gelu).then_inc(z_done, 1)

            exp_head(0)
            exp_head(1)
            act.wait_ge(negm_ready, 3)
            nc.scalar.activation(Ps[0:32, :], bank[2 + A_SS % AUX][0:32, 0:256], ACT.Exp, bias=snegm[0:32],
                                 scale=SCALE, accum_out=srs[0:32]).then_inc(exp_done, 1)
            take_u(Z_U)
            take_u(Z_U + 1)
            exp_head(2)
            exp_head(3)
            for n in range(Z_U + 2, Z_G):
                if n == Z_G - 2:
                    split_hi(0, (0, raw_full(0)))
                take_u(n)
            split_hi(1, (0, raw_full(0)))
            act.wait_ge(sv_ready, 1)
            act.wait_ge(diff_ready, 1)
            for q in range(4):
                nc.scalar.activation(xn_hi[:, 4 * q:4 * q + 4, :], xnT[:, 4 * q:4 * q + 4, :], ACT.Copy).then_inc(xh_done, 1)
            with act.Fori(0, N_GRP) as g:
                for u in range(8):
                    c = u // 2 + 1
                    used = (z_ready, g * 6 + (Z_G + u + 1)) if u < 6 else (br_ready, g * 2 + (u - 5))
                    split_hi(u % 2, (c % 2, raw_full(c, g) if c < 4 else raw_full(0, g + 1)), used)
                    if u < 2:
                        act.wait_ge(merged, g * 2 + (u + 1))
                    if u < 6:
                        nc.scalar.activation(sg[:, u % 2, u // 2, :], bank[u % 2][:, 0:T], ACT.Sigmoid).then_inc(z_done, 1)
            act.wait_ge(merged, 2 + 2 * N_GRP)
            for n in range(Z_O, Z_END):
                ps = take_z(n)
                b = n - Z_O
                if b < 14:
                    c = C_OUT + b // 2 + 1
                    split_hi(b % 2, (c % 2, raw_full(c)))
                if b >= 2:
                    act.wait_ge(aux_ready, A_O[b - 2] + 1)
                nc.scalar.activation(oT[:, b % 2, :], ps[:, 0:T], ACT.Copy).then_inc(z_done, 1)
                if b % 4 == 1 and b > 4:
                    quarter_squares(b // 4 - 1)
            quarter_squares(3)
            act.wait_ge(h_var, 1)
            nc.scalar.activation(rh, ssh, ACT.Sqrt).then_inc(h_sqrt, 1)
            act.wait_ge(lg_exp_in, 1)
            nc.scalar.activation(r4[0], r4[0], ACT.Exp).then_inc(lg_exp, 1)
            act.wait_ge(lg_exp_in, 2)
            nc.scalar.activation(r1[5], r1[5], ACT.Exp).then_inc(lg_exp, 1)
            act.wait_ge(xn2_ready, 1)
            for t, (_, n) in enumerate(TILES):
                nc.scalar.activation(xn2[0:n, t].rearrange("p j c -> p c j"), x[0:n, t, :].rearrange("p (c j) -> p c j", j=KT),
                                     ACT.Copy, scale=rh[0:n, t:t + 1]).then_inc(xn_copied, 1)
            act.wait_ge(np_ready, 1)
            npass = act.value_load(npass_i[0:1, 0:1], min_val=1, max_val=9)
            with act.Fori(0, npass) as k:
                with act.Fori(0, ROUNDS) as r:
                    it = k * ROUNDS + r
                    act.wait_ge(e_used, it * CPR + (CREDIT + 8))
                    nc.scalar.activation(hs, bank[0][:, :], ACT.Silu).then_inc(silu_done, 1)
                    for half in range(2):
                        act.wait_ge(e_used, it * CPR + (CREDIT + 20 + 4 * half))
                        for n in (2 * half, 2 * half + 1):
                            nc.scalar.activation(y[:, n, :], bank[2 + n][:, :], ACT.Copy).then_inc(y_ready, 1)
                        for n in (2 * half, 2 * half + 1):
                            for t, (_, cnt) in enumerate(TILES):
                                q = 3 * n + t
                                act.wait_ge(aux_done, it * JPR + (A_E + 7 + q))
                                act.wait_ge(sq_done, it * 12 + (q + 1))
                                nc.scalar.activation(sq_out[0:cnt, :], x[0:cnt, t, n * 512:(n + 1) * 512], ACT.Square,
                                                     accum_out=ssh4[0:cnt, t, n:n + 1]).then_inc(sq_done, 1)
            act.wait_ge(f_var, 1)
            nc.scalar.activation(rx, ssx, ACT.Sqrt).then_inc(f_sqrt, 1)
            act.wait_ge(f_rms, 1)
            nc.scalar.activation(ys[0:TS, :], x[0:TS, 2, :], ACT.Copy, scale=rx[0:TS, 2:3]).then_inc(ys_scaled, 1)

        @block.vector
        def _(dve):
            chain = [0]

            def link(ins):
                chain[0] += 1
                ins.then_inc(dve_chain, 1)
                dve.wait_ge(dve_chain, chain[0])

            def take(job):
                dve.wait_ge(aux_ready, job + 1)
                return bank[2 + job % AUX]

            V = nc.vector
            nc.vector.memset(small[:, 60:68], 1.0).then_inc(ss_zero, 1)
            V.memset(pT[:, :, 0:PAD], 0.0).then_inc(pad_ok, 1)
            V.memset(ssh4, 1.0).then_inc(ss_zero, 1)
            V.memset(rs, 1.0).then_inc(sq_done, 1)
            V.memset(rx, 1.0).then_inc(merged, 2)
            V.memset(rm, 1.0).then_inc(e_used, CREDIT)

            def mean_eps(ss, n, done):
                V.tensor_scalar(ss, ss, 1.0 / n, EPS, ALU.mult, ALU.add).then_inc(done, 1)

            for t in range(2):
                dve.wait_ge(act_chain, t + 1)
                mean_eps(ssm[:, t:t + 1], D, mem_var)
                dve.wait_ge(mem_sqrt, t + 1)
                link(V.reciprocal(rm[:, t:t + 1], rm[:, t:t + 1]))
                V.tensor_scalar(xs[:, t, :], mem[:, t, :], rm[:, t:t + 1], None, ALU.mult).then_inc(xs_ready, 1)

            def take_t4(job, dst, gain, q, t0):
                ps = take(job)
                V.tensor_tensor(dst[:, 4 * q:4 * q + 4, t0:t0 + P], ps[:, :].rearrange("p (j t) -> p j t", j=4),
                                gain[:, 4 * q:4 * q + 4].unsqueeze(2).to_broadcast([P, 4, P]), ALU.mult).then_inc(aux_done, 1)

            dve.wait_ge(gcol_in, 48)
            for q in range(4):
                take_t4(A_MEM + q, memT, gmemc, q, 0)
            dve.wait_ge(act_chain, 5)
            mean_eps(ssx, D, x_var)
            dve.wait_ge(x_sqrt, 1)
            link(V.reciprocal(rx, rx))
            V.tensor_scalar(xs[:, 0, :], x[:, 0, :], rx[:, 0:1], None, ALU.mult).then_inc(xs_ready, 1)
            for q in range(4):
                take_t4(A_MEM + 4 + q, memT, gmemc, q, P)
            V.tensor_scalar(xs[:, 1, :], x[:, 1, :], rx[:, 1:2], None, ALU.mult).then_inc(xs_ready, 1)
            for q in range(4):
                take_t4(A_X + q, xnT, gmixc, q, 0)
            V.tensor_scalar(xs[0:TS, 0, :], x[0:TS, 2, :], rx[0:TS, 2:3], None, ALU.mult).then_inc(xs_ready, 1)
            for q in range(4):
                take_t4(A_X + 4 + q, xnT, gmixc, q, P)
            ps = take(A_X + 8)
            V.tensor_tensor(xnT[:, :, TP:T], ps[:, 0:P].rearrange("p (j t) -> p j t", j=KT),
                            gmixc.unsqueeze(2).to_broadcast([P, KT, TS]), ALU.mult).then_inc(aux_done, 1)
            for hd in range(NH):
                ps = take(A_KT + hd)
                V.tensor_copy(kT[:, hd, :], ps[:, 0:NM]).then_inc(aux_done, 1)
            dve.wait_ge(const_in, 64)
            dve.wait_ge(id_ok, 1)
            V.tensor_tensor(dg[0:TS], ident[0:TS, 0:TS].unsqueeze(1).to_broadcast([TS, GG, TS]),
                            w00[0:TS, :].unsqueeze(2).to_broadcast([TS, GG, TS]), ALU.mult).then_inc(dg_ready, 1)
            for i in range(2):
                ps, n = take(A_WS + i), 4 - 2 * i
                V.tensor_copy(wsT[:, 4 * i:4 * i + n, :].rearrange("p g i -> p (g i)"), ps[:, 0:n * P]).then_inc(aux_done, 1)
            for t, (_, n) in enumerate(TILES):
                for i in range(2):
                    ps, w = take(A_VN + 2 * t + i), 512 - 256 * i
                    V.tensor_copy(vN[0:n, t, 512 * i:512 * i + w], ps[0:n, 0:w]).then_inc(aux_done, 1)
            ps = take(A_QN)
            V.tensor_copy(qn[0:TS, :], ps[0:TS, 0:512]).then_inc(aux_done, 1)
            link(V.memset(small[:, 82:88], 1.0))
            dve.wait_ge(aux_done, A_VN + 6)
            dve.wait_ge(ln_in, 32)
            dve.wait_ge(aux_ready, A_WS + 2)
            for t, (_, n) in enumerate(TILES):
                v = vN[0:n, t, :]
                link(V.tensor_reduce(lmu[0:n, t:t + 1], v, AX.X, ALU.add))
                link(V.tensor_scalar(lmu[0:n, t:t + 1], lmu[0:n, t:t + 1], -1.0 / BW, None, ALU.mult))
                link(V.tensor_scalar(v, v, lmu[0:n, t:t + 1], None, ALU.add))
                ins = V.tensor_tensor_reduce(out=prod_flat[0:n, 0:BW], in0=v, in1=v, scale=1.0, scalar=0.0,
                                             op0=ALU.mult, op1=ALU.add, accum_out=lvar[0:n, t:t + 1])
                link(ins)
            V.tensor_scalar(lvar, lvar, 1.0 / BW, EPS, ALU.mult, ALU.add).then_inc(ln_var, 1)
            dve.wait_ge(ln_sqrt, 1)
            link(V.reciprocal(lvar, lvar))
            for t, (_, n) in enumerate(TILES):
                v = vN[0:n, t, :]
                link(V.scalar_tensor_tensor(out=v, in0=v, scalar=lvar[0:n, t:t + 1], in1=lng[0:n, :],
                                            op0=ALU.mult, op1=ALU.mult))
                ins = V.tensor_tensor(v, v, lnb[0:n, :], ALU.add)
                if t < 2:
                    link(ins)
            ins.then_inc(ln_done, 1)
            def head_max(hd):
                ps = take(A_SC[hd])
                link(V.tensor_reduce(mx, ps[:, :].rearrange("p (t m) -> p t m", t=2), AX.X, ALU.max))
                V.tensor_scalar(negm, mx, -SCALE, None, ALU.mult).then_inc(negm_ready, 1)

            def head_norm(hd):
                dve.wait_ge(exp_done, hd + 1 + (hd > 1))
                link(V.reciprocal(rs, rs))
                link(V.tensor_scalar(Pp[hd % 2][0], Pp[hd % 2][0], rs[:, 0:1], None, ALU.mult))
                V.tensor_scalar(Pp[hd % 2][1], Pp[hd % 2][1], rs[:, 1:2], None, ALU.mult).then_inc(aux_done, 1)

            def head_out(hd):
                ps = take(A_HEAD[hd])
                V.tensor_copy(PpT_flat[hd % 2], ps[:, :]).then_inc(aux_done, 1)
                ps = take(A_HEAD[hd] + 1)
                V.tensor_copy(brT[:, 12 + hd, 0:TP], ps[:, 0:TP]).then_inc(aux_done, 1)

            for b in range(TS):
                dve.wait_ge(cache_in[b % 2], 16 * (b // 2 + 1))
                ps = take(A_QB + b)
                if b:
                    dve.wait_ge(ck_used, b)
                V.tensor_tensor(prod, cache[b % 2], ps[:, :].unsqueeze(1).to_broadcast([P, 2, 512]),
                                ALU.mult).then_inc(aux_done, 1)
                dve.wait_ge(aux_done, A_QB + b + 1)
                V.tensor_reduce(sT[:, :, 4 * b:4 * b + 4], prod.rearrange("p m (h d) -> p m h d", h=NH),
                                AX.X, ALU.add).then_inc(ck_used, 1)
            head_max(0)
            head_norm(0)
            head_max(1)
            head_norm(1)
            for i in range(2):
                ps, n = take(A_ST + i), 4 - 2 * i
                V.tensor_copy(ext[:, 4 * i:4 * i + n, :, 0:NST],
                              ps[:, 0:n * 120].rearrange("p (k b t) -> p k b t", k=n, b=TS)).then_inc(aux_done, 1)
            dve.wait_ge(z_done, Z_U)
            link(V.tensor_copy(ext[:, :, :, NST], pT[:, :, PAD + TP:PAD + T]))
            ps = take(A_SS)
            link(V.tensor_reduce(smx[0:32], ps[0:32, 0:256], AX.X, ALU.max))
            V.tensor_scalar(snegm[0:32], smx[0:32], -SCALE, None, ALU.mult).then_inc(negm_ready, 1)
            dve.wait_ge(exp_done, 3)
            link(V.reciprocal(srs[0:32], srs[0:32]))
            V.tensor_scalar(Ps[0:32, :], Ps[0:32, :], srs[0:32], None, ALU.mult).then_inc(aux_done, 1)
            dve.wait_ge(pad_ok, 1)
            link(V.tensor_tensor(stA[:, :, 1:272], pT[:, :, 1:272], pT[:, :, 0:271], ALU.add))
            dve.wait_ge(rc_ok, 1)
            for g, w in enumerate(WINDOWS):
                link(V.tensor_scalar(rc[:, g, :], rc[:, g, :], float(w), None, ALU.min))
            link(V.reciprocal(rc, rc))
            ps = take(A_SP)
            V.tensor_copy(PsT.rearrange("p m c -> p (m c)"), ps[:, 0:64]).then_inc(aux_done, 1)

            def pool_group(g, src, other):
                w = WINDOWS[g]
                if g:
                    b0 = (1, 3, 4)[g - 1]
                    lo = w - 1
                    link(V.tensor_tensor(other[:, b0:, lo:272], src[:, b0:, lo:272], src[:, b0:, lo - w // 2:272 - w // 2],
                                         ALU.add))
                    src, other = other, src
                b0 = 3 * (g // 2)
                pieces = ((b0, 0, P), (b0 + 1, 0, 64)) if g % 2 == 0 else ((b0 + 1, 64, P), (b0 + 2, 0, P))
                for k, p0, p1 in pieces:
                    V.scalar_tensor_tensor(out=diff[p0:p1, k, PAD:TP], in0=src[p0:p1, k, 2 * PAD:PAD + TP], scalar=1.0 / w,
                                           in1=pT[p0:p1, k, 2 * PAD:PAD + TP], op0=ALU.mult, op1=ALU.subtract)
                    link(V.tensor_tensor(tmp16[p0:p1, :], src[p0:p1, k, PAD:2 * PAD], rc[p0:p1, g, :], ALU.mult))
                    link(V.tensor_tensor(diff[p0:p1, k, 0:PAD], tmp16[p0:p1, :], pT[p0:p1, k, PAD:2 * PAD], ALU.subtract))
                    link(V.tensor_reduce(wsum[p0:p1, :], ext[p0:p1, k, :, PAD - w:PAD], AX.X, ALU.add))
                    link(V.scalar_tensor_tensor(out=diff[p0:p1, k, TP:T], in0=wsum[p0:p1, :], scalar=1.0 / w,
                                                in1=pT[p0:p1, k, PAD + TP:PAD + T], op0=ALU.mult, op1=ALU.subtract))
                return src, other

            sums = pool_group(0, stA, stB)
            sums = pool_group(1, *sums)
            for hd in range(NH):
                head_out(hd)
                if hd + 2 < NH:
                    head_max(hd + 2)
                    head_norm(hd + 2)
            for i in range(2):
                ps, w = take(A_PN + i), 512 - 256 * i
                V.tensor_copy(pn[0:NST + TS, 512 * i:512 * i + w], ps[0:NST + TS, 0:w]).then_inc(aux_done, 1)
            sums = pool_group(2, *sums)
            pool_group(3, *sums)
            dve.nop().then_inc(diff_ready, 1)
            dve.wait_ge(z_done, Z_G)
            dve.wait_ge(const_in, 64)
            for t in range(2):
                for i in range(2):
                    ps, g0, n = take(A_MX + 2 * t + i), 4 * i, 4 - 2 * i
                    link(V.tensor_tensor(mixt[:, 0:n, :], ps[:, 0:n * P].rearrange("p (g i) -> p g i", g=n),
                                         bs[:, g0:g0 + n, :], ALU.add))
                    u = brT[:, g0:g0 + n, t * P:(t + 1) * P]
                    V.tensor_tensor(u, u, mixt[:, 0:n, :], ALU.mult).then_inc(aux_done, 1)
                    dve.wait_ge(aux_done, A_MX + 2 * t + i + 1)
            ps = take(A_MX + 4)
            m8 = prod_flat[:, 0:GG * TS].rearrange("p (g t) -> p g t", g=GG)
            link(V.tensor_tensor(m8, ps[:, 0:GG * TS].rearrange("p (g t) -> p g t", g=GG),
                                 bs[:, :, 0:1].to_broadcast([P, GG, TS]), ALU.add))
            V.tensor_tensor(brT[:, 0:GG, TP:T], brT[:, 0:GG, TP:T], m8, ALU.mult).then_inc(aux_done, 1)
            for k in range(GG):
                ps = take(A_PL + k)
                V.tensor_scalar(brT[:, GG + k, :], ps[:, 0:T], pscale[:, k:k + 1], None, ALU.mult).then_inc(aux_done, 1)

            dve.wait_ge(sv_ready, 1)
            V.tensor_copy(brT[:, 12:16, TP:T], bank[7][:, 0:32].rearrange("p (h b) -> p h b", h=NH)).then_inc(sv_done, 1)

            def split_lo(b, raw, hi):
                for p in range(PIECES):
                    js = slice(p * KT // PIECES, (p + 1) * KT // PIECES)
                    dve.wait_ge(hi_done, hi + (p + 1))
                    V.tensor_tensor(w_lo[b][:, js, :], slot_half(raw, b)[:, js, :], w_hi[b][:, js, :],
                                    ALU.subtract).then_inc(lo_done, 1)

            split_lo(0, 0, 0)
            dve.wait_ge(st_out, 48)
            for q in range(4):
                dve.wait_ge(xh_done, q + 1)
                V.tensor_tensor(xn_lo[:, 4 * q:4 * q + 4, :], xnT[:, 4 * q:4 * q + 4, :], xn_hi[:, 4 * q:4 * q + 4, :],
                                ALU.subtract).then_inc(xn_split, 1)
            split_lo(1, 0, PIECES)

            with dve.Fori(0, N_GRP) as g:
                for u in range(2, 8):
                    split_lo(u % 2, u // 2, g * (8 * PIECES) + PIECES * u)
                for b in range(2):
                    split_lo(b, 0, g * (8 * PIECES) + PIECES * (8 + b))
                    dve.wait_ge(z_done, g * 6 + (Z_G + 5 + b))
                    dve.wait_ge(br_ready, g * 2 + (b + 1))
                    if b == 1:
                        dve.wait_ge(merged, g * 2 + 3)
                    else:
                        dve.wait_ge(merged, g * 2 + 2)
                    for i in range(3):
                        V.tensor_tensor(gp[:, i, :], sg[:, b, i, :], bank[2 + 3 * b + i][:, 0:T], ALU.mult).then_inc(merge_step, 1)
                    dve.wait_ge(merge_step, g * 12 + (6 * b + 3))
                    V.tensor_tensor(gp[:, 3, :], gp[:, 0, :], gp[:, 1, :], ALU.add).then_inc(merge_step, 1)
                    dve.wait_ge(merge_step, g * 12 + (6 * b + 4))
                    V.tensor_tensor(gp[:, 0, :], gp[:, 3, :], gp[:, 2, :], ALU.add).then_inc(merge_step, 1)
                    dve.wait_ge(merge_step, g * 12 + (6 * b + 5))
                    if b == 0:
                        dve.wait_ge(br_split, 2)
                    V.tensor_copy(mg_hi_f[:, bass.ds(g * (2 * T) + b * T, T)], gp[:, 0, :]).then_inc(merge_step, 1)
                    dve.wait_ge(merge_step, g * 12 + (6 * b + 6))
                    V.tensor_tensor(mg_lo_f[:, bass.ds(g * (2 * T) + b * T, T)], gp[:, 0, :],
                                    mg_hi_f[:, bass.ds(g * (2 * T) + b * T, T)], ALU.subtract).then_inc(merged, 1)

            dve.wait_ge(gffnr_in, 16)

            def take_r(b):
                ps = take(A_R[b])
                if b >= 2:
                    dve.wait_ge(lg_ready, b - 1)
                V.tensor_scalar(hgT[:, b % 2, :], ps[:, 0:T], gffnr[:, b:b + 1], None, ALU.mult).then_inc(aux_done, 1)

            split_lo(0, (C_OUT + 1) % 2, PIECES * (2 * C_OUT + 2))
            for b in range(KT):
                if b + 3 < KT:
                    split_lo((b + 3) % 2, (C_OUT + (b + 3) // 2) % 2, PIECES * (2 * C_OUT + b + 3))
                ps = take(A_O[b])
                cols = slice(b * P, (b + 1) * P)
                link(V.tensor_tensor(x[0:TS, 2, cols], x[0:TS, 2, cols], ps[0:TS, 2 * P:3 * P], ALU.add))
                V.tensor_tensor(x[:, 0:2, cols], x[:, 0:2, cols], ps[:, 0:2 * P].rearrange("p (t c) -> p t c", t=2),
                                ALU.add).then_inc(aux_done, 1)
                if b % 4 == 3:
                    dve.wait_ge(aux_done, A_O[b] + 1)
                    dve.nop().then_inc(h_done, 1)
                if b:
                    take_r(b - 1)
            take_r(KT - 1)
            dve.wait_ge(act_chain, 2 + 3 + NH + 12)
            link(V.tensor_reduce(ssh, ssh4, AX.X, ALU.add))
            V.tensor_scalar(ssh, ssh, 1.0 / D, EPS, ALU.mult, ALU.add).then_inc(h_var, 1)
            dve.wait_ge(h_sqrt, 1)
            V.reciprocal(rh, rh).then_inc(xn2_ready, 1)
            dve.wait_ge(lg_ready, KT)
            V.tensor_copy(lgT[0:36, :], bank[7][0:36, 0:T]).then_inc(xn2_ready, 1)

            dve.wait_ge(xn2_ready, 1)
            dve.wait_ge(router_in, 16 * 7)
            dve.wait_ge(tri_ok, 7)
            ps = take(A_LT)
            for t, (_, n) in enumerate(TILES):
                ins = V.scalar_tensor_tensor(out=lg[0:n, t, :], in0=ps[0:n, t * 36:(t + 1) * 36], scalar=rh[0:n, t:t + 1],
                                             in1=lgb[0:n, :], op0=ALU.mult, op1=ALU.add)
                if t < 2:
                    link(ins)
            ins.then_inc(aux_done, 1)
            dve.wait_ge(aux_done, A_LT + 1)

            def over(a, n):
                return a.unsqueeze(2).to_broadcast([P, 3, n])

            def first_max(vals, n, m, eq, key, km, hot):
                link(V.tensor_reduce(m, vals, AX.X, ALU.max))
                link(V.tensor_tensor(eq, vals, over(m, n), ALU.is_equal))
                link(V.tensor_tensor(key, eq, rev[:, 0:n].unsqueeze(1).to_broadcast([P, 3, n]), ALU.mult))
                link(V.tensor_reduce(km, key, AX.X, ALU.max))
                link(V.tensor_tensor(hot, key, over(km, n), ALU.is_equal))

            gl = lg[:, :, 0:NG]
            gmax, km, gsum, m1, m2, dm, den, w1, w2 = r1[0], r1[1], r1[2], r1[3], r1[4], r1[5], r1[6], r1[7], r1[8]
            ohg = r4[1]
            first_max(gl, NG, gmax, r4[0], r4[2], km, ohg)
            V.tensor_tensor(r4[0], gl, over(gmax, NG), ALU.subtract).then_inc(lg_exp_in, 1)
            link(V.tensor_tensor(t32, lg[:, :, NG:36].rearrange("p t (g e) -> p t g e", g=NG),
                                 ohg.unsqueeze(3).to_broadcast([P, 3, NG, NE]), ALU.mult))
            esel, oh1, oh2, eqk, e2 = r8
            link(V.tensor_reduce(esel, t32.rearrange("p t g e -> p t e g"), AX.X, ALU.add))
            first_max(esel, NE, m1, oh2, eqk, km, oh1)
            link(V.scalar_tensor_tensor(out=e2, in0=oh1, scalar=-1e30, in1=esel, op0=ALU.mult, op1=ALU.add))
            first_max(e2, NE, m2, eqk, esel, km, oh2)
            V.tensor_tensor(dm, m2, m1, ALU.subtract).then_inc(lg_exp_in, 1)
            dve.wait_ge(lg_exp, 2)
            link(V.tensor_reduce(gsum, r4[0], AX.X, ALU.add))
            link(V.tensor_scalar(den, dm, 1.0, None, ALU.add))
            link(V.tensor_tensor(den, den, gsum, ALU.mult))
            link(V.reciprocal(w1, den))
            link(V.tensor_tensor(w2, w1, dm, ALU.mult))
            link(V.tensor_tensor(eqk, oh2, over(w2, NE), ALU.mult))
            link(V.tensor_tensor(esel, oh1, over(w1, NE), ALU.mult))
            link(V.tensor_tensor(esel, esel, eqk, ALU.add))
            link(V.tensor_tensor(e2, oh1, oh2, ALU.add))
            for p1, t0, t1 in ((P, 0, 2), (TS, 2, 3)):
                n = t1 - t0
                hot = ohg[0:p1, t0:t1].unsqueeze(3).to_broadcast([p1, n, NG, NE])
                V.tensor_tensor(sel[0:p1, t0:t1], hot, e2[0:p1, t0:t1].unsqueeze(2).to_broadcast([p1, n, NG, NE]),
                                ALU.mult).then_inc(sel_ready, 1)
                V.tensor_tensor(comb[0:p1, t0:t1], hot, esel[0:p1, t0:t1].unsqueeze(2).to_broadcast([p1, n, NG, NE]),
                                ALU.mult).then_inc(sel_ready, 1)
            dve.wait_ge(sel_ready, 4)
            ps = take(A_POS)
            link(V.scalar_tensor_tensor(out=pos[:, :, 0:NX], in0=self_, scalar=-FAR, in1=ps[:, 0:96].rearrange("p (t x) -> p t x", t=3),
                                        op0=ALU.mult, op1=ALU.add))
            link(V.tensor_scalar(pos[:, :, 0:NX], pos[:, :, 0:NX], FAR, None, ALU.add))
            link(V.tensor_scalar(pos[:, :, NX:NX + EPR], pos[:, :, 0:EPR], -float(CAP), None, ALU.add))
            link(V.tensor_copy(combx[:, :, NX:NX + EPR], combx[:, :, 0:EPR]))

            def slot_maps(e0, step):
                V.tensor_tensor(P01, pos[:, :, e0].unsqueeze(3).to_broadcast([P, 3, EPR, CAP]),
                                cidx.unsqueeze(1).unsqueeze(1).to_broadcast([P, 3, EPR, CAP]), ALU.is_equal).then_inc(p_step, 1)
                dve.wait_ge(p_step, step)
                V.tensor_tensor(Pw, P01, combx[:, :, e0].unsqueeze(3).to_broadcast([P, 3, EPR, CAP]), ALU.mult).then_inc(p_ready, 1)

            slot_maps(slice(0, EPR), 1)
            link(V.tensor_reduce(npf[:, 0:1], ps[:, 96:128], AX.X, ALU.max))
            link(V.tensor_scalar(thr2, thr, npf[:, 0:1], None, ALU.is_lt))
            V.tensor_reduce(npf[:, 1:2], thr2, AX.X, ALU.add).then_inc(aux_done, 1)
            dve.wait_ge(aux_done, A_POS + 1)
            V.tensor_copy(npass_i[:, :], npf[:, 1:2]).then_inc(np_ready, 1)
            dve.wait_ge(np_ready, 1)
            npass = dve.value_load(npass_i[0:1, 0:1], min_val=1, max_val=9)
            with dve.Fori(0, npass) as k:
                with dve.Fori(0, ROUNDS) as r:
                    it = k * ROUNDS + r
                    for q in range(4):
                        dve.wait_ge(aux_ready, it * JPR + (A_E + q + 1))
                        V.tensor_tensor(xgT[:, 4 * q:4 * q + 4, :], bank[6 + q % 2][:, :].rearrange("p (j t) -> p j t", j=4),
                                        gffnc[:, 4 * q:4 * q + 4].unsqueeze(2).to_broadcast([P, 4, P]),
                                        ALU.mult).then_inc(aux_done, 1)
                    dve.wait_ge(aux_ready, it * JPR + (A_E + 5))
                    V.tensor_copy(PwT, bank[6][:, 0:T]).then_inc(aux_done, 1)
                    slot_maps(bass.ds(r * EPR + EPR, EPR), it + k + 2)
                    dve.wait_ge(silu_done, it + 1)
                    dve.wait_ge(e_used, it * CPR + (CREDIT + 16))
                    V.tensor_tensor(h.rearrange("s j p -> s p j"), hs.rearrange("s (p j) -> s p j", j=4),
                                    bank[1][:, :].rearrange("s (p j) -> s p j", j=4), ALU.mult).then_inc(h_ready, 1)
                    dve.wait_ge(aux_ready, it * JPR + (A_E + 6))
                    V.tensor_copy(hT.rearrange("p j s -> p (j s)"), bank[7][:, :]).then_inc(aux_done, 1)
                    dve.wait_ge(sq_done, it * 12 + 1)
                    for n in range(4):
                        for t, (_, cnt) in enumerate(TILES):
                            q = 6 + 3 * n + t
                            dve.wait_ge(aux_ready, it * JPR + (A_E + q + 1))
                            xv = x[0:cnt, t, n * 512:(n + 1) * 512]
                            V.tensor_tensor(xv, xv, bank[6 + q % 2][0:cnt, :], ALU.add).then_inc(aux_done, 1)
                V.tensor_scalar(cidx, cidx, float(CAP), None, ALU.add).then_inc(p_step, 1)
                dve.wait_ge(p_step, k * (ROUNDS + 1) + (ROUNDS + 2))
            dve.wait_ge(sq_done, npass * (12 * ROUNDS) + 1)
            link(V.tensor_reduce(ssx, ssh4, AX.X, ALU.add))
            mean_eps(ssx, D, f_var)
            dve.wait_ge(f_sqrt, 1)
            V.reciprocal(rx, rx).then_inc(f_rms, 1)
            dve.wait_ge(f_rms, 1)
            dve.wait_ge(gfin_in, 16)
            for t in range(2):
                for half in range(2):
                    cols = slice(half * 1024, (half + 1) * 1024)
                    V.scalar_tensor_tensor(out=x[:, t, cols], in0=x[:, t, cols], scalar=rx[:, t:t + 1], in1=gfin[:, cols],
                                           op0=ALU.mult, op1=ALU.mult).then_inc(y_final, 1)

        @block.tensor
        def _(pe):
            mm, tr = nc.tensor.matmul, nc.tensor.transpose

            def aux(job):
                if job >= AUX:
                    pe.wait_ge(aux_done, job - AUX + 1)
                return bank[2 + job % AUX]

            def z(n):
                if n >= 2:
                    pe.wait_ge(z_done, n - 1)
                return bank[n % 2]

            def rows_to_columns(base, src, n, wait):
                wait()
                if n == P:
                    for q in range(4):
                        ps = aux(base + q)
                        for j in range(4):
                            ins = tr(ps[:, j * P:(j + 1) * P], src(4 * q + j), ident[:, :])
                        ins.then_inc(aux_ready, 1)
                else:
                    ps = aux(base)
                    for j in range(KT):
                        ins = tr(ps[:, j * n:(j + 1) * n], src(j), ident[0:n, 0:n])
                    ins.then_inc(aux_ready, 1)

            def strided(b, n):
                v = xs[0:n, b, :].rearrange("p (c j) -> p j c", j=KT)
                return lambda j: v[:, j, :]

            pe.wait_ge(id_ok, 1)
            rows_to_columns(A_MEM, strided(0, P), P, lambda: pe.wait_ge(xs_ready, 1))
            rows_to_columns(A_MEM + 4, strided(1, P), P, lambda: pe.wait_ge(xs_ready, 2))
            pe.wait_ge(aux_done, A_MEM + 8)
            for c in range(N_MKV):
                pe.wait_ge(full[c % 4], early_full(c))
                w = slot(c)
                for t in range(2):
                    ps = z(2 * c + t)
                    for j in range(KT):
                        ins = mm(ps[:, 0:CC], memT[:, j, t * P:(t + 1) * P], w[:, j, :], start=j == 0, stop=j == KT - 1)
                    ins.then_inc(z_ready, 1)
                if c == 0:
                    rows_to_columns(A_X, strided(0, P), P, lambda: pe.wait_ge(xs_ready, 3))
                    rows_to_columns(A_X + 4, strided(1, P), P, lambda: pe.wait_ge(xs_ready, 4))
                    rows_to_columns(A_X + 8, strided(0, TS), TS, lambda: pe.wait_ge(xs_ready, 5))

            def project(c, between=None):
                n = N_MKV + c
                pe.wait_ge(full[n % 4], early_full(n))
                w = slot(n)
                for b in range(2):
                    ps = z(2 * n + b)
                    for j in range(KT):
                        ins = mm(ps[:, 0:T], w[:, j, b * P:(b + 1) * P], xnT[:, j, :], start=j == 0, stop=j == KT - 1)
                    ins.then_inc(z_ready, 1)
                    if b == 0 and between:
                        between()

            pe.wait_ge(aux_done, A_X + 9)
            for c in range(3):
                project(c)
            for hd in range(NH):
                ps = aux(A_KT + hd)
                for t in range(2):
                    ins = tr(ps[:, t * P:(t + 1) * P], kvK[:, t, hd * P:(hd + 1) * P], ident[:, :])
                ins.then_inc(aux_ready, 1)
            project(3)
            pe.wait_ge(pool_chain, 2)
            for i in range(2):
                ps, n = aux(A_WS + i), 4 - 2 * i
                for g in range(n):
                    ins = tr(ps[:, g * P:(g + 1) * P], wsN[:, 4 * i + g, :], ident[:, :])
                ins.then_inc(aux_ready, 1)
            project(4)
            for t, (t0, cnt) in enumerate(TILES):
                for i in range(2):
                    ps, n = aux(A_VN + 2 * t + i), 4 - 2 * i
                    for g in range(n):
                        ins = tr(ps[0:cnt, g * P:(g + 1) * P], vT[:, 4 * i + g, t0:t0 + cnt], ident[:, :])
                    ins.then_inc(aux_ready, 1)
            pe.wait_ge(z_done, Z_P)
            ps = aux(A_QN)
            for hd in range(NH):
                ins = tr(ps[0:TS, hd * P:(hd + 1) * P], qT[:, hd, TP:T], ident[:, :])
            ins.then_inc(aux_ready, 1)

            def sample_q(b):
                ps = aux(A_QB + b)
                mm(ps[:, :], ident[0:TS, b:b + 1].to_broadcast([TS, P]), qn[0:TS, :], start=True, stop=True).then_inc(aux_ready, 1)

            def scores(hd):
                ps = aux(A_SC[hd])
                for t in range(2):
                    ins = mm(ps[:, t * NM:(t + 1) * NM], qT[:, hd, t * P:(t + 1) * P], kT[:, hd, :], start=True, stop=True)
                ins.then_inc(aux_ready, 1)

            def head(hd):
                ps = aux(A_HEAD[hd])
                pe.wait_ge(aux_done, A_SC[hd] + 1)
                for m in range(2):
                    for t in range(2):
                        ins = tr(ps[:, m * NM + t * P:m * NM + (t + 1) * P], Pp[hd % 2][t][:, m * P:(m + 1) * P],
                                 ident[:, :])
                ins.then_inc(aux_ready, 1)
                ps = aux(A_HEAD[hd] + 1)
                pe.wait_ge(aux_done, A_HEAD[hd] + 1)
                for m in range(2):
                    ins = mm(ps[:, 0:TP], kvV[:, m, hd * P:(hd + 1) * P], PpT[hd % 2][m], start=m == 0, stop=m == 1)
                ins.then_inc(aux_ready, 1)

            def sample_out(b):
                pe.wait_ge(cache_in[b % 2], 64 + 16 * (b // 2 + 1))
                for hd in range(NH):
                    for m in range(2):
                        ins = mm(bank[7][:, hd * TS + b:hd * TS + b + 1], cache[b % 2][:, m, hd * P:(hd + 1) * P],
                                 PsT[:, m, 4 * b + hd:4 * b + hd + 1], start=m == 0, stop=m == 1)
                ins.then_inc(cv_used if b < TS - 1 else sv_ready, 1)

            project(5)
            pe.wait_ge(aux_done, A_QN + 1)
            for b in range(4):
                sample_q(b)
            project(6)
            for b in range(4, TS):
                sample_q(b)
            project(7)
            pe.wait_ge(aux_done, A_KT + 4)
            scores(0)
            scores(1)
            pe.wait_ge(state_in, 16)
            for i in range(2):
                ps, n = aux(A_ST + i), 4 - 2 * i
                for g in range(n):
                    ins = tr(ps[:, g * 120:(g + 1) * 120], stN[0:120, (4 * i + g) * P:(4 * i + g + 1) * P],
                             ident[0:120, 0:120])
                ins.then_inc(aux_ready, 1)
            pe.wait_ge(ck_used, TS)
            ps = aux(A_SS)
            for m in range(2):
                ins = tr(ps[0:32, m * P:(m + 1) * P], sT[:, m, :], ident[:, :])
            ins.then_inc(aux_ready, 1)

            def sample_probs():
                ps = aux(A_SP)
                pe.wait_ge(aux_done, A_SS + 1)
                for m in range(2):
                    ins = tr(ps[:, m * 32:(m + 1) * 32], Ps[0:32, m * P:(m + 1) * P], ident[0:32, 0:32])
                ins.then_inc(aux_ready, 1)

            project(8, sample_probs)
            head(0)
            scores(2)
            head(1)
            scores(3)
            pe.wait_ge(aux_done, A_SP + 1)
            sample_out(0)
            sample_out(1)
            project(9, lambda: sample_out(2))
            sample_out(3)
            head(2)
            head(3)
            for i in range(2):
                ps, n = aux(A_PN + i), 4 - 2 * i
                for g in range(n):
                    ins = tr(ps[0:NST + TS, g * P:(g + 1) * P], pT[:, 4 * i + g, PAD + TP - NST:PAD + T], ident[:, :])
                ins.then_inc(aux_ready, 1)
            project(10, lambda: sample_out(4))
            sample_out(5)
            pe.wait_ge(ln_done, 1)
            pe.wait_ge(aux_done, A_WS + 2)
            for t in range(2):
                for i in range(2):
                    ps, n = aux(A_MX + 2 * t + i), 4 - 2 * i
                    for g in range(n):
                        ins = mm(ps[:, g * P:(g + 1) * P], vN[:, t, (4 * i + g) * P:(4 * i + g + 1) * P], wsT[:, 4 * i + g, :],
                                 start=True, stop=True)
                    ins.then_inc(aux_ready, 1)
            sample_out(6)
            ps = aux(A_MX + 4)
            pe.wait_ge(dg_ready, 1)
            for g in range(GG):
                ins = mm(ps[:, g * TS:(g + 1) * TS], vN[0:TS, 2, g * P:(g + 1) * P], dg[0:TS, g, :], start=True, stop=True)
            ins.then_inc(aux_ready, 1)
            sample_out(7)
            pe.wait_ge(diff_ready, 1)
            pe.wait_ge(pool_in, 128)
            for k in range(GG):
                ps = aux(A_PL + k)
                b0 = 3 * (k // 3)
                lo = ((b0, 0, P), (b0 + 1, 0, 64))
                hi = ((b0 + 1, 64, P), (b0 + 2, 0, P))
                parts = (((0, P, lo, 0),), ((0, 64, lo, P), (64, P, hi, 0)), ((0, P, hi, 64),))[k % 3]
                for o0, o1, ins_of, c0 in parts:
                    for i, (kb, p0, p1) in enumerate(ins_of):
                        ins = mm(ps[o0:o1, 0:T], wp[p0:p1, kb, c0:c0 + o1 - o0], diff[p0:p1, kb, :], start=i == 0, stop=i == 1)
                ins.then_inc(aux_ready, 1)

            pe.wait_ge(aux_done, A_PL + 6)
            pe.wait_ge(sv_done, 1)

            def three_products(ps, b, x_hi, x_lo, k0, k1, lo, rows=None):
                for j in range(k0, k1):
                    if j % (KT // PIECES) == 0:
                        pe.wait_ge(lo_done, lo + (j * PIECES // KT + 1))
                    if rows:
                        rows(j)
                    mm(ps[:, 0:T], w_hi[b][:, j, :], x_hi[:, j, :], start=j == k0, stop=False)
                    mm(ps[:, 0:T], w_hi[b][:, j, :], x_lo[:, j, :], start=False, stop=False)
                    ins = mm(ps[:, 0:T], w_lo[b][:, j, :], x_hi[:, j, :], start=False, stop=j == k1 - 1)
                return ins

            with pe.Fori(0, N_GRP) as g:
                for u in range(6):
                    def x_parts(j):
                        if u == 0 and j % 4 == 0:
                            pe.wait_ge(xn_split, j // 4 + 1)
                    pe.wait_ge(z_done, g * 6 + (Z_G + u - 1))
                    three_products(bank[u % 2], u % 2, xn_hi, xn_lo, 0, KT, g * (8 * PIECES) + PIECES * u,
                                   x_parts).then_inc(z_ready, 1)
                pe.wait_ge(br_split, 2)
                for b in range(2):
                    pe.wait_ge(merged, g * 2 + (b + 1))
                    for i, (k0, k1) in enumerate(((0, 6), (6, 12), (12, 16))):
                        ins = three_products(bank[2 + 3 * b + i], b, br_hi, br_lo, k0, k1,
                                             g * (8 * PIECES) + PIECES * (6 + b))
                    ins.then_inc(br_ready, 1)

            pe.wait_ge(merged, 2 * N_GRP)

            def out_rows(b):
                ps = aux(A_O[b])
                pe.wait_ge(z_done, Z_O + b + 1)
                for t, (t0, cnt) in enumerate(TILES):
                    ins = tr(ps[0:cnt, t * P:(t + 1) * P], oT[:, b % 2, t0:t0 + cnt], ident[:, :])
                ins.then_inc(aux_ready, 1)

            def new_columns(b):
                ps = aux(A_R[b])
                pe.wait_ge(aux_done, A_O[b] + 1)
                for t, (t0, cnt) in enumerate(TILES):
                    ins = tr(ps[:, t0:t0 + cnt], x[0:cnt, t, b * P:(b + 1) * P], ident[0:cnt, 0:cnt])
                ins.then_inc(aux_ready, 1)

            def logits(b):
                pe.wait_ge(aux_done, A_R[b] + 1)
                mm(bank[7][0:36, 0:T], wr[:, b, :], hgT[:, b % 2, :], start=b == 0, stop=b == KT - 1).then_inc(lg_ready, 1)

            def last_merged(j):
                if j >= KT - 2:
                    pe.wait_ge(merged, 2 * N_GRP + j + 3 - KT)

            pe.wait_ge(router_in, 16 * 7)
            for c in range(8):
                for b in range(2):
                    k = 2 * c + b
                    three_products(z(Z_O + k), b, mg_hi, mg_lo, 0, KT, PIECES * (2 * C_OUT + k),
                                   last_merged if k == 0 else None).then_inc(z_ready, 1)
                    if k >= 1:
                        out_rows(k - 1)
                    if k >= 2:
                        new_columns(k - 2)
                    if k >= 3:
                        logits(k - 3)
            out_rows(15)
            new_columns(14)
            logits(13)
            new_columns(15)
            logits(14)
            logits(15)
            ps = aux(A_LT)
            pe.wait_ge(xn2_ready, 2)
            for t, (t0, cnt) in enumerate(TILES):
                ins = tr(ps[0:cnt, t * 36:(t + 1) * 36], lgT[0:36, t0:t0 + cnt], ident[0:36, 0:36])
            ins.then_inc(aux_ready, 1)
            pe.wait_ge(sel_ready, 4)
            pe.wait_ge(tri_ok, 7)
            ps = aux(A_POS)
            for t in range(4):
                last = min(t, 2)
                for u in range(last + 1):
                    lhs = tri if u == t else ones
                    ins = mm(ps[:, t * NX:(t + 1) * NX], lhs, self_[:, u, :], start=u == 0, stop=u == last)
            ins.then_inc(aux_ready, 1)

            pe.wait_ge(xn_copied, 3)
            pe.wait_ge(np_ready, 1)
            npass = pe.value_load(npass_i[0:1, 0:1], min_val=1, max_val=9)
            with pe.Fori(0, npass) as k:
                with pe.Fori(0, ROUNDS) as r:
                    it = k * ROUNDS + r

                    def eaux(q):
                        pe.wait_ge(aux_done, it * JPR + (A_E + q - 1))
                        return bank[6 + q % 2]

                    pe.wait_ge(p_ready, it + 1)

                    def gather(q):
                        ps = eaux(q)
                        for jj in range(4):
                            for t, (_, cnt) in enumerate(TILES):
                                ins = mm(ps[:, jj * P:(jj + 1) * P], xn2[0:cnt, t, 4 * q + jj, :], P01f[0:cnt, t, :],
                                         start=t == 0, stop=t == 2)
                        ins.then_inc(aux_ready, 1)

                    def scatter(n):
                        for t, (t0, cnt) in enumerate(TILES):
                            ps = eaux(6 + 3 * n + t)
                            if t == 0:
                                pe.wait_ge(y_ready, it * 4 + (n + 1))
                            mm(ps[0:cnt, :], PwT[:, t0:t0 + cnt], y[:, n, :], start=True, stop=True).then_inc(aux_ready, 1)

                    gather(0)
                    for c in range(CPR):
                        s = EORDER[c % ESLOTS]
                        if c < 8 and c % 2 == 0:
                            if c < 6:
                                gather(c // 2 + 1)
                            else:
                                ps = eaux(4)
                                for t, (t0, cnt) in enumerate(TILES):
                                    ins = tr(ps[:, t0:t0 + cnt], Pwf[0:cnt, t, :], ident[0:cnt, 0:cnt])
                                ins.then_inc(aux_ready, 1)
                            pe.wait_ge(aux_done, it * JPR + (A_E + c // 2 + 1))
                        if c == 22:
                            scatter(0)
                            scatter(1)
                        if c == 16:
                            ps = eaux(5)
                            pe.wait_ge(h_ready, it + 1)
                            for j in range(4):
                                ins = tr(ps[:, j * P:(j + 1) * P], h[:, j, :], ident[:, :])
                            ins.then_inc(aux_ready, 1)
                            pe.wait_ge(aux_done, it * JPR + (A_E + 6))
                        pe.wait_ge(full[s], it * (16 * CPR // ESLOTS) + (before[s] + 16 * (c // ESLOTS + 1)))
                        w = e_slot[s].rearrange("p (e j n) -> p e j n", e=EPR, j=2)
                        for jj in range(2):
                            for e in range(EPR):
                                sl = slice(e * CAP, (e + 1) * CAP)
                                if c < 16:
                                    j = 2 * (c % 8) + jj
                                    ins = mm(bank[c // 8][sl, :], xgT[:, j, sl], w[:, e, jj, :], start=j == 0, stop=j == KT - 1)
                                else:
                                    half, j = (c - 16) // 4, (c - 16) % 4
                                    ins = mm(bank[2 + 2 * half + jj][sl, :], hT[:, j, sl], w[:, e, jj, :],
                                             start=j == 0, stop=j == 3)
                        ins.then_inc(e_used, 1)
                    scatter(2)
                    scatter(3)


_INS = ["x_prompt", "x_sample", "mem_prompt", "cache_mem_k", "cache_mem_v", "state_pool", "g_mix", "w_in", "ln_v_g",
        "ln_v_b", "w_s", "b_s", "w_pool", "pool_scale", "g_mem", "w_mkv", "w_br_a", "w_br_b", "w_br_c", "w_o", "g_ffn",
        "w_rg", "b_rg", "w_re", "b_re", "w_gate", "w_up", "w_down", "g_final"]
_OUTS = [(1, 256, 2048), (8, 1, 2048), (1, 1, 256, 4, 128), (1, 1, 256, 4, 128), (1, 1, 15, 768), (1, 8, 15, 768),
         (1, 8, 1, 768)]


def kernel(**inputs):
    import numpy as _np
    import concourse.bacc as _bacc
    from concourse.bass_utils import run_bass_kernel_spmd as _run

    nc = _bacc.Bacc("TRN2", target_bir_lowering=False, num_devices=1)
    arrays, ins, outs = {}, [], []
    for name in _INS:
        a = _np.ascontiguousarray(inputs[name])
        arrays[f"in_{name}"] = a
        ins.append(nc.dram_tensor(f"in_{name}", a.shape, mybir.dt.from_np(a.dtype), kind="ExternalInput").ap())
    for i, shape in enumerate(_OUTS):
        outs.append(nc.dram_tensor(f"out_{i}", shape, F32, kind="ExternalOutput").ap())
    branch_kernel(nc, ins, outs)
    r = _run(nc, [arrays], core_ids=[0])
    return tuple(r.results[0][f"out_{i}"] for i in range(len(_OUTS)))
```

```python
import concourse.bass as bass
from concourse import mybir
from contextlib import ExitStack

F32 = mybir.dt.float32
F32R = mybir.dt.float32r
I32 = mybir.dt.int32
ALU = mybir.AluOpType
ACT = mybir.ActivationFunctionType
AX = mybir.AxisListType

P = 128
D = 2048
KT = D // P
TP, TS = 256, 8
T = TP + TS
TILES = ((0, P), (P, P), (TP, TS))
NM = 256
NH, DH = 4, 128
GG = 6
BW = GG * P
PG = 192
WINDOWS = (2, 4, 8, 16)
NST = 15
PAD = 16
NG, NE = 4, 8
NX = NG * NE
DE = 512
EPS = 1e-6
SCALE = float(DH) ** -0.5
CAP = 32
EPR = 4
ROUNDS = NX // EPR
CHUNK = 4096
CC = CHUNK // KT
FAR = 10000.0

N_MKV, N_Z, N_GRP = 4, 22, 8
N_OUT = N_Z + 8 * N_GRP
POOL_LO = 10
PIECES = 2
LN_SQRT = 1
LO_AFTER_LOAD = ((), (), (), (14,), (), (15,), (), (16,), (), (17, 18, 19), (), (20,), (21,), (), (), ())
Z_COLS = (768, 1024, 1280, 2304, 2560, 1536, 1792, 2048, 0, 256, 512)
GATE_COL = 2816
Z_V, Z_Q, Z_P, Z_U, Z_G = 8, 14, 18, 24, 30
Z_O = Z_G + 6 * N_GRP
Z_END = Z_O + 16
ESLOTS = 6
EORDER = (4, 5, 1, 0, 3, 2)
CPR = 24
CREDIT = ESLOTS

_n = 0


def _span(count):
    global _n
    _n += count
    return _n - count


A_MEM = _span(8)
A_X = _span(9)
A_KT = _span(4)
A_WS = _span(2)
A_VN = _span(6)
A_QN = _span(1)
A_QB = _span(TS)
A_SC = [_span(1), _span(1)]
A_ST = _span(2)
A_SS = _span(1)
A_SP = _span(1)
A_HEAD = []
for _h in range(NH):
    A_HEAD.append(_span(2))
    if _h + 2 < NH:
        A_SC.append(_span(1))
A_PN = _span(2)
A_MX = _span(5)
A_PL = _span(6)
A_O, A_R = [], []
for _b in range(KT):
    A_O.append(_span(1))
    if _b:
        A_R.append(_span(1))
A_R.append(_span(1))
A_LT = _span(1)
A_POS = _span(1)
A_E = _n
AUX = 5
JPR = 18


def branch_kernel(nc, io, outs):
    (x_prompt, x_sample, mem_prompt, cache_k, cache_v, state_pool, g_mix, w_in, ln_v_g, ln_v_b,
     w_s, b_s, w_pool, pool_scale, g_mem, w_mkv, w_br_a, w_br_b, w_br_c, w_o, g_ffn, w_rg, b_rg,
     w_re, b_re, w_gate, w_up, w_down, g_final) = io
    (y_prompt, y_sample, new_k, new_v, new_st_p, new_st_s, new_gv) = outs

    ctx = ExitStack()
    with ctx:
        def sb(name, n, dt=F32):
            return ctx.enter_context(nc.sbuf_tensor(name, [P, n], dt))

        def sem(name):
            return ctx.enter_context(nc.semaphore(name))

        arena = -(-nc.sbuf_base // 32) * 32
        ring = sb("ring", 4 * CHUNK + P)
        x_all = sb("x_all", 3 * D)
        trunk = sb("trunk", 3 * KT * T)
        side = sb("side", 17456)
        ident = sb("ident", P)
        small = sb("small", 256)
        npass_i = sb("npass_i", 1, I32)
        bank = [ctx.enter_context(nc.psum_tensor(f"bank{i}", [P, 512], F32)) for i in range(8)]

        def view(t, at, *dims):
            n = 1
            for d in dims:
                n *= d
            v = t[:, at:at + n]
            if len(dims) == 1:
                return v
            names = "abc"[:len(dims)]
            pat = f"p ({' '.join(names)}) -> p {' '.join(names)}"
            return v.rearrange(pat, **dict(zip(names, dims)))

        x = view(x_all, 0, 3, D)
        brT = view(trunk, KT * T, KT, T)
        memT = view(trunk, KT * T, KT, NM)
        mem = view(trunk, 2 * KT * T, 2, D)
        stA = view(trunk, 2 * KT * T, 6, 272)
        stB = view(trunk, 2 * KT * T + 1632, 6, 272)
        stN = view(trunk, 2 * KT * T, 768)
        sT = view(trunk, 2 * KT * T + 3264, 2, 32)
        Ps = view(trunk, 2 * KT * T + 3328, 256)
        PsT = view(trunk, 2 * KT * T + 3584, 2, 32)
        qn = view(trunk, 2 * KT * T + 3648, 512)
        at = 0
        xs = view(side, 0, 2, D)
        vN = view(side, 0, 3, BW)
        vT = view(side, 3 * BW, GG, T)
        diff = view(side, 3 * BW, GG, T)
        sg = side[:, 0:2 * 3 * T].rearrange(
            "p (b i t) -> p b i t", b=2, i=3)
        gp = view(side, 2 * 3 * T, 4, T)
        oT = view(side, 2 * 3 * T + 4 * T, 2, T)
        hgT = view(side, 2 * 3 * T + 6 * T, 2, T)
        lgT = view(side, 2 * 3 * T + 8 * T, T)
        at = 4096
        kvK = view(side, at, 2, 512)
        kvV = view(side, at + 1024, 2, 512)
        Pp = [[view(side, at + b * 512 + t * NM, NM) for t in range(2)] for b in range(2)]
        at += 2048
        kT = view(side, at, NH, NM)
        at += NH * NM
        qT = view(side, at, NH, T)
        at += NH * T
        pT = view(side, at, GG, PAD + T)
        at += GG * (PAD + T)
        wp = view(side, at, GG, PG)
        at += GG * PG
        wsT = view(side, at, GG, P)
        at += GG * P
        bs = view(side, at, GG, P)
        at += GG * P
        lng, lnb = view(trunk, KT * T, BW), view(trunk, KT * T + BW, BW)
        cache_flat = [view(side, at + 1024 * b, 1024) for b in range(2)]
        cache = [view(side, at + 1024 * b, 2, 512) for b in range(2)]
        at += 2048
        prod = view(side, at, 2, 512)
        prod_flat = view(side, at, 1024)
        wsN = view(side, at, GG, P)
        mixt = view(side, at, 4, P)
        at += 1024
        PpT_flat = [view(side, at + b * 512, 512) for b in range(2)]
        PpT = [[view(side, at + b * 512 + m * NM, NM) for m in range(2)] for b in range(2)]
        pn = view(side, at, BW)
        at += 1024
        ext = side[:, at:at + 768].rearrange("p (k b t) -> p k b t", k=GG, b=TS)
        at += 768
        assert at <= 17456, at

        def split_part(name, at, n):
            return nc.alloc_sbuf_tensor_at(name, [P, n], F32R, offset=arena + 4 * at)

        TRUNK0 = 4 * CHUNK + P + 3 * D
        UNIT0 = CHUNK + KT * T
        SIDE0 = TRUNK0 + 3 * KT * T
        w_hi = [split_part(f"w_hi{b}", UNIT0 + b * CHUNK, KT * P).rearrange("p (j c) -> p j c", j=KT) for b in range(2)]
        w_lo = [split_part(f"w_lo{b}", UNIT0 + b * CHUNK + KT * P, KT * P).rearrange("p (j c) -> p j c", j=KT)
                for b in range(2)]
        mg_hi_f = split_part("mg_hi", TRUNK0 + 2 * KT * T, KT * T)
        mg_lo_f = split_part("mg_lo", TRUNK0 + KT * T, KT * T)
        three = [mg_hi_f, mg_lo_f, split_part("xn_hi", TRUNK0, KT * T),
                 split_part("br_hi", SIDE0 + 4096, KT * T), split_part("br_lo", SIDE0 + 4096 + KT * T, KT * T),
                 split_part("xn_lo", CHUNK, KT * T)]
        mg_hi, mg_lo, xn_hi, br_hi, br_lo, xn_lo = [v.rearrange("p (j t) -> p j t", j=KT) for v in three]
        e_slot = {0: view(ring, 0, CHUNK), 1: view(ring, CHUNK, CHUNK), 2: view(ring, UNIT0 + CHUNK, CHUNK),
                  3: view(ring, UNIT0, CHUNK), 4: view(side, 4096, CHUNK), 5: view(side, 8192, CHUNK)}
        y = view(side, 0, 4, 512)
        hs = view(side, 2048, 512)
        h = view(side, 2560, 4, P)
        hT = view(side, 3072, 4, P)
        PwT = view(side, 3584, T)
        at = 12288
        gfin = view(side, at, D)
        at += D
        P01 = side[:, at:at + 384].rearrange("p (t e c) -> p t e c", t=3, e=EPR)
        P01f = view(side, at, 3, P)
        at += 384
        Pw = side[:, at:at + 384].rearrange("p (t e c) -> p t e c", t=3, e=EPR)
        Pwf = view(side, at, 3, P)
        at += 384
        tri = view(side, at, P)
        ones = view(side, at + P, P)
        at += 2 * P
        lg = view(side, at, 3, 36)
        at += 108
        combx = view(side, at, 3, NX + EPR)
        comb = combx[:, :, 0:NX].rearrange("p t (g e) -> p t g e", g=NG)
        at += 108
        sel = side[:, at:at + 96].rearrange("p (t g e) -> p t g e", t=3, g=NG)
        self_ = view(side, at, 3, NX)
        at += 96
        pos = view(side, at, 3, NX + EPR)
        at += 108
        t32 = side[:, at:at + 96].rearrange("p (t g e) -> p t g e", t=3, g=NG)
        at += 96
        r4 = [view(side, at + 12 * i, 3, NG) for i in range(3)]
        at += 36
        r8 = [view(side, at + 24 * i, 3, NE) for i in range(6)]
        at += 144
        r1 = [view(side, at + 3 * i, 3) for i in range(12)]
        at += 36
        cidx = view(side, at, CAP)
        at += CAP
        rev = view(side, at, NE)
        at += NE
        thr = view(side, at, 9)
        at += 9
        thr2 = view(side, at, 9)
        at += 9
        npf = view(side, at, 2)
        at += 2
        assert at <= 4096 + 3 * KT * T
        at = 4096 + 3 * KT * T
        wr = view(side, at, KT, 36)
        at += 576
        lgb = view(side, at, 36)
        at += 36
        assert at <= 17456, at
        xn2 = trunk[:, 0:3 * D].rearrange("p (t j c) -> p t j c", t=3, j=KT)
        xgT = view(trunk, 3 * D, KT, P)
        ys = view(trunk, 0, D)
        sq_out = view(trunk, 3 * D + KT * P, 512)

        gmixc, gmemc, gffnc = view(small, 0, KT), view(small, 16, KT), view(small, 32, KT)
        pscale = view(small, 48, GG)
        w00 = view(small, 54, GG)
        gffnr = view(small, 228, KT)
        ssm, ssx, ssh = view(small, 60, 2), view(small, 62, 3), view(small, 65, 3)
        ssh4 = view(small, 244, 3, 4)
        rm, rx, rh = view(small, 68, 2), view(small, 70, 3), view(small, 73, 3)
        mx = view(small, 76, 2)
        negm = view(small, 78, 2)
        rs = view(small, 80, 2)
        lmu, lvar = view(small, 82, 3), view(small, 85, 3)
        dg = view(small, 88, GG, TS)
        rc = view(small, 136, 4, 16)
        wsum = view(small, 200, TS)
        tmp16 = view(small, 208, 16)
        smx, snegm, srs = view(small, 224, 1), view(small, 225, 1), view(small, 226, 1)

        full = [sem(f"slot{i}_full") for i in range(6)]
        mem_in, x_in = [sem("mem0_in"), sem("mem1_in")], sem("x_in")
        gcol_in, const_in, ln_in, pool_in = sem("gcol_in"), sem("const_in"), sem("ln_in"), sem("pool_w_in")
        state_in, router_in, gfin_in = sem("state_in"), sem("router_in"), sem("gfin_in")
        cache_in = [sem("cache0_in"), sem("cache1_in")]
        kv_out, gv_out, st_out, y_out = sem("kv_out"), sem("gv_out"), sem("st_out"), sem("y_out")
        z_ready, z_done = sem("z_ready"), sem("z_done")
        aux_ready, aux_done = sem("aux_ready"), sem("aux_done")
        br_ready, merged = sem("br_ready"), sem("merged")
        id_ok, pool_chain, rc_ok = sem("id_ok"), sem("pool_chain"), sem("rc_ok")
        act_chain, dve_chain = sem("act_chain"), sem("dve_chain")
        mem_ss, mem_sqrt, x_ss, x_sqrt = sem("mem_ss"), sem("mem_sqrt"), sem("x_ss"), sem("x_sqrt")
        mem_var, x_var, ln_var, ln_sqrt = sem("mem_var"), sem("x_var"), sem("ln_var"), sem("ln_sqrt")
        xs_ready, ss_zero = sem("xs_ready"), sem("ss_zero")
        ln_done, negm_ready, exp_done = sem("ln_done"), sem("negm_ready"), sem("exp_done")
        ck_used, cv_used = sem("ck_used"), sem("cv_used")
        diff_ready, pad_ok = sem("diff_ready"), sem("pad_ok")
        s_ready, dg_ready = sem("s_ready"), sem("dg_ready")
        merge_step = sem("merge_step")
        h_done, h_var, h_sqrt, xn2_ready = sem("h_done"), sem("h_var"), sem("h_sqrt"), sem("xn2_ready")
        sv_ready, sv_done, lg_ready = sem("sv_ready"), sem("sv_done"), sem("lg_ready")
        raw_full = [sem("raw0_full"), sem("raw1_full")]
        hi_done, lo_done, lo_pool, br_split, x_step = (
            sem("hi_done"), sem("lo_done"), sem("lo_pool"), sem("br_split"), sem("x_step"))
        sp_step, gffnr_in, xn_copied = sem("sp_step"), sem("gffnr_in"), sem("xn_copied")
        lg_exp_in, lg_exp = sem("lg_exp_in"), sem("lg_exp")
        tri_ok, sel_ready, np_ready = sem("tri_ok"), sem("sel_ready"), sem("np_ready")
        e_used, p_ready, p_step, silu_done, h_ready, y_ready = (
            sem("e_used"), sem("p_ready"), sem("p_step"), sem("silu_done"), sem("h_ready"), sem("y_ready"))
        sq_done, f_var, f_sqrt, f_rms = sem("sq_done"), sem("f_var"), sem("f_sqrt"), sem("f_rms")
        y_final, ys_gained, ys_final, x_final = sem("y_final"), sem("ys_gained"), sem("ys_final"), sem("x_final")

        def raw_count(n, g=0):
            if n < N_Z:
                return 16 * (n // 2 + 1)
            if n < N_OUT:
                return g * 96 + (16 * (N_Z // 2) + (96 if n - N_Z >= 6 else 16 * ((n - N_Z) // 2 + 1)))
            return 16 * (N_Z // 2) + 96 * N_GRP + 16 * ((n - N_OUT) // 2 + 1)

        def lo_after(n, g=0):
            if n < POOL_LO:
                return lo_done, PIECES * (n + 1)
            if n < N_Z:
                return lo_pool, PIECES * (n + 1 - POOL_LO)
            return lo_done, g * (8 * PIECES) + PIECES * (n + 1 - N_Z + POOL_LO)

        before = {0: 16, 1: 16, 2: 16, 3: 16, 4: 0, 5: 0}

        def expert_full(c):
            return sum(16 if k < 16 else 32 for k in range(c % ESLOTS, c + 1, ESLOTS))

        win_v = w_in[0].rearrange("(p j) c -> p j c", j=KT)
        wmkv_v = w_mkv[0].rearrange("(p j) c -> p j c", j=KT)
        wo_v = w_o[0].rearrange("(j p) c -> p j c", p=P)
        bra_v = w_br_a[0].rearrange("(j p) c -> p j c", p=P)
        brb_v = w_br_b[0].rearrange("(j p) c -> p j c", p=P)
        brc_v = w_br_c[0].rearrange("(j p) c -> p j c", p=P)
        wg_v = w_gate[0].rearrange("g e (p j) f -> p (g e) (j f)", j=KT)
        wu_v = w_up[0].rearrange("g e (p j) f -> p (g e) (j f)", j=KT)
        wd_v = w_down[0].rearrange("g e (p j) n -> p (g e) (j n)", j=4)

        MKV_SLOT = (1, 0, 3, 2)

        def slot(s):
            return e_slot[s].rearrange("p (j c) -> p j c", j=KT)

        raw = [view(ring, b * KT * P, KT, P) for b in range(2)]

        def early_load(sp, n):
            c0 = Z_COLS[n // 2] + n % 2 * P
            sp.dma_start(raw[n % 2], win_v[:, :, c0:c0 + P]).then_inc(raw_full[n % 2], 16)

        def gate_load(sp, g, u):
            b = u % 2
            src = win_v[:, :, bass.ds(g * CC + (GATE_COL + u // 2 * D + b * P), P)]
            sp.dma_start(raw[b], src).then_inc(raw_full[b], 16)

        def branch_load(sp, cols, b):
            sp.dma_start(raw[b][:, 0:6, :], bra_v[:, :, cols]).then_inc(raw_full[b], 16)
            sp.dma_start(raw[b][:, 6:12, :], brb_v[:, :, cols]).then_inc(raw_full[b], 16)
            sp.dma_start(raw[b][:, 12:16, :], brc_v[:, :, cols]).then_inc(raw_full[b], 16)

        block = ctx.enter_context(nc.Block())

        @block.sync
        def _(sp):
            for t in range(2):
                sp.dma_start(mem[:, t, :], mem_prompt[0, t * P:(t + 1) * P, :]).then_inc(mem_in[t], 16)
            sp.dma_start(slot(MKV_SLOT[0]), wmkv_v[:, :, 0:CC]).then_inc(full[MKV_SLOT[0]], 16)
            sp.dma_start(x[:, 0, :], x_prompt[0, 0:P, :]).then_inc(x_in, 16)
            sp.dma_start(x[:, 1, :], x_prompt[0, P:TP, :]).then_inc(x_in, 16)
            sp.dma_start(x[0:TS, 2, :], x_sample[:, 0, :]).then_inc(x_in, 16)
            for n in range(1, N_MKV):
                sp.dma_start(slot(MKV_SLOT[n]), wmkv_v[:, :, n * CC:(n + 1) * CC]).then_inc(full[MKV_SLOT[n]], 16)
            sp.wait_ge(z_ready, 4)
            for n in range(N_Z + 2):
                if n >= 2:
                    sp.wait_ge(*lo_after(n - 2))
                if n < N_Z:
                    early_load(sp, n)
                else:
                    gate_load(sp, 0, n - N_Z)
            with sp.Fori(0, N_GRP - 1) as g:
                for u in range(2, 10):
                    sp.wait_ge(*lo_after(N_Z + u - 2, g))
                    if u == 6:
                        sp.sem_inc(sp_step, 1)
                    if u in (6, 7):
                        branch_load(sp, bass.ds(g * CC + (u - 6) * P, P), u - 6)
                    else:
                        gate_load(sp, g + u // 8, u % 8)
            for n in range(N_OUT - 6, N_OUT + 16):
                sp.wait_ge(*lo_after(n - 2))
                if n < N_OUT - 2:
                    gate_load(sp, N_GRP - 1, n - (N_OUT - 8))
                elif n < N_OUT:
                    b = n - (N_OUT - 2)
                    branch_load(sp, slice(D - CC + b * P, D - CC + (b + 1) * P), b)
                else:
                    k = n - N_OUT
                    sp.dma_start(raw[k % 2], wo_v[:, :, k * P:(k + 1) * P]).then_inc(raw_full[k % 2], 16)

            def expert_load(c, e0):
                s = EORDER[c % ESLOTS]
                if c < 16:
                    dst = e_slot[s].rearrange("p (e n) -> p e n", e=EPR)
                    src = (wg_v if c < 8 else wu_v)[:, e0, (c % 8) * 1024:(c % 8 + 1) * 1024]
                    sp.dma_start(dst, src).then_inc(full[s], 16)
                else:
                    n, j = (c - 16) // 2, 2 * (c % 2)
                    for i in range(2):
                        dst = e_slot[s].rearrange("p (e j n) -> p e j n", e=EPR, j=2)[:, :, i, :]
                        src = wd_v[:, e0, (j + i) * D + n * 512:(j + i) * D + (n + 1) * 512]
                        sp.dma_start(dst, src).then_inc(full[s], 16)

            for c, (signal, count) in enumerate(((br_ready, 2 * N_GRP), (br_ready, 2 * N_GRP), (br_ready, 2 * N_GRP),
                                                 lo_after(N_OUT + 15), (z_ready, Z_END - 1), (z_ready, Z_END))):
                sp.wait_ge(signal, count)
                expert_load(c, slice(0, EPR))
            sp.wait_ge(np_ready, 1)
            npass = sp.value_load(npass_i[0:1, 0:1], min_val=1, max_val=9)
            with sp.Fori(0, npass) as k:
                with sp.Fori(2, ROUNDS + 1) as r:
                    for c in range(ESLOTS, CPR + ESLOTS):
                        sp.wait_ge(e_used, k * (ROUNDS * CPR) + r * CPR + (c + 1 - 2 * CPR))
                        if c in (8, 16):
                            sp.sem_inc(sp_step, 1)
                        expert_load(c % CPR, bass.ds(r * EPR + EPR * (c // CPR - 2), EPR))
                for c in range(ESLOTS, CPR):
                    sp.wait_ge(e_used, k * (ROUNDS * CPR) + ((ROUNDS - 1) * CPR + c + 1))
                    expert_load(c, slice(NX - EPR, NX))
                with sp.If(k < npass - 1):
                    for c in range(ESLOTS):
                        sp.wait_ge(e_used, k * (ROUNDS * CPR) + (ROUNDS * CPR + c + 1))
                        expert_load(c, slice(0, EPR))
                sp.nop()
            for i in range(4):
                t, cols = i // 2, slice(i % 2 * 1024, (i % 2 + 1) * 1024)
                sp.wait_ge(y_final, i + 1)
                sp.dma_start(y_prompt[0, t * P:(t + 1) * P, cols], x[:, t, cols]).then_inc(y_out, 16)
            sp.wait_ge(ys_final, 1)
            sp.dma_start(y_sample[:, 0, :], ys[0:TS, :]).then_inc(y_out, 16)
            sp.wait_ge(y_out, 80)

        @block.gpsimd
        def _(pool):
            nc.gpsimd.memset(ident[:, :], 0.0).then_inc(pool_chain, 1)
            pool.wait_ge(pool_chain, 1)
            nc.gpsimd.affine_select(out=ident[:, :], in_=ident[:, :], compare_op=ALU.not_equal, fill=1.0, base=0,
                                    pattern=[[-1, P]], channel_multiplier=1).then_inc(id_ok, 1)
            for t in range(2):
                pool.wait_ge(mem_in[t], 16)
            row = lambda a, n: a.rearrange("(o n) -> o n", o=1).to_broadcast([n, a.shape[0]])
            pool.dma_start(wsN, w_s[0].rearrange("g i j -> i g j")).then_inc(const_in, 16)
            pool.dma_start(bs, b_s[0].rearrange("(o g) i -> o g i", o=1).to_broadcast([P, GG, P])).then_inc(const_in, 16)
            with nc.allow_non_contiguous_dma(reason="a few hundred words of per-channel constants"):
                pool.dma_start(pscale, pool_scale[0].rearrange("(k p) -> p k", p=P)).then_inc(const_in, 16)
                pool.dma_start(w00[0:TS, :], w_s[0, :, 0, 0:1].rearrange("(o g) a -> o (g a)", o=1)
                               .to_broadcast([TS, GG])).then_inc(const_in, 16)
            for g in range(4):
                b0 = 3 * (g // 2)
                if g % 2 == 0:
                    pool.dma_start(wp[:, b0, :], w_pool[0, g, 0:P, :]).then_inc(pool_in, 16)
                    pool.dma_start(wp[0:64, b0 + 1, :], w_pool[0, g, P:PG, :]).then_inc(pool_in, 16)
                else:
                    pool.dma_start(wp[64:P, b0 + 1, :], w_pool[0, g, 0:64, :]).then_inc(pool_in, 16)
                    pool.dma_start(wp[:, b0 + 2, :], w_pool[0, g, 64:PG, :]).then_inc(pool_in, 16)
            nc.gpsimd.iota(rc, pattern=[[0, 4], [1, 16]], base=1, channel_multiplier=0,
                           allow_small_or_imprecise_dtypes=True).then_inc(rc_ok, 1)
            pool.wait_ge(const_in, 64)
            nc.gpsimd.affine_select(out=wsN, in_=wsN, compare_op=ALU.is_ge, fill=0.0, base=0,
                                    pattern=[[0, GG], [-1, P]], channel_multiplier=1).then_inc(pool_chain, 1)
            pool.dma_start(new_st_s[0, :, 0:NST - 1, :], state_pool[0, :, 1:NST, :]).then_inc(st_out, 16)
            with nc.allow_non_contiguous_dma(reason="2048 gains"):
                pool.dma_start(gffnr, g_ffn[0].rearrange("(j p) -> p j", p=P)).then_inc(gffnr_in, 16)
            pool.wait_ge(aux_ready, A_MEM + 8)
            pool.dma_start(stN[0:TS * NST, :], state_pool[0].rearrange("b t c -> (b t) c")).then_inc(state_in, 16)
            pool.wait_ge(z_done, Z_V)
            pool.dma_start(lng, row(ln_v_g[0], P)).then_inc(ln_in, 16)
            pool.dma_start(lnb, row(ln_v_b[0], P)).then_inc(ln_in, 16)
            for t in range(2):
                pool.dma_start(new_k[0, 0, t * P:(t + 1) * P].rearrange("m h d -> m (h d)"), kvK[:, t, :]).then_inc(kv_out, 16)
                pool.dma_start(new_v[0, 0, t * P:(t + 1) * P].rearrange("m h d -> m (h d)"), kvV[:, t, :]).then_inc(kv_out, 16)

            def split_lo_here(n):
                for p in range(PIECES):
                    js = slice(p * KT // PIECES, (p + 1) * KT // PIECES)
                    pool.wait_ge(hi_done, PIECES * n + (p + 1))
                    nc.gpsimd.tensor_tensor(w_lo[n % 2][:, js, :], raw[n % 2][:, js, :], w_hi[n % 2][:, js, :],
                                            ALU.subtract).then_inc(lo_pool, 1)

            def cache_load(i):
                if 2 <= i < TS + 2:
                    pool.wait_ge(ck_used, i - 1)
                elif i >= TS + 2:
                    pool.wait_ge(cv_used, i - TS - 1)
                src = (cache_k if i < TS else cache_v)[0, i % TS].rearrange("(p m) h d -> p m (h d)", m=2)
                pool.dma_start(cache_flat[i % 2], src).then_inc(cache_in[i % 2], 16)

            cache_load(0)
            cache_load(1)
            for n in range(POOL_LO, 14):
                split_lo_here(n)
            pool.wait_ge(ln_done, 1)
            pool.dma_start(new_gv[0, :, 0, :], vN[0:TS, 2, :]).then_inc(gv_out, 16)
            for i, split in zip(range(2 * TS), LO_AFTER_LOAD):
                if i >= 2:
                    cache_load(i)
                for n in split:
                    split_lo_here(n)
            pool.wait_ge(aux_done, A_PN + 2)
            pool.dma_start(new_st_p[0, 0], pn[0:NST, :]).then_inc(st_out, 16)
            pool.dma_start(new_st_s[0, :, NST - 1, :], pn[NST:NST + TS, :]).then_inc(st_out, 16)
            pool.wait_ge(st_out, 48)
            pool.wait_ge(kv_out, 64)
            pool.wait_ge(gv_out, 16)
            pool.wait_ge(aux_done, A_PL + 6)
            pool.wait_ge(sv_ready, 1)
            with nc.allow_non_contiguous_dma(reason="router weights, d = (j p)"):
                pool.dma_start(wr[:, :, 0:NG], w_rg[0].rearrange("(j p) g -> p j g", p=P)).then_inc(router_in, 16)
                for g in range(NG):
                    pool.dma_start(wr[:, :, NG + g * NE:NG + (g + 1) * NE],
                                   w_re[0, g].rearrange("(j p) e -> p j e", p=P)).then_inc(router_in, 16)
            pool.dma_start(lgb[:, 0:NG], row(b_rg[0], P)).then_inc(router_in, 16)
            pool.dma_start(lgb[:, NG:36], row(b_re[0].rearrange("g e -> (g e)"), P)).then_inc(router_in, 16)
            pool.wait_ge(sv_done, 1)
            nc.gpsimd.tensor_copy(br_hi, brT).then_inc(br_split, 1)
            pool.wait_ge(br_split, 1)
            nc.gpsimd.tensor_tensor(br_lo, brT, br_hi, ALU.subtract).then_inc(br_split, 1)
            pool.wait_ge(br_ready, 2 * N_GRP)
            nc.gpsimd.memset(comb, 0.0).then_inc(tri_ok, 1)
            nc.gpsimd.memset(sel, 0.0).then_inc(tri_ok, 1)
            nc.gpsimd.memset(lg, 0.0).then_inc(tri_ok, 1)
            pool.dma_start(gfin, row(g_final, P)).then_inc(gfin_in, 16)
            nc.gpsimd.iota(cidx, pattern=[[1, CAP]], base=0, channel_multiplier=0,
                           allow_small_or_imprecise_dtypes=True).then_inc(tri_ok, 1)
            nc.gpsimd.iota(rev, pattern=[[-1, NE]], base=NE, channel_multiplier=0,
                           allow_small_or_imprecise_dtypes=True).then_inc(tri_ok, 1)
            nc.gpsimd.iota(thr, pattern=[[CAP, 9]], base=0, channel_multiplier=0,
                           allow_small_or_imprecise_dtypes=True).then_inc(tri_ok, 1)
            nc.gpsimd.memset(ones, 1.0).then_inc(pool_chain, 1)
            pool.wait_ge(pool_chain, 3)
            nc.gpsimd.affine_select(out=tri, in_=ones, compare_op=ALU.is_gt, fill=0.0, base=0,
                                    pattern=[[1, P]], channel_multiplier=-1).then_inc(tri_ok, 1)
            pool.wait_ge(x_final, 1)
            pool.wait_ge(gfin_in, 16)
            nc.gpsimd.tensor_tensor(ys[0:TS, :], x[0:TS, 2, :], gfin[0:TS, :], ALU.mult).then_inc(ys_gained, 1)

        @block.scalar
        def _(act):
            with nc.allow_non_contiguous_dma(reason="per-channel gains, 64 bytes a partition"):
                act.dma_start(gmemc, g_mem[0].rearrange("(p j) -> p j", j=KT)).then_inc(gcol_in, 16)
                act.dma_start(gmixc, g_mix[0].rearrange("(p j) -> p j", j=KT)).then_inc(gcol_in, 16)
                act.dma_start(gffnc, g_ffn[0].rearrange("(p j) -> p j", j=KT)).then_inc(gcol_in, 16)
            chain = [0]

            def link(ins):
                chain[0] += 1
                ins.then_inc(act_chain, 1)
                act.wait_ge(act_chain, chain[0])

            act.wait_ge(ss_zero, 2)
            for t in range(2):
                act.wait_ge(mem_in[t], 16)
                link(nc.scalar.activation(trunk[:, 0:D], mem[:, t, :], ACT.Square, accum_out=ssm[:, t:t + 1]))
                act.wait_ge(mem_var, t + 1)
                nc.scalar.activation(rm[:, t:t + 1], ssm[:, t:t + 1], ACT.Sqrt).then_inc(mem_sqrt, 1)
            act.wait_ge(x_in, 48)
            for t, (_, n) in enumerate(TILES):
                link(nc.scalar.activation(trunk[0:n, 0:D], x[0:n, t, :], ACT.Square, accum_out=ssx[0:n, t:t + 1]))
            act.wait_ge(x_var, 1)
            nc.scalar.activation(rx, ssx, ACT.Sqrt).then_inc(x_sqrt, 1)

            def take_z(n):
                act.wait_ge(z_ready, n + 1)
                return bank[n % 2]

            def split_hi(b, count, used):
                act.wait_ge(raw_full[b], count)
                act.wait_ge(*used)
                for p in range(PIECES):
                    js = slice(p * KT // PIECES, (p + 1) * KT // PIECES)
                    nc.scalar.activation(w_hi[b][:, js, :], raw[b][:, js, :], ACT.Copy).then_inc(hi_done, 1)

            def next_hi(n):
                k = n - Z_V + 2
                split_hi(k % 2, raw_count(k), (z_ready, n + 1))

            for n in range(Z_V):
                if n == Z_V - 2:
                    split_hi(0, raw_count(0), (z_ready, Z_V - 2))
                ps, c, t = take_z(n), n // 2, n % 2
                dst = (kvK if c < 2 else kvV)[:, t, (c % 2) * CC:(c % 2 + 1) * CC]
                nc.scalar.activation(dst, ps[:, 0:CC], ACT.Copy).then_inc(z_done, 1)
            split_hi(1, raw_count(1), (z_ready, Z_V))
            for n in range(Z_V, Z_Q):
                next_hi(n)
                nc.scalar.activation(vT[:, n - Z_V, :], take_z(n)[:, 0:T], ACT.Gelu).then_inc(z_done, 1)
            for n in range(Z_Q, Z_P):
                next_hi(n)
                nc.scalar.activation(qT[:, n - Z_Q, :], take_z(n)[:, 0:T], ACT.Copy).then_inc(z_done, 1)
            for n in range(Z_P, Z_U):
                if n == Z_P + LN_SQRT:
                    act.wait_ge(ln_var, 1)
                    nc.scalar.activation(lvar, lvar, ACT.Sqrt).then_inc(ln_sqrt, 1)
                next_hi(n)
                nc.scalar.activation(pT[:, n - Z_P, PAD:PAD + T], take_z(n)[:, 0:T], ACT.Copy).then_inc(z_done, 1)

            def quarter_squares(q):
                act.wait_ge(h_done, q + 1)
                for t, (_, n) in enumerate(TILES):
                    link(nc.scalar.activation(trunk[0:n, 0:512], x[0:n, t, 512 * q:512 * (q + 1)], ACT.Square,
                                              accum_out=ssh4[0:n, t, q:q + 1]))

            def exp_head(hd):
                act.wait_ge(negm_ready, hd + 1 + (hd > 1))
                if hd == 0:
                    act.wait_ge(kv_out, 64)
                ps = bank[2 + A_SC[hd] % AUX]
                for t in range(2):
                    ins = nc.scalar.activation(Pp[hd % 2][t],
                                               ps[:, t * NM:(t + 1) * NM], ACT.Exp, bias=negm[:, t:t + 1],
                                               scale=SCALE, accum_out=rs[:, t:t + 1])
                    if t == 0:
                        link(ins)
                ins.then_inc(exp_done, 1)

            def take_u(n):
                next_hi(n)
                nc.scalar.activation(brT[:, n - Z_U, :], take_z(n)[:, 0:T], ACT.Gelu).then_inc(z_done, 1)

            exp_head(0)
            exp_head(1)
            act.wait_ge(negm_ready, 3)
            nc.scalar.activation(Ps[0:32, :], bank[2 + A_SS % AUX][0:32, 0:256], ACT.Exp, bias=snegm[0:32],
                                 scale=SCALE, accum_out=srs[0:32]).then_inc(exp_done, 1)
            take_u(Z_U)
            take_u(Z_U + 1)
            exp_head(2)
            exp_head(3)
            for n in range(Z_U + 2, Z_G):
                take_u(n)
            with act.Fori(0, N_GRP) as g:
                for u in range(8):
                    used = (z_ready, g * 6 + (Z_G + u + 1)) if u < 6 else (br_ready, g * 2 + (u - 5))
                    split_hi(u % 2, raw_count(N_Z + (u + 2) % 8, g + (u + 2) // 8), used)
                    if u < 2:
                        act.wait_ge(merged, g * 2 + (u + 1))
                    if u < 6:
                        nc.scalar.activation(sg[:, u % 2, u // 2, :], bank[u % 2][:, 0:T], ACT.Sigmoid).then_inc(z_done, 1)
            act.wait_ge(merged, 2 + 2 * N_GRP)
            for n in range(Z_O, Z_END):
                ps = take_z(n)
                b = n - Z_O
                if b < 14:
                    split_hi(b % 2, raw_count(N_OUT + b + 2), (z_ready, n + 1))
                if b >= 2:
                    act.wait_ge(aux_ready, A_O[b - 2] + 1)
                nc.scalar.activation(oT[:, b % 2, :], ps[:, 0:T], ACT.Copy).then_inc(z_done, 1)
                if b % 4 == 1 and b > 4:
                    quarter_squares(b // 4 - 1)
            quarter_squares(3)
            act.wait_ge(h_var, 1)
            nc.scalar.activation(rh, ssh, ACT.Sqrt).then_inc(h_sqrt, 1)
            act.wait_ge(lg_exp_in, 1)
            nc.scalar.activation(r4[0], r4[0], ACT.Exp).then_inc(lg_exp, 1)
            act.wait_ge(lg_exp_in, 2)
            nc.scalar.activation(r1[5], r1[5], ACT.Exp).then_inc(lg_exp, 1)
            act.wait_ge(xn2_ready, 1)
            for t, (_, n) in enumerate(TILES):
                nc.scalar.activation(xn2[0:n, t].rearrange("p j c -> p c j"), x[0:n, t, :].rearrange("p (c j) -> p c j", j=KT),
                                     ACT.Copy, scale=rh[0:n, t:t + 1]).then_inc(xn_copied, 1)
            act.wait_ge(np_ready, 1)
            npass = act.value_load(npass_i[0:1, 0:1], min_val=1, max_val=9)
            with act.Fori(0, npass) as k:
                with act.Fori(0, ROUNDS) as r:
                    it = k * ROUNDS + r
                    act.wait_ge(e_used, it * CPR + (CREDIT + 8))
                    nc.scalar.activation(hs, bank[0][:, :], ACT.Silu).then_inc(silu_done, 1)
                    for n in range(4):
                        act.wait_ge(e_used, it * CPR + (CREDIT + 18 + 2 * n))
                        nc.scalar.activation(y[:, n, :], bank[2 + n][:, :], ACT.Copy).then_inc(y_ready, 1)
                        for t, (_, cnt) in enumerate(TILES):
                            q = 3 * n + t
                            act.wait_ge(aux_done, it * JPR + (A_E + 7 + q))
                            act.wait_ge(sq_done, it * 12 + (q + 1))
                            nc.scalar.activation(sq_out[0:cnt, :], x[0:cnt, t, n * 512:(n + 1) * 512], ACT.Square,
                                                 accum_out=ssh4[0:cnt, t, n:n + 1]).then_inc(sq_done, 1)
            act.wait_ge(f_var, 1)
            nc.scalar.activation(rx, ssx, ACT.Sqrt).then_inc(f_sqrt, 1)
            act.wait_ge(f_rms, 1)
            act.wait_ge(ys_gained, 1)
            nc.scalar.activation(ys[0:TS, :], ys[0:TS, :], ACT.Copy, scale=rx[0:TS, 2:3]).then_inc(ys_final, 1)

        @block.vector
        def _(dve):
            chain = [0]

            def link(ins):
                chain[0] += 1
                ins.then_inc(dve_chain, 1)
                dve.wait_ge(dve_chain, chain[0])

            def take(job):
                dve.wait_ge(aux_ready, job + 1)
                return bank[2 + job % AUX]

            V = nc.vector
            nc.vector.memset(small[:, 60:68], 1.0).then_inc(ss_zero, 1)
            V.memset(pT[:, :, 0:PAD], 0.0).then_inc(pad_ok, 1)
            V.memset(ssh4, 1.0).then_inc(ss_zero, 1)
            V.memset(rs, 1.0).then_inc(sq_done, 1)
            V.memset(rx, 1.0).then_inc(merged, 2)
            V.memset(rm, 1.0).then_inc(e_used, CREDIT)

            def mean_eps(ss, n, done):
                V.tensor_scalar(ss, ss, 1.0 / n, EPS, ALU.mult, ALU.add).then_inc(done, 1)

            def split_lo(n, g=0):
                for p in range(PIECES):
                    js = slice(p * KT // PIECES, (p + 1) * KT // PIECES)
                    dve.wait_ge(hi_done, g * (8 * PIECES) + (PIECES * n + p + 1))
                    V.tensor_tensor(w_lo[n % 2][:, js, :], raw[n % 2][:, js, :], w_hi[n % 2][:, js, :],
                                    ALU.subtract).then_inc(lo_done, 1)

            xp = view(side, 7168, 2, 512)

            def split_x(job, ins_of, hi, lo):
                k = job - A_X
                p = xp[:, k % 2, :] if k < 8 else xp[:, 0, 0:P]
                p = p.rearrange("p (j t) -> p j t", j=hi.shape[1])
                ins_of(p).then_inc(x_step, 1)
                dve.wait_ge(x_step, 2 * k + 1)
                V.tensor_copy(hi, p).then_inc(x_step, 1)
                dve.wait_ge(x_step, 2 * k + 2)
                V.tensor_tensor(lo, p, hi, ALU.subtract).then_inc(aux_done, 1)

            def take_x4(job, q, t0):
                ps = take(job)
                if job > A_X + 1:
                    dve.wait_ge(aux_done, job - 1)
                js = slice(4 * q, 4 * q + 4)
                split_x(job, lambda p: V.tensor_tensor(p, ps[:, :].rearrange("p (j t) -> p j t", j=4),
                                                       gmixc[:, js].unsqueeze(2).to_broadcast([P, 4, P]), ALU.mult),
                        xn_hi[:, js, t0:t0 + P], xn_lo[:, js, t0:t0 + P])

            for t in range(2):
                dve.wait_ge(act_chain, t + 1)
                mean_eps(ssm[:, t:t + 1], D, mem_var)
                dve.wait_ge(mem_sqrt, t + 1)
                link(V.reciprocal(rm[:, t:t + 1], rm[:, t:t + 1]))
                V.tensor_scalar(xs[:, t, :], mem[:, t, :], rm[:, t:t + 1], None, ALU.mult).then_inc(xs_ready, 1)

            def take_t4(job, dst, gain, q, t0):
                ps = take(job)
                V.tensor_tensor(dst[:, 4 * q:4 * q + 4, t0:t0 + P], ps[:, :].rearrange("p (j t) -> p j t", j=4),
                                gain[:, 4 * q:4 * q + 4].unsqueeze(2).to_broadcast([P, 4, P]), ALU.mult).then_inc(aux_done, 1)

            dve.wait_ge(gcol_in, 48)
            for q in range(4):
                take_t4(A_MEM + q, memT, gmemc, q, 0)
            for q in range(4):
                take_t4(A_MEM + 4 + q, memT, gmemc, q, P)
            dve.wait_ge(act_chain, 5)
            mean_eps(ssx, D, x_var)
            dve.wait_ge(x_sqrt, 1)
            link(V.reciprocal(rx, rx))
            V.tensor_scalar(xs[:, 0, :], x[:, 0, :], rx[:, 0:1], None, ALU.mult).then_inc(xs_ready, 1)
            V.tensor_scalar(xs[:, 1, :], x[:, 1, :], rx[:, 1:2], None, ALU.mult).then_inc(xs_ready, 1)
            for q in range(4):
                take_x4(A_X + q, q, 0)
            V.tensor_scalar(xs[0:TS, 0, :], x[0:TS, 2, :], rx[0:TS, 2:3], None, ALU.mult).then_inc(xs_ready, 1)
            for q in range(4):
                take_x4(A_X + 4 + q, q, P)
            ps = take(A_X + 8)
            dve.wait_ge(aux_done, A_X + 7)
            split_x(A_X + 8, lambda p: V.tensor_tensor(p, ps[:, 0:P].rearrange("p (j t) -> p j t", j=KT),
                                                       gmixc.unsqueeze(2).to_broadcast([P, KT, TS]), ALU.mult),
                    xn_hi[:, :, TP:T], xn_lo[:, :, TP:T])
            for n in range(8):
                split_lo(n)
            for hd in range(NH):
                ps = take(A_KT + hd)
                V.tensor_copy(kT[:, hd, :], ps[:, 0:NM]).then_inc(aux_done, 1)
            dve.wait_ge(const_in, 64)
            dve.wait_ge(id_ok, 1)
            V.tensor_tensor(dg[0:TS], ident[0:TS, 0:TS].unsqueeze(1).to_broadcast([TS, GG, TS]),
                            w00[0:TS, :].unsqueeze(2).to_broadcast([TS, GG, TS]), ALU.mult).then_inc(dg_ready, 1)
            split_lo(8)
            split_lo(9)
            for i in range(2):
                ps, n = take(A_WS + i), 4 - 2 * i
                V.tensor_copy(wsT[:, 4 * i:4 * i + n, :].rearrange("p g i -> p (g i)"), ps[:, 0:n * P]).then_inc(aux_done, 1)
            for t, (_, n) in enumerate(TILES):
                for i in range(2):
                    ps, w = take(A_VN + 2 * t + i), 512 - 256 * i
                    V.tensor_copy(vN[0:n, t, 512 * i:512 * i + w], ps[0:n, 0:w]).then_inc(aux_done, 1)
            ps = take(A_QN)
            V.tensor_copy(qn[0:TS, :], ps[0:TS, 0:512]).then_inc(aux_done, 1)
            link(V.memset(small[:, 82:88], 1.0))
            dve.wait_ge(aux_done, A_VN + 6)
            dve.wait_ge(ln_in, 32)
            dve.wait_ge(aux_ready, A_WS + 2)
            for t, (_, n) in enumerate(TILES):
                v = vN[0:n, t, :]
                link(V.tensor_reduce(lmu[0:n, t:t + 1], v, AX.X, ALU.add))
                link(V.tensor_scalar(lmu[0:n, t:t + 1], lmu[0:n, t:t + 1], -1.0 / BW, None, ALU.mult))
                link(V.tensor_scalar(v, v, lmu[0:n, t:t + 1], None, ALU.add))
                ins = V.tensor_tensor_reduce(out=prod_flat[0:n, 0:BW], in0=v, in1=v, scale=1.0, scalar=0.0,
                                             op0=ALU.mult, op1=ALU.add, accum_out=lvar[0:n, t:t + 1])
                link(ins)
            V.tensor_scalar(lvar, lvar, 1.0 / BW, EPS, ALU.mult, ALU.add).then_inc(ln_var, 1)
            dve.wait_ge(ln_sqrt, 1)
            link(V.reciprocal(lvar, lvar))
            for t, (_, n) in enumerate(TILES):
                v = vN[0:n, t, :]
                link(V.scalar_tensor_tensor(out=v, in0=v, scalar=lvar[0:n, t:t + 1], in1=lng[0:n, :],
                                            op0=ALU.mult, op1=ALU.mult))
                ins = V.tensor_tensor(v, v, lnb[0:n, :], ALU.add)
                if t < 2:
                    link(ins)
            ins.then_inc(ln_done, 1)
            def head_max(hd):
                ps = take(A_SC[hd])
                link(V.tensor_reduce(mx, ps[:, :].rearrange("p (t m) -> p t m", t=2), AX.X, ALU.max))
                V.tensor_scalar(negm, mx, -SCALE, None, ALU.mult).then_inc(negm_ready, 1)

            def head_norm(hd):
                dve.wait_ge(exp_done, hd + 1 + (hd > 1))
                link(V.reciprocal(rs, rs))
                link(V.tensor_scalar(Pp[hd % 2][0], Pp[hd % 2][0], rs[:, 0:1], None, ALU.mult))
                V.tensor_scalar(Pp[hd % 2][1], Pp[hd % 2][1], rs[:, 1:2], None, ALU.mult).then_inc(aux_done, 1)

            def head_out(hd):
                ps = take(A_HEAD[hd])
                V.tensor_copy(PpT_flat[hd % 2], ps[:, :]).then_inc(aux_done, 1)
                ps = take(A_HEAD[hd] + 1)
                V.tensor_copy(brT[:, 12 + hd, 0:TP], ps[:, 0:TP]).then_inc(aux_done, 1)

            for b in range(TS):
                dve.wait_ge(cache_in[b % 2], 16 * (b // 2 + 1))
                ps = take(A_QB + b)
                if b:
                    dve.wait_ge(ck_used, b)
                V.tensor_tensor(prod, cache[b % 2], ps[:, :].unsqueeze(1).to_broadcast([P, 2, 512]),
                                ALU.mult).then_inc(aux_done, 1)
                dve.wait_ge(aux_done, A_QB + b + 1)
                V.tensor_reduce(sT[:, :, 4 * b:4 * b + 4], prod.rearrange("p m (h d) -> p m h d", h=NH),
                                AX.X, ALU.add).then_inc(ck_used, 1)
            head_max(0)
            head_norm(0)
            head_max(1)
            head_norm(1)
            for i in range(2):
                ps, n = take(A_ST + i), 4 - 2 * i
                V.tensor_copy(ext[:, 4 * i:4 * i + n, :, 0:NST],
                              ps[:, 0:n * 120].rearrange("p (k b t) -> p k b t", k=n, b=TS)).then_inc(aux_done, 1)
            dve.wait_ge(z_done, Z_U)
            link(V.tensor_copy(ext[:, :, :, NST], pT[:, :, PAD + TP:PAD + T]))
            ps = take(A_SS)
            link(V.tensor_reduce(smx[0:32], ps[0:32, 0:256], AX.X, ALU.max))
            V.tensor_scalar(snegm[0:32], smx[0:32], -SCALE, None, ALU.mult).then_inc(negm_ready, 1)
            dve.wait_ge(exp_done, 3)
            link(V.reciprocal(srs[0:32], srs[0:32]))
            V.tensor_scalar(Ps[0:32, :], Ps[0:32, :], srs[0:32], None, ALU.mult).then_inc(aux_done, 1)
            dve.wait_ge(pad_ok, 1)
            link(V.tensor_tensor(stA[:, :, 1:272], pT[:, :, 1:272], pT[:, :, 0:271], ALU.add))
            dve.wait_ge(rc_ok, 1)
            for g, w in enumerate(WINDOWS):
                link(V.tensor_scalar(rc[:, g, :], rc[:, g, :], float(w), None, ALU.min))
            link(V.reciprocal(rc, rc))
            ps = take(A_SP)
            V.tensor_copy(PsT.rearrange("p m c -> p (m c)"), ps[:, 0:64]).then_inc(aux_done, 1)

            def pool_group(g, src, other):
                w = WINDOWS[g]
                if g:
                    b0 = (1, 3, 4)[g - 1]
                    lo = w - 1
                    link(V.tensor_tensor(other[:, b0:, lo:272], src[:, b0:, lo:272], src[:, b0:, lo - w // 2:272 - w // 2],
                                         ALU.add))
                    src, other = other, src
                b0 = 3 * (g // 2)
                pieces = ((b0, 0, P), (b0 + 1, 0, 64)) if g % 2 == 0 else ((b0 + 1, 64, P), (b0 + 2, 0, P))
                for k, p0, p1 in pieces:
                    V.scalar_tensor_tensor(out=diff[p0:p1, k, PAD:TP], in0=src[p0:p1, k, 2 * PAD:PAD + TP], scalar=1.0 / w,
                                           in1=pT[p0:p1, k, 2 * PAD:PAD + TP], op0=ALU.mult, op1=ALU.subtract)
                    link(V.tensor_tensor(tmp16[p0:p1, :], src[p0:p1, k, PAD:2 * PAD], rc[p0:p1, g, :], ALU.mult))
                    link(V.tensor_tensor(diff[p0:p1, k, 0:PAD], tmp16[p0:p1, :], pT[p0:p1, k, PAD:2 * PAD], ALU.subtract))
                    link(V.tensor_reduce(wsum[p0:p1, :], ext[p0:p1, k, :, PAD - w:PAD], AX.X, ALU.add))
                    link(V.scalar_tensor_tensor(out=diff[p0:p1, k, TP:T], in0=wsum[p0:p1, :], scalar=1.0 / w,
                                                in1=pT[p0:p1, k, PAD + TP:PAD + T], op0=ALU.mult, op1=ALU.subtract))
                return src, other

            sums = pool_group(0, stA, stB)
            sums = pool_group(1, *sums)
            for hd in range(NH):
                head_out(hd)
                if hd + 2 < NH:
                    head_max(hd + 2)
                    head_norm(hd + 2)
            for i in range(2):
                ps, w = take(A_PN + i), 512 - 256 * i
                V.tensor_copy(pn[0:NST + TS, 512 * i:512 * i + w], ps[0:NST + TS, 0:w]).then_inc(aux_done, 1)
            sums = pool_group(2, *sums)
            pool_group(3, *sums)
            dve.nop().then_inc(diff_ready, 1)

            split_lo(N_Z)
            dve.wait_ge(z_done, Z_G)
            dve.wait_ge(const_in, 64)
            for t in range(2):
                for i in range(2):
                    ps, g0, n = take(A_MX + 2 * t + i), 4 * i, 4 - 2 * i
                    link(V.tensor_tensor(mixt[:, 0:n, :], ps[:, 0:n * P].rearrange("p (g i) -> p g i", g=n),
                                         bs[:, g0:g0 + n, :], ALU.add))
                    u = brT[:, g0:g0 + n, t * P:(t + 1) * P]
                    V.tensor_tensor(u, u, mixt[:, 0:n, :], ALU.mult).then_inc(aux_done, 1)
                    dve.wait_ge(aux_done, A_MX + 2 * t + i + 1)
            ps = take(A_MX + 4)
            m8 = prod_flat[:, 0:GG * TS].rearrange("p (g t) -> p g t", g=GG)
            link(V.tensor_tensor(m8, ps[:, 0:GG * TS].rearrange("p (g t) -> p g t", g=GG),
                                 bs[:, :, 0:1].to_broadcast([P, GG, TS]), ALU.add))
            V.tensor_tensor(brT[:, 0:GG, TP:T], brT[:, 0:GG, TP:T], m8, ALU.mult).then_inc(aux_done, 1)
            for k in range(GG):
                ps = take(A_PL + k)
                V.tensor_scalar(brT[:, GG + k, :], ps[:, 0:T], pscale[:, k:k + 1], None, ALU.mult).then_inc(aux_done, 1)

            dve.wait_ge(sv_ready, 1)
            V.tensor_copy(brT[:, 12:16, TP:T], bank[7][:, 0:32].rearrange("p (h b) -> p h b", h=NH)).then_inc(sv_done, 1)

            split_lo(N_Z + 1)

            with dve.Fori(0, N_GRP) as g:
                for u in range(2, 8):
                    split_lo(N_Z + u, g)
                for b in range(2):
                    split_lo(N_Z + 8 + b, g)
                    dve.wait_ge(z_done, g * 6 + (Z_G + 5 + b))
                    dve.wait_ge(br_ready, g * 2 + (b + 1))
                    if b == 1:
                        dve.wait_ge(merged, g * 2 + 3)
                    else:
                        dve.wait_ge(merged, g * 2 + 2)
                    for i in range(3):
                        V.tensor_tensor(gp[:, i, :], sg[:, b, i, :], bank[2 + 3 * b + i][:, 0:T], ALU.mult).then_inc(merge_step, 1)
                    dve.wait_ge(merge_step, g * 12 + (6 * b + 3))
                    V.tensor_tensor(gp[:, 3, :], gp[:, 0, :], gp[:, 1, :], ALU.add).then_inc(merge_step, 1)
                    dve.wait_ge(merge_step, g * 12 + (6 * b + 4))
                    V.tensor_tensor(gp[:, 0, :], gp[:, 3, :], gp[:, 2, :], ALU.add).then_inc(merge_step, 1)
                    dve.wait_ge(merge_step, g * 12 + (6 * b + 5))
                    if b == 0:
                        dve.wait_ge(br_split, 2)
                    V.tensor_copy(mg_hi_f[:, bass.ds(g * (2 * T) + b * T, T)], gp[:, 0, :]).then_inc(merge_step, 1)
                    dve.wait_ge(merge_step, g * 12 + (6 * b + 6))
                    V.tensor_tensor(mg_lo_f[:, bass.ds(g * (2 * T) + b * T, T)], gp[:, 0, :],
                                    mg_hi_f[:, bass.ds(g * (2 * T) + b * T, T)], ALU.subtract).then_inc(merged, 1)

            dve.wait_ge(gffnr_in, 16)

            def take_r(b):
                ps = take(A_R[b])
                if b >= 2:
                    dve.wait_ge(lg_ready, b - 1)
                V.tensor_scalar(hgT[:, b % 2, :], ps[:, 0:T], gffnr[:, b:b + 1], None, ALU.mult).then_inc(aux_done, 1)

            split_lo(N_OUT + 2)
            for b in range(KT):
                if b + 3 < KT:
                    split_lo(N_OUT + b + 3)
                ps = take(A_O[b])
                cols = slice(b * P, (b + 1) * P)
                link(V.tensor_tensor(x[0:TS, 2, cols], x[0:TS, 2, cols], ps[0:TS, 2 * P:3 * P], ALU.add))
                V.tensor_tensor(x[:, 0:2, cols], x[:, 0:2, cols], ps[:, 0:2 * P].rearrange("p (t c) -> p t c", t=2),
                                ALU.add).then_inc(aux_done, 1)
                if b % 4 == 3:
                    dve.wait_ge(aux_done, A_O[b] + 1)
                    dve.nop().then_inc(h_done, 1)
                if b:
                    take_r(b - 1)
            take_r(KT - 1)
            dve.wait_ge(act_chain, 2 + 3 + NH + 12)
            link(V.tensor_reduce(ssh, ssh4, AX.X, ALU.add))
            V.tensor_scalar(ssh, ssh, 1.0 / D, EPS, ALU.mult, ALU.add).then_inc(h_var, 1)
            dve.wait_ge(h_sqrt, 1)
            V.reciprocal(rh, rh).then_inc(xn2_ready, 1)
            dve.wait_ge(lg_ready, KT)
            V.tensor_copy(lgT[0:36, :], bank[7][0:36, 0:T]).then_inc(xn2_ready, 1)

            dve.wait_ge(xn2_ready, 1)
            dve.wait_ge(router_in, 16 * 7)
            dve.wait_ge(tri_ok, 7)
            ps = take(A_LT)
            for t, (_, n) in enumerate(TILES):
                ins = V.scalar_tensor_tensor(out=lg[0:n, t, :], in0=ps[0:n, t * 36:(t + 1) * 36], scalar=rh[0:n, t:t + 1],
                                             in1=lgb[0:n, :], op0=ALU.mult, op1=ALU.add)
                if t < 2:
                    link(ins)
            ins.then_inc(aux_done, 1)
            dve.wait_ge(aux_done, A_LT + 1)

            def over(a, n):
                return a.unsqueeze(2).to_broadcast([P, 3, n])

            def first_max(vals, n, m, eq, key, km, hot):
                link(V.tensor_reduce(m, vals, AX.X, ALU.max))
                link(V.tensor_tensor(eq, vals, over(m, n), ALU.is_equal))
                link(V.tensor_tensor(key, eq, rev[:, 0:n].unsqueeze(1).to_broadcast([P, 3, n]), ALU.mult))
                link(V.tensor_reduce(km, key, AX.X, ALU.max))
                link(V.tensor_tensor(hot, key, over(km, n), ALU.is_equal))

            gl = lg[:, :, 0:NG]
            gmax, km, gsum, m1, m2, dm, den, w1, w2 = r1[0], r1[1], r1[2], r1[3], r1[4], r1[5], r1[6], r1[7], r1[8]
            ohg = r4[1]
            first_max(gl, NG, gmax, r4[0], r4[2], km, ohg)
            V.tensor_tensor(r4[0], gl, over(gmax, NG), ALU.subtract).then_inc(lg_exp_in, 1)
            link(V.tensor_tensor(t32, lg[:, :, NG:36].rearrange("p t (g e) -> p t g e", g=NG),
                                 ohg.unsqueeze(3).to_broadcast([P, 3, NG, NE]), ALU.mult))
            esel, oh1, oh2, eqk, e2, t8 = r8
            link(V.tensor_reduce(esel, t32.rearrange("p t g e -> p t e g"), AX.X, ALU.add))
            first_max(esel, NE, m1, oh2, eqk, km, oh1)
            link(V.scalar_tensor_tensor(out=e2, in0=oh1, scalar=-1e30, in1=esel, op0=ALU.mult, op1=ALU.add))
            first_max(e2, NE, m2, eqk, esel, km, oh2)
            V.tensor_tensor(dm, m2, m1, ALU.subtract).then_inc(lg_exp_in, 1)
            link(V.tensor_tensor(t8, oh1, oh2, ALU.add))
            for p1, t0, t1 in ((P, 0, 2), (TS, 2, 3)):
                n = t1 - t0
                hot = ohg[0:p1, t0:t1].unsqueeze(3).to_broadcast([p1, n, NG, NE])
                V.tensor_tensor(sel[0:p1, t0:t1], hot, t8[0:p1, t0:t1].unsqueeze(2).to_broadcast([p1, n, NG, NE]),
                                ALU.mult).then_inc(sel_ready, 1)
            dve.wait_ge(lg_exp, 2)
            link(V.tensor_reduce(gsum, r4[0], AX.X, ALU.add))
            link(V.tensor_scalar(den, dm, 1.0, None, ALU.add))
            link(V.tensor_tensor(den, den, gsum, ALU.mult))
            link(V.reciprocal(w1, den))
            link(V.tensor_tensor(w2, w1, dm, ALU.mult))
            dve.wait_ge(sel_ready, 2)
            ps = take(A_POS)
            link(V.scalar_tensor_tensor(out=pos[:, :, 0:NX], in0=self_, scalar=-FAR, in1=ps[:, 0:96].rearrange("p (t x) -> p t x", t=3),
                                        op0=ALU.mult, op1=ALU.add))
            link(V.tensor_scalar(pos[:, :, 0:NX], pos[:, :, 0:NX], FAR, None, ALU.add))

            def slot_maps(e0, step):
                V.tensor_tensor(P01, pos[:, :, e0].unsqueeze(3).to_broadcast([P, 3, EPR, CAP]),
                                cidx.unsqueeze(1).unsqueeze(1).to_broadcast([P, 3, EPR, CAP]), ALU.is_equal).then_inc(p_step, 1)
                dve.wait_ge(p_step, step)
                V.tensor_tensor(Pw, P01, combx[:, :, e0].unsqueeze(3).to_broadcast([P, 3, EPR, CAP]), ALU.mult).then_inc(p_ready, 1)

            V.tensor_tensor(P01, pos[:, :, 0:EPR].unsqueeze(3).to_broadcast([P, 3, EPR, CAP]),
                            cidx.unsqueeze(1).unsqueeze(1).to_broadcast([P, 3, EPR, CAP]), ALU.is_equal).then_inc(p_step, 1)
            link(V.tensor_reduce(npf[:, 0:1], ps[:, 96:128], AX.X, ALU.max))
            link(V.tensor_scalar(thr2, thr, npf[:, 0:1], None, ALU.is_lt))
            V.tensor_reduce(npf[:, 1:2], thr2, AX.X, ALU.add).then_inc(aux_done, 1)
            dve.wait_ge(aux_done, A_POS + 1)
            V.tensor_copy(npass_i[:, :], npf[:, 1:2]).then_inc(np_ready, 1)
            link(V.tensor_tensor(eqk, oh2, over(w2, NE), ALU.mult))
            link(V.tensor_tensor(esel, oh1, over(w1, NE), ALU.mult))
            link(V.tensor_tensor(esel, esel, eqk, ALU.add))
            for p1, t0, t1 in ((P, 0, 2), (TS, 2, 3)):
                n = t1 - t0
                hot = ohg[0:p1, t0:t1].unsqueeze(3).to_broadcast([p1, n, NG, NE])
                V.tensor_tensor(comb[0:p1, t0:t1], hot, esel[0:p1, t0:t1].unsqueeze(2).to_broadcast([p1, n, NG, NE]),
                                ALU.mult).then_inc(sel_ready, 1)
            dve.wait_ge(sel_ready, 4)
            dve.wait_ge(p_step, 1)
            V.tensor_tensor(Pw, P01, combx[:, :, 0:EPR].unsqueeze(3).to_broadcast([P, 3, EPR, CAP]), ALU.mult).then_inc(p_ready, 1)
            link(V.tensor_scalar(pos[:, :, NX:NX + EPR], pos[:, :, 0:EPR], -float(CAP), None, ALU.add))
            link(V.tensor_copy(combx[:, :, NX:NX + EPR], combx[:, :, 0:EPR]))
            dve.wait_ge(np_ready, 1)
            npass = dve.value_load(npass_i[0:1, 0:1], min_val=1, max_val=9)
            with dve.Fori(0, npass) as k:
                with dve.Fori(0, ROUNDS) as r:
                    it = k * ROUNDS + r
                    for q in range(4):
                        dve.wait_ge(aux_ready, it * JPR + (A_E + q + 1))
                        V.tensor_tensor(xgT[:, 4 * q:4 * q + 4, :], bank[6 + q % 2][:, :].rearrange("p (j t) -> p j t", j=4),
                                        gffnc[:, 4 * q:4 * q + 4].unsqueeze(2).to_broadcast([P, 4, P]),
                                        ALU.mult).then_inc(aux_done, 1)
                    dve.wait_ge(aux_ready, it * JPR + (A_E + 5))
                    V.tensor_copy(PwT, bank[6][:, 0:T]).then_inc(aux_done, 1)
                    slot_maps(bass.ds(r * EPR + EPR, EPR), it + k + 2)
                    dve.wait_ge(silu_done, it + 1)
                    dve.wait_ge(e_used, it * CPR + (CREDIT + 16))
                    V.tensor_tensor(h.rearrange("s j p -> s p j"), hs.rearrange("s (p j) -> s p j", j=4),
                                    bank[1][:, :].rearrange("s (p j) -> s p j", j=4), ALU.mult).then_inc(h_ready, 1)
                    dve.wait_ge(aux_ready, it * JPR + (A_E + 6))
                    V.tensor_copy(hT.rearrange("p j s -> p (j s)"), bank[7][:, :]).then_inc(aux_done, 1)
                    dve.wait_ge(sq_done, it * 12 + 1)
                    for n in range(4):
                        for t, (_, cnt) in enumerate(TILES):
                            q = 6 + 3 * n + t
                            dve.wait_ge(aux_ready, it * JPR + (A_E + q + 1))
                            xv = x[0:cnt, t, n * 512:(n + 1) * 512]
                            V.tensor_tensor(xv, xv, bank[6 + q % 2][0:cnt, :], ALU.add).then_inc(aux_done, 1)
                V.tensor_scalar(cidx, cidx, float(CAP), None, ALU.add).then_inc(p_step, 1)
                dve.wait_ge(p_step, k * (ROUNDS + 1) + (ROUNDS + 2))
            dve.wait_ge(aux_done, npass * (JPR * ROUNDS) + A_E)
            dve.nop().then_inc(x_final, 1)
            dve.wait_ge(sq_done, npass * (12 * ROUNDS) + 1)
            link(V.tensor_reduce(ssx, ssh4, AX.X, ALU.add))
            mean_eps(ssx, D, f_var)
            dve.wait_ge(f_sqrt, 1)
            V.reciprocal(rx, rx).then_inc(f_rms, 1)
            dve.wait_ge(f_rms, 1)
            dve.wait_ge(gfin_in, 16)
            for t in range(2):
                for half in range(2):
                    cols = slice(half * 1024, (half + 1) * 1024)
                    V.scalar_tensor_tensor(out=x[:, t, cols], in0=x[:, t, cols], scalar=rx[:, t:t + 1], in1=gfin[:, cols],
                                           op0=ALU.mult, op1=ALU.mult).then_inc(y_final, 1)

        @block.tensor
        def _(pe):
            mm, tr = nc.tensor.matmul, nc.tensor.transpose

            def aux(job):
                if job >= AUX:
                    pe.wait_ge(aux_done, job - AUX + 1)
                return bank[2 + job % AUX]

            def z(n):
                if n >= 2:
                    pe.wait_ge(z_done, n - 1)
                return bank[n % 2]

            def rows_to_columns(base, src, n, wait):
                wait()
                if n == P:
                    for q in range(4):
                        ps = aux(base + q)
                        for j in range(4):
                            ins = tr(ps[:, j * P:(j + 1) * P], src(4 * q + j), ident[:, :])
                        ins.then_inc(aux_ready, 1)
                else:
                    ps = aux(base)
                    for j in range(KT):
                        ins = tr(ps[:, j * n:(j + 1) * n], src(j), ident[0:n, 0:n])
                    ins.then_inc(aux_ready, 1)

            def strided(b, n):
                v = xs[0:n, b, :].rearrange("p (c j) -> p j c", j=KT)
                return lambda j: v[:, j, :]

            pe.wait_ge(id_ok, 1)
            rows_to_columns(A_MEM, strided(0, P), P, lambda: pe.wait_ge(xs_ready, 1))
            rows_to_columns(A_MEM + 4, strided(1, P), P, lambda: pe.wait_ge(xs_ready, 2))
            pe.wait_ge(aux_done, A_MEM + 8)
            for c in range(N_MKV):
                pe.wait_ge(full[MKV_SLOT[c]], 16)
                w = slot(MKV_SLOT[c])
                for t in range(2):
                    ps = z(2 * c + t)
                    for j in range(KT):
                        ins = mm(ps[:, 0:CC], memT[:, j, t * P:(t + 1) * P], w[:, j, :], start=j == 0, stop=j == KT - 1)
                    ins.then_inc(z_ready, 1)
                if c == 0:
                    rows_to_columns(A_X, strided(0, P), P, lambda: pe.wait_ge(xs_ready, 3))
                if c == 1:
                    rows_to_columns(A_X + 4, strided(1, P), P, lambda: pe.wait_ge(xs_ready, 4))
                if c == 2:
                    rows_to_columns(A_X + 8, strided(0, TS), TS, lambda: pe.wait_ge(xs_ready, 5))

            def stay_busy(n, b=1):
                for _ in range(n):
                    mm(bank[b][:, 0:P], ident[:, :], ident[:, :], start=True, stop=True)

            def three_products(ps, b, x_hi, x_lo, k0, k1, lo, rows=None):
                for j in range(k0, k1):
                    if j % (KT // PIECES) == 0:
                        pe.wait_ge(lo[0], lo[1] + (j * PIECES // KT + 1 - PIECES))
                    if rows:
                        rows(j)
                    mm(ps[:, 0:T], w_hi[b][:, j, :], x_hi[:, j, :], start=j == k0, stop=False)
                    mm(ps[:, 0:T], w_hi[b][:, j, :], x_lo[:, j, :], start=False, stop=False)
                    ins = mm(ps[:, 0:T], w_lo[b][:, j, :], x_hi[:, j, :], start=False, stop=j == k1 - 1)
                return ins

            def project(c, between=None):
                for b in range(2):
                    n = 2 * c + b
                    three_products(z(Z_V + n), b, xn_hi, xn_lo, 0, KT, lo_after(n)).then_inc(z_ready, 1)
                    if b == 0 and between:
                        between()

            pe.wait_ge(aux_done, A_X + 9)
            for c in range(3):
                project(c)
            for hd in range(NH):
                ps = aux(A_KT + hd)
                for t in range(2):
                    ins = tr(ps[:, t * P:(t + 1) * P], kvK[:, t, hd * P:(hd + 1) * P], ident[:, :])
                ins.then_inc(aux_ready, 1)
            project(3)
            pe.wait_ge(pool_chain, 2)
            for i in range(2):
                ps, n = aux(A_WS + i), 4 - 2 * i
                for g in range(n):
                    ins = tr(ps[:, g * P:(g + 1) * P], wsN[:, 4 * i + g, :], ident[:, :])
                ins.then_inc(aux_ready, 1)
            project(4)
            for t, (t0, cnt) in enumerate(TILES):
                for i in range(2):
                    ps, n = aux(A_VN + 2 * t + i), 4 - 2 * i
                    for g in range(n):
                        ins = tr(ps[0:cnt, g * P:(g + 1) * P], vT[:, 4 * i + g, t0:t0 + cnt], ident[:, :])
                    ins.then_inc(aux_ready, 1)
            pe.wait_ge(z_done, Z_P)
            ps = aux(A_QN)
            for hd in range(NH):
                ins = tr(ps[0:TS, hd * P:(hd + 1) * P], qT[:, hd, TP:T], ident[:, :])
            ins.then_inc(aux_ready, 1)

            def sample_q(b):
                ps = aux(A_QB + b)
                mm(ps[:, :], ident[0:TS, b:b + 1].to_broadcast([TS, P]), qn[0:TS, :], start=True, stop=True).then_inc(aux_ready, 1)

            def scores(hd):
                ps = aux(A_SC[hd])
                for t in range(2):
                    ins = mm(ps[:, t * NM:(t + 1) * NM], qT[:, hd, t * P:(t + 1) * P], kT[:, hd, :], start=True, stop=True)
                ins.then_inc(aux_ready, 1)

            def head(hd):
                ps = aux(A_HEAD[hd])
                pe.wait_ge(aux_done, A_SC[hd] + 1)
                for m in range(2):
                    for t in range(2):
                        ins = tr(ps[:, m * NM + t * P:m * NM + (t + 1) * P], Pp[hd % 2][t][:, m * P:(m + 1) * P],
                                 ident[:, :])
                ins.then_inc(aux_ready, 1)
                if hd < 2:
                    stay_busy(16 - 6 * hd, 7)
                ps = aux(A_HEAD[hd] + 1)
                pe.wait_ge(aux_done, A_HEAD[hd] + 1)
                for m in range(2):
                    ins = mm(ps[:, 0:TP], kvV[:, m, hd * P:(hd + 1) * P], PpT[hd % 2][m], start=m == 0, stop=m == 1)
                ins.then_inc(aux_ready, 1)

            def sample_out(b):
                pe.wait_ge(cache_in[b % 2], 64 + 16 * (b // 2 + 1))
                for hd in range(NH):
                    for m in range(2):
                        ins = mm(bank[7][:, hd * TS + b:hd * TS + b + 1], cache[b % 2][:, m, hd * P:(hd + 1) * P],
                                 PsT[:, m, 4 * b + hd:4 * b + hd + 1], start=m == 0, stop=m == 1)
                ins.then_inc(cv_used if b < TS - 1 else sv_ready, 1)

            project(5)
            pe.wait_ge(aux_done, A_QN + 1)
            for b in range(4):
                sample_q(b)
            project(6)
            for b in range(4, TS):
                sample_q(b)
            project(7)
            pe.wait_ge(aux_done, A_KT + 4)
            scores(0)
            scores(1)
            pe.wait_ge(state_in, 16)
            for i in range(2):
                ps, n = aux(A_ST + i), 4 - 2 * i
                for g in range(n):
                    ins = tr(ps[:, g * 120:(g + 1) * 120], stN[0:120, (4 * i + g) * P:(4 * i + g + 1) * P],
                             ident[0:120, 0:120])
                ins.then_inc(aux_ready, 1)
            pe.wait_ge(ck_used, TS)
            ps = aux(A_SS)
            for m in range(2):
                ins = tr(ps[0:32, m * P:(m + 1) * P], sT[:, m, :], ident[:, :])
            ins.then_inc(aux_ready, 1)

            def sample_probs():
                ps = aux(A_SP)
                pe.wait_ge(aux_done, A_SS + 1)
                for m in range(2):
                    ins = tr(ps[:, m * 32:(m + 1) * 32], Ps[0:32, m * P:(m + 1) * P], ident[0:32, 0:32])
                ins.then_inc(aux_ready, 1)

            project(8, sample_probs)
            head(0)
            scores(2)
            head(1)
            scores(3)
            pe.wait_ge(aux_done, A_SP + 1)
            sample_out(0)
            sample_out(1)
            project(9, lambda: sample_out(2))
            sample_out(3)
            head(2)
            head(3)
            for i in range(2):
                ps, n = aux(A_PN + i), 4 - 2 * i
                for g in range(n):
                    ins = tr(ps[0:NST + TS, g * P:(g + 1) * P], pT[:, 4 * i + g, PAD + TP - NST:PAD + T], ident[:, :])
                ins.then_inc(aux_ready, 1)
            project(10, lambda: sample_out(4))
            sample_out(5)
            pe.wait_ge(ln_done, 1)
            pe.wait_ge(aux_done, A_WS + 2)
            for t in range(2):
                for i in range(2):
                    ps, n = aux(A_MX + 2 * t + i), 4 - 2 * i
                    for g in range(n):
                        ins = mm(ps[:, g * P:(g + 1) * P], vN[:, t, (4 * i + g) * P:(4 * i + g + 1) * P], wsT[:, 4 * i + g, :],
                                 start=True, stop=True)
                    ins.then_inc(aux_ready, 1)
            sample_out(6)
            ps = aux(A_MX + 4)
            pe.wait_ge(dg_ready, 1)
            for g in range(GG):
                ins = mm(ps[:, g * TS:(g + 1) * TS], vN[0:TS, 2, g * P:(g + 1) * P], dg[0:TS, g, :], start=True, stop=True)
            ins.then_inc(aux_ready, 1)
            pe.wait_ge(diff_ready, 1)
            pe.wait_ge(pool_in, 128)
            for k in range(GG):
                ps = aux(A_PL + k)
                b0 = 3 * (k // 3)
                lo = ((b0, 0, P), (b0 + 1, 0, 64))
                hi = ((b0 + 1, 64, P), (b0 + 2, 0, P))
                parts = (((0, P, lo, 0),), ((0, 64, lo, P), (64, P, hi, 0)), ((0, P, hi, 64),))[k % 3]
                for o0, o1, ins_of, c0 in parts:
                    for i, (kb, p0, p1) in enumerate(ins_of):
                        ins = mm(ps[o0:o1, 0:T], wp[p0:p1, kb, c0:c0 + o1 - o0], diff[p0:p1, kb, :], start=i == 0, stop=i == 1)
                ins.then_inc(aux_ready, 1)

            sample_out(7)
            pe.wait_ge(aux_done, A_PL + 6)
            pe.wait_ge(sv_done, 1)


            with pe.Fori(0, N_GRP) as g:
                for u in range(6):
                    pe.wait_ge(z_done, g * 6 + (Z_G + u - 1))
                    three_products(bank[u % 2], u % 2, xn_hi, xn_lo, 0, KT, lo_after(N_Z + u, g)).then_inc(z_ready, 1)
                pe.wait_ge(br_split, 2)
                for b in range(2):
                    pe.wait_ge(merged, g * 2 + (b + 1))
                    for i, (k0, k1) in enumerate(((0, 6), (6, 12), (12, 16))):
                        ins = three_products(bank[2 + 3 * b + i], b, br_hi, br_lo, k0, k1,
                                             lo_after(N_Z + 6 + b, g))
                    ins.then_inc(br_ready, 1)

            pe.wait_ge(merged, 2 * N_GRP)

            def out_rows(b):
                ps = aux(A_O[b])
                pe.wait_ge(z_done, Z_O + b + 1)
                for t, (t0, cnt) in enumerate(TILES):
                    ins = tr(ps[0:cnt, t * P:(t + 1) * P], oT[:, b % 2, t0:t0 + cnt], ident[:, :])
                ins.then_inc(aux_ready, 1)

            def new_columns(b):
                ps = aux(A_R[b])
                pe.wait_ge(aux_done, A_O[b] + 1)
                for t, (t0, cnt) in enumerate(TILES):
                    ins = tr(ps[:, t0:t0 + cnt], x[0:cnt, t, b * P:(b + 1) * P], ident[0:cnt, 0:cnt])
                ins.then_inc(aux_ready, 1)

            def logits(b):
                pe.wait_ge(aux_done, A_R[b] + 1)
                mm(bank[7][0:36, 0:T], wr[:, b, :], hgT[:, b % 2, :], start=b == 0, stop=b == KT - 1).then_inc(lg_ready, 1)

            def last_merged(j):
                if j >= KT - 2:
                    pe.wait_ge(merged, 2 * N_GRP + j + 3 - KT)

            pe.wait_ge(router_in, 16 * 7)
            for c in range(8):
                for b in range(2):
                    k = 2 * c + b
                    three_products(z(Z_O + k), b, mg_hi, mg_lo, 0, KT, lo_after(N_OUT + k),
                                   last_merged if k == 0 else None).then_inc(z_ready, 1)
                    if k >= 1:
                        out_rows(k - 1)
                    if k >= 2:
                        new_columns(k - 2)
                    if k >= 3:
                        logits(k - 3)
            out_rows(15)
            new_columns(14)
            logits(13)
            new_columns(15)
            logits(14)
            logits(15)
            ps = aux(A_LT)
            pe.wait_ge(xn2_ready, 2)
            for t, (t0, cnt) in enumerate(TILES):
                ins = tr(ps[0:cnt, t * 36:(t + 1) * 36], lgT[0:36, t0:t0 + cnt], ident[0:36, 0:36])
            ins.then_inc(aux_ready, 1)
            stay_busy(24)
            pe.wait_ge(sel_ready, 2)
            pe.wait_ge(tri_ok, 7)
            ps = aux(A_POS)
            for t in range(4):
                last = min(t, 2)
                for u in range(last + 1):
                    lhs = tri if u == t else ones
                    ins = mm(ps[:, t * NX:(t + 1) * NX], lhs, self_[:, u, :], start=u == 0, stop=u == last)
            ins.then_inc(aux_ready, 1)

            stay_busy(12)
            pe.wait_ge(xn_copied, 3)
            pe.wait_ge(np_ready, 1)
            npass = pe.value_load(npass_i[0:1, 0:1], min_val=1, max_val=9)
            with pe.Fori(0, npass) as k:
                with pe.Fori(0, ROUNDS) as r:
                    it = k * ROUNDS + r

                    def eaux(q):
                        pe.wait_ge(aux_done, it * JPR + (A_E + q - 1))
                        return bank[6 + q % 2]

                    pe.wait_ge(p_step, k * (ROUNDS + 1) + (r + 1))

                    def gather(q):
                        ps = eaux(q)
                        for jj in range(4):
                            for t, (_, cnt) in enumerate(TILES):
                                ins = mm(ps[:, jj * P:(jj + 1) * P], xn2[0:cnt, t, 4 * q + jj, :], P01f[0:cnt, t, :],
                                         start=t == 0, stop=t == 2)
                        ins.then_inc(aux_ready, 1)

                    def scatter(n):
                        for t, (t0, cnt) in enumerate(TILES):
                            ps = eaux(6 + 3 * n + t)
                            if t == 0:
                                pe.wait_ge(y_ready, it * 4 + (n + 1))
                            mm(ps[0:cnt, :], PwT[:, t0:t0 + cnt], y[:, n, :], start=True, stop=True).then_inc(aux_ready, 1)

                    gather(0)
                    for c in range(CPR):
                        s = EORDER[c % ESLOTS]
                        if c < 8 and c % 2 == 0:
                            if c < 6:
                                gather(c // 2 + 1)
                            else:
                                ps = eaux(4)
                                pe.wait_ge(p_ready, it + 1)
                                for t, (t0, cnt) in enumerate(TILES):
                                    ins = tr(ps[:, t0:t0 + cnt], Pwf[0:cnt, t, :], ident[0:cnt, 0:cnt])
                                ins.then_inc(aux_ready, 1)
                            pe.wait_ge(aux_done, it * JPR + (A_E + c // 2 + 1))
                        if c in (19, 21, 23):
                            scatter((c - 19) // 2)
                        if c == 16:
                            ps = eaux(5)
                            pe.wait_ge(h_ready, it + 1)
                            for j in range(4):
                                ins = tr(ps[:, j * P:(j + 1) * P], h[:, j, :], ident[:, :])
                            ins.then_inc(aux_ready, 1)
                            pe.wait_ge(aux_done, it * JPR + (A_E + 6))
                        pe.wait_ge(full[s], it * expert_full(CPR - ESLOTS + c % ESLOTS) + (before[s] + expert_full(c)))
                        w = e_slot[s].rearrange("p (e j n) -> p e j n", e=EPR, j=2)
                        for jj in range(2):
                            for e in range(EPR):
                                sl = slice(e * CAP, (e + 1) * CAP)
                                if c < 16:
                                    j = 2 * (c % 8) + jj
                                    ins = mm(bank[c // 8][sl, :], xgT[:, j, sl], w[:, e, jj, :], start=j == 0, stop=j == KT - 1)
                                else:
                                    n, j = (c - 16) // 2, 2 * (c % 2) + jj
                                    ins = mm(bank[2 + n][sl, :], hT[:, j, sl], w[:, e, jj, :],
                                             start=j == 0, stop=j == 3)
                        ins.then_inc(e_used, 1)
                    scatter(3)


_INS = ["x_prompt", "x_sample", "mem_prompt", "cache_mem_k", "cache_mem_v", "state_pool", "g_mix", "w_in", "ln_v_g",
        "ln_v_b", "w_s", "b_s", "w_pool", "pool_scale", "g_mem", "w_mkv", "w_br_a", "w_br_b", "w_br_c", "w_o", "g_ffn",
        "w_rg", "b_rg", "w_re", "b_re", "w_gate", "w_up", "w_down", "g_final"]
_OUTS = [(1, 256, 2048), (8, 1, 2048), (1, 1, 256, 4, 128), (1, 1, 256, 4, 128), (1, 1, 15, 768), (1, 8, 15, 768),
         (1, 8, 1, 768)]


def kernel(**inputs):
    import numpy as _np
    import concourse.bacc as _bacc
    from concourse.bass_utils import run_bass_kernel_spmd as _run

    nc = _bacc.Bacc("TRN2", target_bir_lowering=False, num_devices=1)
    arrays, ins, outs = {}, [], []
    for name in _INS:
        a = _np.ascontiguousarray(inputs[name])
        arrays[f"in_{name}"] = a
        ins.append(nc.dram_tensor(f"in_{name}", a.shape, mybir.dt.from_np(a.dtype), kind="ExternalInput").ap())
    for i, shape in enumerate(_OUTS):
        outs.append(nc.dram_tensor(f"out_{i}", shape, F32, kind="ExternalOutput").ap())
    branch_kernel(nc, ins, outs)
    r = _run(nc, [arrays], core_ids=[0])
    return tuple(r.results[0][f"out_{i}"] for i in range(len(_OUTS)))
```
